# Optimizing a Trainium2 kernel written in Bass

```python
import jax
import jax.numpy as jnp
from jax import lax
import numpy as np

D_MODEL = 1024
BATCH = 1
SEQ = 512
DEPTH = 2

HEAD_DIM = 64
GMLP_GROUPS = 8
GMLP_WIDTH = GMLP_GROUPS * HEAD_DIM
CHUNK = 128
FOX_HEADS = 8
FOX_WIDTH = FOX_HEADS * HEAD_DIM
Q_BLOCK = 128
SWA_Q_HEADS = 8
SWA_KV_HEADS = 2
SWA_GROUP = SWA_Q_HEADS // SWA_KV_HEADS
SWA_WIDTH = SWA_Q_HEADS * HEAD_DIM
KV_WIDTH = SWA_KV_HEADS * HEAD_DIM
WINDOW = 128
CONV_CH = 512
CONV_WIDTH = 31
ROPE_THETA = 500000.0
ROT_DIM = HEAD_DIM // 4
N_GROUPS = 4
EXPERTS_PER_GROUP = 8
N_EXPERTS = N_GROUPS * EXPERTS_PER_GROUP
TOP_K = 2
D_EXPERT = 256
D_PLE = 256
EPS = 1e-6
N_EVEN = (DEPTH + 1) // 2
N_ODD = DEPTH // 2
EVEN_IN = 2 * GMLP_WIDTH + 3 * FOX_WIDTH + FOX_HEADS
EVEN_SPLITS = (2 * GMLP_WIDTH, 2 * GMLP_WIDTH + FOX_WIDTH, 2 * GMLP_WIDTH + 2 * FOX_WIDTH, 2 * GMLP_WIDTH + 3 * FOX_WIDTH)
ODD_IN = SWA_WIDTH + 2 * KV_WIDTH + 2 * CONV_CH
ODD_SPLITS = (SWA_WIDTH, SWA_WIDTH + KV_WIDTH, SWA_WIDTH + 2 * KV_WIDTH)

kernel_name = 'hybrid_gmlp_fox_swa_conformer_hmoe'

def rmsnorm(x, g):
    xf = x.astype(jnp.float32)
    y = xf * lax.rsqrt(jnp.mean(xf * xf, axis=-1, keepdims=True) + EPS)
    return (y * g.astype(jnp.float32)).astype(x.dtype)

def layernorm(x, g, b):
    xf = x.astype(jnp.float32)
    mu = jnp.mean(xf, axis=-1, keepdims=True)
    var = jnp.mean(jnp.square(xf - mu), axis=-1, keepdims=True)
    y = (xf - mu) * lax.rsqrt(var + EPS) * g.astype(jnp.float32) + b.astype(jnp.float32)
    return y.astype(x.dtype)

def partial_rope(x, pos):
    half = ROT_DIM // 2
    inv_freq = ROPE_THETA ** (-jnp.arange(half, dtype=jnp.float32) * 2.0 / ROT_DIM)
    ang = pos.astype(jnp.float32)[:, None] * inv_freq[None, :]
    cos = jnp.cos(ang)[None, :, None, :]
    sin = jnp.sin(ang)[None, :, None, :]
    xr = x[..., :ROT_DIM].astype(jnp.float32)
    x1, x2 = xr[..., :half], xr[..., half:]
    rot = jnp.concatenate([x1 * cos - x2 * sin, x2 * cos + x1 * sin], axis=-1).astype(x.dtype)
    return jnp.concatenate([rot, x[..., ROT_DIM:]], axis=-1)

def chunked_gmlp(z, ln_g, ln_b, w_s, b_s):
    B, S, _ = z.shape
    z = jax.nn.gelu(z)
    u, v = z[..., :GMLP_WIDTH], z[..., GMLP_WIDTH:]
    v = layernorm(v, ln_g, ln_b)
    v = v.reshape(B, S // CHUNK, CHUNK, GMLP_GROUPS, HEAD_DIM)
    causal = jnp.tril(jnp.ones((CHUNK, CHUNK), dtype=bool))
    w = jnp.where(causal[None], w_s, jnp.zeros_like(w_s))
    mixed = jnp.einsum('gts,bcsgd->bctgd', w, v) + b_s.T[None, None, :, :, None]
    return u * mixed.reshape(B, S, GMLP_WIDTH)

def forgetting_attention(q, k, v, f_logit, q_g, k_g):
    B, S, H, Dh = q.shape
    q = rmsnorm(q, q_g)
    k = rmsnorm(k, k_g)
    c = jnp.cumsum(jax.nn.log_sigmoid(f_logit.astype(jnp.float32)), axis=1)
    c_k = c.transpose(0, 2, 1)
    n_blk = S // Q_BLOCK
    q_blocks = q.reshape(B, n_blk, Q_BLOCK, H, Dh).transpose(1, 0, 2, 3, 4)
    c_blocks = c.reshape(B, n_blk, Q_BLOCK, H).transpose(1, 0, 3, 2)
    k_pos = jnp.arange(S)
    scale = Dh ** -0.5

    def one_block(args):
        q_i, c_i, i = args
        s = jnp.einsum('bqhd,bkhd->bhqk', q_i, k, preferred_element_type=jnp.float32) * scale
        s = s + c_i[..., :, None] - c_k[:, :, None, :]
        q_pos = i * Q_BLOCK + jnp.arange(Q_BLOCK)
        s = jnp.where(q_pos[:, None] >= k_pos[None, :], s, -jnp.inf)
        prob = jax.nn.softmax(s, axis=-1)
        return jnp.einsum('bhqk,bkhd->bqhd', prob.astype(v.dtype), v)

    out = lax.map(one_block, (q_blocks, c_blocks, jnp.arange(n_blk)))
    return out.transpose(1, 0, 2, 3, 4).reshape(B, S, H * Dh)

def sliding_window_attention(q, k, v, sinks, q_g, k_g, pos):
    B, S, _, Dh = q.shape
    q = partial_rope(rmsnorm(q, q_g), pos)
    k = partial_rope(rmsnorm(k, k_g), pos)
    n_blk = S // WINDOW
    qb = q.reshape(B, n_blk, WINDOW, SWA_KV_HEADS, SWA_GROUP, Dh)

    def band(t):
        tb = t.reshape(B, n_blk, WINDOW, SWA_KV_HEADS, Dh)
        prev = jnp.pad(tb, ((0, 0), (1, 0), (0, 0), (0, 0), (0, 0)))[:, :-1]
        return jnp.concatenate([prev, tb], axis=2)

    kb, vb = band(k), band(v)
    s = jnp.einsum('bnqkgd,bnskd->bnkgqs', qb, kb, preferred_element_type=jnp.float32) * (Dh ** -0.5)
    i = jnp.arange(WINDOW)[:, None]
    j = jnp.arange(2 * WINDOW)[None, :]
    in_band = (j > i) & (j <= i + WINDOW)
    not_pad = (jnp.arange(n_blk)[:, None, None] > 0) | (j >= WINDOW)[None]
    mask = in_band[None] & not_pad
    s = jnp.where(mask[None, :, None, None], s, -jnp.inf)
    sink = sinks.astype(jnp.float32).reshape(SWA_KV_HEADS, SWA_GROUP)[None, None, :, :, None, None]
    sink = jnp.broadcast_to(sink, s.shape[:-1] + (1,))
    prob = jax.nn.softmax(jnp.concatenate([s, sink], axis=-1), axis=-1)[..., :-1]
    o = jnp.einsum('bnkgqs,bnskd->bnqkgd', prob.astype(v.dtype), vb)
    return o.reshape(B, S, SWA_WIDTH)

def conformer_conv(z, w_dw, ln_g, ln_b):
    a, gate = z[..., :CONV_CH], z[..., CONV_CH:]
    h = a * jax.nn.sigmoid(gate)
    h = lax.conv_general_dilated(h, w_dw[:, None, :].astype(h.dtype), window_strides=(1,),
                                 padding=((CONV_WIDTH - 1, 0),),
                                 dimension_numbers=('NWC', 'WIO', 'NWC'),
                                 feature_group_count=CONV_CH)
    h = layernorm(h, ln_g, ln_b)
    return jax.nn.silu(h)

def hierarchical_moe(x, w_coarse, b_coarse, w_fine, b_fine, w_gate, w_up, w_down):
    coarse = (x @ w_coarse).astype(jnp.float32) + b_coarse.astype(jnp.float32)
    p_coarse = jax.nn.softmax(coarse, axis=-1)
    g_idx = jnp.argmax(coarse, axis=-1)
    p_g = jnp.take_along_axis(p_coarse, g_idx[:, None], axis=-1)
    fine_all = jnp.einsum('td,gde->tge', x, w_fine).astype(jnp.float32) + b_fine.astype(jnp.float32)
    fine = jnp.take_along_axis(fine_all, g_idx[:, None, None], axis=1)[:, 0]
    top_v, top_i = lax.top_k(fine, TOP_K)
    p_e = jax.nn.softmax(top_v, axis=-1) * p_g
    expert_id = g_idx[:, None] * EXPERTS_PER_GROUP + top_i
    combine = jnp.einsum('tk,tke->te', p_e, jax.nn.one_hot(expert_id, N_EXPERTS, dtype=jnp.float32))
    h = jax.nn.silu(jnp.einsum('td,edf->tef', x, w_gate)) * jnp.einsum('td,edf->tef', x, w_up)
    h = h * combine.astype(h.dtype)[..., None]
    return jnp.einsum('tef,efd->td', h, w_down)

def setup_inputs(seed: int = 0) -> dict:
    key = jax.random.key(seed)
    ks = jax.random.split(key, 32)
    f32 = jnp.float32

    def nrm(k, shape, scale):
        return jax.random.normal(k, shape, f32) * scale

    def gain(k, shape):
        return 1.0 + 0.05 * jax.random.normal(k, shape, f32)

    D = D_MODEL
    return {
        'x': nrm(ks[0], (BATCH, SEQ, D), 1.0),
        'p': nrm(ks[1], (DEPTH, BATCH, SEQ, D_PLE), 1.0),
        'norm_mix': gain(ks[2], (DEPTH, D)),
        'even_w_in': nrm(ks[3], (N_EVEN, D, EVEN_IN), D ** -0.5),
        'fox_b_f': 2.0 + 0.5 * jax.random.normal(ks[4], (N_EVEN, FOX_HEADS), f32),
        'gmlp_ln_g': gain(ks[5], (N_EVEN, GMLP_WIDTH)),
        'gmlp_ln_b': nrm(ks[6], (N_EVEN, GMLP_WIDTH), 0.02),
        'gmlp_w_s': nrm(ks[7], (N_EVEN, GMLP_GROUPS, CHUNK, CHUNK), CHUNK ** -0.5),
        'gmlp_b_s': 1.0 + 0.1 * jax.random.normal(ks[8], (N_EVEN, GMLP_GROUPS, CHUNK), f32),
        'fox_q_norm': gain(ks[9], (N_EVEN, HEAD_DIM)),
        'fox_k_norm': gain(ks[10], (N_EVEN, HEAD_DIM)),
        'even_w_out': nrm(ks[11], (N_EVEN, GMLP_WIDTH + FOX_WIDTH, D), (GMLP_WIDTH + FOX_WIDTH) ** -0.5),
        'odd_w_in': nrm(ks[12], (N_ODD, D, ODD_IN), D ** -0.5),
        'swa_q_norm': gain(ks[13], (N_ODD, HEAD_DIM)),
        'swa_k_norm': gain(ks[14], (N_ODD, HEAD_DIM)),
        'swa_sinks': nrm(ks[15], (N_ODD, SWA_Q_HEADS), 0.5),
        'conv_w': nrm(ks[16], (N_ODD, CONV_WIDTH, CONV_CH), CONV_WIDTH ** -0.5),
        'conv_ln_g': gain(ks[17], (N_ODD, CONV_CH)),
        'conv_ln_b': nrm(ks[18], (N_ODD, CONV_CH), 0.02),
        'odd_w_out': nrm(ks[19], (N_ODD, SWA_WIDTH + CONV_CH, D), (SWA_WIDTH + CONV_CH) ** -0.5),
        'norm_ffn': gain(ks[20], (DEPTH, D)),
        'moe_w_coarse': nrm(ks[21], (DEPTH, D, N_GROUPS), D ** -0.5),
        'moe_b_coarse': nrm(ks[22], (DEPTH, N_GROUPS), 0.01),
        'moe_w_fine': nrm(ks[23], (DEPTH, N_GROUPS, D, EXPERTS_PER_GROUP), D ** -0.5),
        'moe_b_fine': nrm(ks[24], (DEPTH, N_GROUPS, EXPERTS_PER_GROUP), 0.01),
        'moe_w_gate': nrm(ks[25], (DEPTH, N_EXPERTS, D, D_EXPERT), D ** -0.5),
        'moe_w_up': nrm(ks[26], (DEPTH, N_EXPERTS, D, D_EXPERT), D ** -0.5),
        'moe_w_down': nrm(ks[27], (DEPTH, N_EXPERTS, D_EXPERT, D), D_EXPERT ** -0.5),
        'ple_w_proj': nrm(ks[28], (DEPTH, D_PLE, D), D_PLE ** -0.5),
        'ple_norm': gain(ks[29], (DEPTH, D)),
        'ple_w_gate': nrm(ks[30], (DEPTH, D, D), D ** -0.5),
    }

def reference(x, p, norm_mix, even_w_in, fox_b_f, gmlp_ln_g, gmlp_ln_b, gmlp_w_s, gmlp_b_s,
              fox_q_norm, fox_k_norm, even_w_out, odd_w_in, swa_q_norm, swa_k_norm, swa_sinks,
              conv_w, conv_ln_g, conv_ln_b, odd_w_out, norm_ffn, moe_w_coarse, moe_b_coarse,
              moe_w_fine, moe_b_fine, moe_w_gate, moe_w_up, moe_w_down, ple_w_proj, ple_norm,
              ple_w_gate):
    B, S, D = x.shape
    pos = jnp.arange(S)
    h = x
    for i in range(DEPTH):
        a = rmsnorm(h, norm_mix[i])
        j = i // 2
        if i % 2 == 0:
            z = a @ even_w_in[j]
            z_a, q, k, v, f = jnp.split(z, EVEN_SPLITS, axis=-1)
            y_a = chunked_gmlp(z_a, gmlp_ln_g[j], gmlp_ln_b[j], gmlp_w_s[j], gmlp_b_s[j])
            y_b = forgetting_attention(q.reshape(B, S, FOX_HEADS, HEAD_DIM),
                                       k.reshape(B, S, FOX_HEADS, HEAD_DIM),
                                       v.reshape(B, S, FOX_HEADS, HEAD_DIM),
                                       f + fox_b_f[j], fox_q_norm[j], fox_k_norm[j])
            mix = jnp.concatenate([y_a, y_b], axis=-1) @ even_w_out[j]
        else:
            z = a @ odd_w_in[j]
            q, k, v, z_d = jnp.split(z, ODD_SPLITS, axis=-1)
            y_c = sliding_window_attention(q.reshape(B, S, SWA_Q_HEADS, HEAD_DIM),
                                           k.reshape(B, S, SWA_KV_HEADS, HEAD_DIM),
                                           v.reshape(B, S, SWA_KV_HEADS, HEAD_DIM),
                                           swa_sinks[j], swa_q_norm[j], swa_k_norm[j], pos)
            y_d = conformer_conv(z_d, conv_w[j], conv_ln_g[j], conv_ln_b[j])
            mix = jnp.concatenate([y_c, y_d], axis=-1) @ odd_w_out[j]
        h = h + mix
        m = rmsnorm(h, norm_ffn[i]).reshape(B * S, D)
        h = h + hierarchical_moe(m, moe_w_coarse[i], moe_b_coarse[i], moe_w_fine[i], moe_b_fine[i],
                                 moe_w_gate[i], moe_w_up[i], moe_w_down[i]).reshape(B, S, D)
        gate = jax.nn.sigmoid(rmsnorm(h, ple_norm[i]) @ ple_w_gate[i])
        h = h + gate * (p[i] @ ple_w_proj[i])
    return h


_drawn_inputs = setup_inputs


def setup_inputs(seed=0):
    import zlib

    import numpy as np

    out = dict(_drawn_inputs(seed))
    spreads = {}
    factors = {'swa_q_norm': 5.65,
     'swa_k_norm': 3.825,
     'swa_sinks': 64.0,
     'conv_ln_b': 5.037,
     'moe_b_coarse': 3.013,
     'moe_b_fine': 3.912,
     'ple_norm': 3.308}
    for name, (base, spread) in spreads.items():
        noise = np.random.default_rng([zlib.crc32(name.encode()), seed]).standard_normal(out[name].shape)
        drawn = base * np.exp(spread * noise) if base else spread * noise
        out[name] = jnp.asarray(drawn.astype(out[name].dtype))
    for name, factor in factors.items():
        out[name] = (out[name] * factor).astype(out[name].dtype)
    return out
```

```python
from contextlib import ExitStack

import numpy as np
import concourse.bass as bass
from concourse import mybir

F32 = mybir.dt.float32
BF16 = mybir.dt.bfloat16
I32 = mybir.dt.int32
U32 = mybir.dt.uint32
ALU = mybir.AluOpType
ACT = mybir.ActivationFunctionType
AX = mybir.AxisListType

P = 128
SEQ, D, DEPTH = 512, 1024, 2
NT, KC = SEQ // P, D // P
HALF = 512
HEADS, DH = 8, 64
GMLP = 8
GROUPS, PER_GROUP, EXPERTS, FE = 4, 8, 32, 256
CAP = 64
ROUNDS = SEQ // CAP
PAIRS = EXPERTS // 2
TAPS = 31
PLE = 256
EPS = 1e-6
NEG = -1e30
SLOTS, SLOT = 12, 2048
ROT = 16
KB = 256


class Chain:

    def __init__(self, eng, sem):
        self.eng, self.sem, self.count = eng, sem, 0

    def step(self, ins):
        ins.then_inc(self.sem, 1)
        self.count += 1

    def link(self, ins):
        self.step(ins)
        self.wait()

    def wait(self, behind=0):
        if self.count > behind:
            self.eng.wait_ge(self.sem, self.count - behind)


def build(nc, a, out, stages=3 * DEPTH):
    with ExitStack() as ctx:
        def sb(name, shape, dt=F32):
            return ctx.enter_context(nc.sbuf_tensor(name, shape, dt))

        def sem(name):
            return ctx.enter_context(nc.semaphore(name))

        PS = ctx.enter_context(nc.psum_tensor("psum_banks", [P, 8, HALF], F32))
        ring = sb("ring", [P, SLOTS, SLOT])
        h = sb("h_res", [P, NT, D])
        aT = sb("aT", [P, KC, SEQ])
        work = sb("work", [P, 60 * KB])

        def area(kb0, kb1, **dims):
            return work[:, int(kb0 * KB):int(kb1 * KB)]

        xn = area(0, 16).rearrange("p (t d) -> p t d", t=NT)
        junk = area(16, 20)
        zq = area(0, 8).rearrange("p (t d) -> p t d", t=NT)
        zk = area(8, 16).rearrange("p (t d) -> p t d", t=NT)
        ws_raw = area(16, 20).rearrange("p (g s) -> p g s", g=HEADS)
        qT = area(20, 28).rearrange("p (j s) -> p j s", j=4)
        kT = area(28, 36).rearrange("p (j s) -> p j s", j=4)
        zv = area(36, 44).rearrange("p (t d) -> p t d", t=NT)
        zu = area(44, 52).rearrange("p (t d) -> p t d", t=NT)
        zg = area(52, 60).rearrange("p (t d) -> p t d", t=NT)
        yb = zq
        yT = area(20, 36).rearrange("p (c s) -> p c s", c=KC)
        aflat = aT[:, :, :].rearrange("p c s -> p (c s)")
        wsT = aflat[:, 0:1024].rearrange("p (g s) -> p g s", g=HEADS)
        ebuf = aflat[:, 1024:2048].rearrange("p (b s) -> p b s", b=2)
        ptbuf = aflat[:, 2048:3072].rearrange("p (b s) -> p b s", b=2)
        cin = area(36, 45).rearrange("p (j s) -> p j s", j=4)
        cacc = area(45, 53).rearrange("p (j s) -> p j s", j=4)
        cacc2 = area(53, 55)
        sgc = area(55, 59).rearrange("p (b s) -> p b s", b=2)
        kv = area(8, 12).rearrange("p (t d) -> p t d", t=NT)
        qT1 = area(0, 8).rearrange("p (j s) -> p j s", j=4)
        sq1 = area(12, 20)
        qp = area(12, 20).rearrange("p (t d) -> p t d", t=NT)
        y1 = qp
        kT1 = aflat[:, 3072:3584]
        junk_r = aflat[:, 3584:3840]
        cd = cin[:, :, 0:SEQ]
        xT = area(20, 28).rearrange("p (b c s) -> p b c s", b=2, c=KC)
        sel = area(28, 32).rearrange("p (b t s) -> p b t s", b=2, t=NT)
        sgate = area(32, 34).rearrange("p (b s) -> p b s", b=2)
        hid_area = area(34, 36)
        hid = area(34, 36).rearrange("p (b s) -> p b s", b=2)
        hidT = area(36, 38).rearrange("p (b f s) -> p b f s", b=2, f=2)
        ysb = area(38, 46).rearrange("p (b d) -> p b d", b=2)
        rtmp = area(46, 52)
        cold_down = (area(24, 28), area(42, 46))
        cold_up = aflat[:, 2048:4096]
        cold_gate = aflat[:, 0:2048]
        gath = area(0, 16).rearrange("p (b d) -> p b d", b=NT)
        psb = area(52, 56).rearrange("p (t d) -> p t d", t=NT)
        pT = area(56, 60).rearrange("p (k s) -> p k s", k=2)
        sgp = area(46, 50).rearrange("p (b s) -> p b s", b=2)

        ident = sb("ident", [P, P])
        ones = sb("ones", [P, P])
        mean_w = sb("mean_w", [P, P])
        upper = sb("upper", [P, P])
        ident_b = sb("ident_b", [P, P], BF16)
        mask = sb("mask", [P, 2 * P], BF16)
        pick = sb("pick", [96, HEADS, P], BF16)
        decay = sb("decay", [96, SEQ], BF16)
        iota = sb("iota", [P, CAP])
        steps64 = sb("steps64", [P, ROUNDS - 1])
        eps = sb("eps", [P, 1])
        rows = sb("rows", [P, P])
        cols = sb("cols", [P, P])
        lng = sb("lng", [P, HALF])
        lnb = sb("lnb", [P, HALF])
        wf = sb("wf", [P, KC, HEADS])
        wr = sb("wr", [P, DEPTH, KC, 36])
        rbias = sb("rbias", [P, DEPTH, 36])
        bf8 = sb("bf8", [HEADS, 1])
        rope = sb("rope_sb", [P, 2, NT, ROT // 2])
        gq1 = sb("gq1", [P, 2, DH])
        sinks = sb("sinks", [P, HEADS])
        tapw = sb("tapw", [P, NT, TAPS])
        tap_rows = work[0:TAPS, int(36 * KB):int(38 * KB)]
        ss = sb("ss", [P, 6 * NT])
        root = sb("root", [P, 6 * NT])
        rstd = sb("rstd", [P, 6 * NT])
        qk_ss = sb("qk_ss", [P, 2, 32])
        stat6 = sb("stat6", [P, NT, 6])
        stat2 = sb("stat2", [P, NT, 2])
        lnr = sb("lnr", [P, NT])
        gq8 = sb("gq8", [P, 1])
        nmax = sb("nmax", [P, 32])
        rsum = sb("rsum", [P, 32])
        esink = sb("esink", [P, 32])
        rinv = sb("rinv", [P, 32])
        rsel = sb("rsel", [P, NT, EXPERTS])
        prob = sb("prob", [P, NT, 2])
        posn = sb("posn", [P, NT, 2], I32)
        most = sb("most", [P, 1], I32)
        table = nc.dram_tensor("expert_rows", [ROUNDS * EXPERTS * CAP, D], F32).ap()

        const_ready = sem("const_ready")
        small_loaded = sem("small_loaded")
        x_loaded = [sem(f"x_loaded{t}") for t in range(NT)]
        slot_loaded = [sem(f"slot_loaded{s}") for s in range(SLOTS)]
        cols_done = sem("cols_done")
        cols_ready = sem("cols_ready")
        h_ready = sem("h_ready")
        out_half = sem("out_half")
        act_chain, dve_chain, pool_chain = sem("act_chain"), sem("dve_chain"), sem("pool_chain")
        root_ready = sem("root_ready")
        xn_ready = sem("xn_ready")
        turned = sem("turned")
        aT_act, aT_dve = sem("aT_act"), sem("aT_dve")
        out_stored = sem("out_stored")
        proj_done = sem("proj_done")
        z_done, z_copied = sem("z_done"), sem("z_copied")

        def kblocks(w, c0, c1, n0, n1):
            return w.rearrange("(c p) n -> p c n", p=P)[:, c0:c1, n0:n1]

        def dense_blocks(w, col_list):
            for n0 in col_list:
                for k0 in (0, KC // 2):
                    yield kblocks(w, k0, k0 + KC // 2, n0, n0 + HALF), KC // 2

        even_w, odd_w = a["even_w_in"][0], a["odd_w_in"][0]
        EVEN_COLS = (1536, 1024, 2048, 512, 0)
        ODD_A, ODD_GATE, ODD_Q, ODD_KV = 768, 1280, 0, 512
        items, first = [], {}

        def add(name, its):
            first[name] = len(items)
            items.extend(its)

        def add_tail(l):
            first[f"moe{l}"] = len(items)
            for e in range(EXPERTS):
                items.extend([
                    (a["moe_w_gate"][l, e].rearrange("(c p) f -> p c f", p=P), KC),
                    (a["moe_w_up"][l, e].rearrange("(c p) f -> p c f", p=P), KC),
                    (a["moe_w_down"][l, e].rearrange("(c p) n -> p c n", p=P), 2)])
            add(f"pgate{l}", dense_blocks(a["ple_w_gate"][l], (0, HALF)))
            add(f"pproj{l}", [(a["ple_w_proj"][l].rearrange("(c p) n -> p c n", p=P), 2)])

        add("even_in", dense_blocks(even_w, EVEN_COLS))
        add("out0", dense_blocks(a["even_w_out"][0], (0, HALF)))
        add_tail(0)
        add("odd_conv", dense_blocks(odd_w, (ODD_A, ODD_GATE)))
        add("odd_q", dense_blocks(odd_w, (ODD_Q,)))
        add("odd_kv", [(kblocks(odd_w, 0, KC, ODD_KV, ODD_KV + 256), KC)])
        add("out1", dense_blocks(a["odd_w_out"][0], (0, HALF)))
        add_tail(1)

        def slot(n, c):
            return ring[:, n % SLOTS, :].rearrange("p (c n) -> p c n", c=c)

        def landed(pe, n):
            pe.wait_ge(slot_loaded[n % SLOTS], 16 * (n // SLOTS + 1))

        MIX, FFN, PNORM, BS, CLG, CLB, FQ, FK = 0, 16, 32, 48, 56, 60, 64, 65
        NROWS = 66

        def gain_col(u, c):
            l, kind = u // 3, u % 3
            return cols[:, (MIX, FFN, PNORM)[kind] + KC * l + c:][:, 0:1]

        block = ctx.enter_context(nc.Block())

        UNITS = [(hd, i) for hd in range(HEADS) for i in range(NT)]

        class Attention:

            def __init__(self, layer):
                n = f"att{layer}_"
                self.layer = layer
                self.scored = sem(n + "scored")
                self.maxed = sem(n + "maxed")
                self.exped = sem(n + "exped")
                self.turned = sem(n + "turned")
                self.copied = sem(n + "copied")
                self.summed = sem(n + "summed")
                self.written = sem(n + "written")

            def blocks(self, i):
                return range(i + 1) if self.layer == 0 else range(max(i - 1, 0), i + 1)

            def scores(self, pe, u):
                hd, i = UNITS[u]
                ks = self.blocks(i)
                n = P * len(ks)
                S = PS[:, u % 3, 0:n]
                if self.layer == 0:
                    b, j, q, k = DH * (hd % 2), hd // 2, qT, kT[:, hd // 2, :]
                else:
                    b, j, q, k = DH * (hd // 4), hd % 4, qT1, kT1
                if u >= 3:
                    pe.wait_ge(self.exped, u - 2)
                pe.matmul(S, q[b:b + DH, j, P * i:P * (i + 1)], k[b:b + DH, P * ks[0]:P * (i + 1)],
                          start=True, stop=False)
                if self.layer == 0:
                    pe.matmul(S, pick[:, hd, :], decay[:, 0:n], start=False, stop=False)
                    m = mask[:, P:2 * P]
                    S = PS[:, u % 3, n - P:n]
                else:
                    m = mask[:, 2 * P - n:2 * P]
                pe.matmul(S, ident_b[:, :], m, start=False, stop=True).then_inc(self.scored, 1)

            def turn(self, pe, u):
                hd, i = UNITS[u]
                pe.wait_ge(self.exped, u + 1)
                if u >= 2:
                    pe.wait_ge(self.copied, u - 1)
                for x in range(len(self.blocks(i))):
                    last = pe.transpose(PS[:, 3 + u % 2, P * x:P * (x + 1)],
                                        ebuf[:, u % 2, P * x:P * (x + 1)], ident[:, :])
                last.then_inc(self.turned, 1)

            def values(self, pe, u):
                hd, i = UNITS[u]
                ks = self.blocks(i)
                pe.wait_ge(self.copied, u + 1)
                if u >= 2:
                    pe.wait_ge(self.written, u - 1)
                for x, kb in enumerate(ks):
                    v = zv[:, kb, DH * hd:DH * (hd + 1)] if self.layer == 0 else \
                        kv[:, kb, P + DH * (hd // 4):P + DH * (hd // 4 + 1)]
                    last = pe.matmul(PS[:, 5 + u % 2, 0:DH], ptbuf[:, u % 2, P * x:P * (x + 1)], v,
                                     start=(x == 0), stop=(x == len(ks) - 1))
                last.then_inc(self.summed, 1)

            def pe(self, pe):
                n = len(UNITS)
                self.scores(pe, 0)
                self.scores(pe, 1)
                for u in range(n + 1):
                    if u + 2 < n:
                        self.scores(pe, u + 2)
                    if u < n:
                        self.turn(pe, u)
                    if u >= 1:
                        self.values(pe, u - 1)

            def act(self, act):
                for u, (hd, i) in enumerate(UNITS):
                    n = P * len(self.blocks(i))
                    act.wait_ge(self.maxed, u + 1)
                    if u >= 2:
                        act.wait_ge(self.turned, u - 1)
                    if self.layer == 1:
                        nc.scalar.activation(esink[:, u:u + 1], sinks[:, hd:hd + 1], ACT.Exp,
                                             bias=nmax[:, u:u + 1])
                    nc.scalar.activation(ebuf[:, u % 2, 0:n], PS[:, u % 3, 0:n], ACT.Exp,
                                         bias=nmax[:, u:u + 1],
                                         accum_out=rsum[:, u:u + 1]).then_inc(self.exped, 1)

            def dve(self, dve, chain, y):
                n = len(UNITS)

                def maxima(u):
                    hd, i = UNITS[u]
                    S = PS[:, u % 3, 0:P * len(self.blocks(i))]
                    dve.wait_ge(self.scored, u + 1)
                    if self.layer == 0:
                        nc.vector.tensor_reduce(nmax[:, u:u + 1], S, AX.X, ALU.max,
                                                negate=True).then_inc(self.maxed, 1)
                    else:
                        chain.link(nc.vector.tensor_reduce(rinv[:, u:u + 1], S, AX.X, ALU.max))
                        nc.vector.tensor_scalar(nmax[:, u:u + 1], rinv[:, u:u + 1],
                                                sinks[:, hd:hd + 1], -1.0, ALU.max,
                                                ALU.mult).then_inc(self.maxed, 1)

                maxima(0)
                for u in range(n + 1):
                    if u + 1 < n:
                        maxima(u + 1)
                    if u < n:
                        w = P * len(self.blocks(UNITS[u][1]))
                        dve.wait_ge(self.turned, u + 1)
                        if u >= 2:
                            dve.wait_ge(self.summed, u - 1)
                        nc.vector.tensor_copy(ptbuf[:, u % 2, 0:w],
                                              PS[:, 3 + u % 2, 0:w]).then_inc(self.copied, 1)
                    if u >= 1:
                        v = u - 1
                        hd, i = UNITS[v]
                        if self.layer == 1:
                            chain.link(nc.vector.tensor_tensor(rsum[:, v:v + 1], rsum[:, v:v + 1],
                                                               esink[:, v:v + 1], ALU.add))
                        chain.link(nc.vector.reciprocal(rinv[:, v:v + 1], rsum[:, v:v + 1]))
                        dve.wait_ge(self.summed, v + 1)
                        nc.vector.tensor_scalar(y[:, i, DH * hd:DH * (hd + 1)],
                                                PS[:, 5 + v % 2, 0:DH], rinv[:, v:v + 1], None,
                                                ALU.mult).then_inc(self.written, 1)

        att = [Attention(0), Attention(1)]

        def wait_h(eng, u, t):
            if u == 0:
                eng.wait_ge(x_loaded[t], 16)
            else:
                eng.wait_ge(h_ready, NT * (u - 1) + t + 1)

        def norm_act(act, chain, u):
            for t in range(NT):
                k = NT * u + t
                wait_h(act, u, t)
                chain.link(nc.scalar.activation(junk[:, 0:D], h[:, t, :], ACT.Square,
                                                accum_out=ss[:, k:k + 1]))
                nc.scalar.activation(root[:, k:k + 1], ss[:, k:k + 1], ACT.Sqrt, bias=eps[:, :],
                                     scale=1.0 / D).then_inc(root_ready, 1)
            for c in range(1, KC, 2):
                act.wait_ge(turned, KC * u + turn_order.index(c) + 1)
                nc.scalar.activation(aT[:, c, :], PS[:, turn_bank(c), :], ACT.Copy,
                                     scale=gain_col(u, c)).then_inc(aT_act, 1)

        turn_order = [0, 1, 2, 3, 4, 5, 6, 7]

        def turn_bank(c):
            return (c + 4) % 8

        def norm_dve(dve, chain, u):
            for t in range(NT):
                k = NT * u + t
                dve.wait_ge(root_ready, k + 1)
                chain.link(nc.vector.reciprocal(rstd[:, k:k + 1], root[:, k:k + 1]))
                wait_h(dve, u, t)
                nc.vector.tensor_scalar(xn[:, t, :], h[:, t, :], rstd[:, k:k + 1], None,
                                        ALU.mult).then_inc(xn_ready, 1)
            for c in range(0, KC, 2):
                dve.wait_ge(turned, KC * u + c + 1)
                nc.vector.tensor_scalar(aT[:, c, :], PS[:, turn_bank(c), :], gain_col(u, c), None,
                                        ALU.mult).then_inc(aT_dve, 1)

        def norm_pe(pe, u):
            if u % 3 == 0:
                pe.wait_ge(xn_ready, NT * (u + 1))
            for t in range(NT):
                pe.wait_ge(xn_ready, NT * u + t + 1)
                for c in range(4):
                    ins = pe.transpose(PS[:, turn_bank(c), P * t:P * (t + 1)],
                                       xn[:, t, P * c:P * (c + 1)], ident[:, :])
                    if t == NT - 1:
                        ins.then_inc(turned, 1)
            if u == 0:
                pe.wait_ge(cols_ready, 1)
            for c in range(4, KC):
                for t in range(NT):
                    ins = pe.transpose(PS[:, turn_bank(c), P * t:P * (t + 1)],
                                       xn[:, t, P * c:P * (c + 1)], ident[:, :])
                ins.then_inc(turned, 1)

        def wait_aT(pe, u):
            pe.wait_ge(aT_act, KC // 2 * (u + 1))
            pe.wait_ge(aT_dve, KC // 2 * (u + 1))

        y_turned = sem("y_turned")
        yT_act, yT_dve = sem("yT_act"), sem("yT_dve")

        def out_pe(pe, l):
            n0 = first[f"out{l}"]
            pe.wait_ge(yT_act, Y_ACT[l])
            pe.wait_ge(yT_dve, Y_DVE[l])
            for x in range(4):
                landed(pe, n0 + x)
            for t in range(NT):
                if t >= 2:
                    pe.wait_ge(h_ready, 3 * NT * l + t - 1)
                for n in range(2):
                    for c in range(KC):
                        last = pe.matmul(PS[:, (2 * t + n) % 4, :], yT[:, c, P * t:P * (t + 1)],
                                         slot(n0 + 2 * n + c // 4, 4)[:, c % 4, :],
                                         start=(c == 0), stop=(c == KC - 1))
                    last.then_inc(proj_done, 1)

        def out_dve(dve, l):
            for t in range(NT):
                for n in range(2):
                    dve.wait_ge(proj_done, 8 * l + 2 * t + n + 1)
                    part = h[:, t, HALF * n:HALF * (n + 1)]
                    nc.vector.tensor_tensor(part, part, PS[:, (2 * t + n) % 4, :],
                                            ALU.add).then_inc(h_ready if n else out_half, 1)

        Y_ACT, Y_DVE = (4, 4 + 6), (4, 4 + 2)

        f_done, f_root = sem("f_done"), sem("f_root")
        f_abs, f_log = sem("f_abs"), sem("f_log")
        taps_done, taps_copied = sem("taps_done"), sem("taps_copied")
        decay_ready = sem("decay_ready")
        qk_squared = sem("qk_squared")
        qk_summed = sem("qk_summed")
        qk_root = sem("qk_root")
        qk_normed = sem("qk_normed")
        qk_turned = sem("qk_turned")
        qk_copied = sem("qk_copied")
        ws_loaded = sem("ws_loaded")
        ws_turned, ws_copied, ws_masked = sem("ws_turned"), sem("ws_copied"), sem("ws_masked")
        g_stats, g_root, g_scaled, g_normed = sem("g_stats"), sem("g_root"), sem("g_scaled"), sem("g_normed")
        g_mixed, ya_done = sem("g_mixed"), sem("ya_done")

        def even_pe(pe):
            wait_aT(pe, 0)
            pe.wait_ge(small_loaded, 16 * N_SMALL)
            for j in range(NT):
                last = pe.transpose(PS[:, 5, 32 * j:32 * j + TAPS], tap_rows[:, P * j:P * (j + 1)],
                                    ident[0:TAPS, 0:TAPS])
            last.then_inc(taps_done, 1)
            for c in range(KC):
                last = pe.matmul(PS[0:HEADS, 4, :], wf[:, c, :], aT[:, c, :], start=(c == 0),
                                 stop=(c == KC - 1))
            last.then_inc(f_done, 1)
            n0 = first["even_in"]
            for b in range(5):
                for x in range(2):
                    landed(pe, n0 + 2 * b + x)
                for t in range(NT):
                    m = NT * b + t
                    if m >= 4:
                        pe.wait_ge(z_copied, m - 3)
                    for c in range(KC):
                        last = pe.matmul(PS[:, m % 4, :], aT[:, c, P * t:P * (t + 1)],
                                         slot(n0 + 2 * b + c // 4, 4)[:, c % 4, :],
                                         start=(c == 0), stop=(c == KC - 1))
                    last.then_inc(z_done, 1)
                if b == 3:
                    for x, z in enumerate((zk, zq)):
                        pe.wait_ge(qk_normed, x + 1)
                        for j in range(4):
                            if x:
                                pe.wait_ge(qk_copied, j + 1)
                            else:
                                pe.wait_ge(f_abs, 1)
                                pe.wait_ge(taps_copied, 1)
                            for t in range(NT):
                                last = pe.transpose(PS[:, 4 + j, P * t:P * (t + 1)],
                                                    z[:, t, P * j:P * (j + 1)], ident[:, :])
                            last.then_inc(qk_turned, 1)
            pe.wait_ge(ws_loaded, 16)
            pe.wait_ge(qk_copied, 8)
            for g in range(HEADS):
                last = pe.transpose(PS[:, 6 + g // 4, P * (g % 4):P * (g % 4 + 1)], ws_raw[:, g, :],
                                    ident[:, :])
            last.then_inc(ws_turned, 1)
            pe.wait_ge(z_copied, 5 * NT)
            pe.wait_ge(decay_ready, 1)
            pe.wait_ge(ws_copied, 1)
            att[0].pe(pe)
            pe.wait_ge(ws_masked, 1)
            pe.wait_ge(g_normed, 1)
            pe.wait_ge(att[0].written, len(UNITS))
            for g in range(GMLP):
                pe.matmul(PS[:, g // 2, 256 * (g % 2):256 * (g % 2 + 1)].rearrange(
                    "p (c d) -> p c d", c=NT), wsT[:, g, :],
                    zg[:, :, DH * g:DH * (g + 1)], start=True, stop=True).then_inc(g_mixed, 1)
            for n, c in enumerate((4, 5, 6, 7, 0, 1, 2, 3)):
                if c < 4:
                    pe.wait_ge(ya_done, GMLP)
                y = yb if c >= 4 else zu
                for t in range(NT):
                    last = pe.transpose(PS[:, c, P * t:P * (t + 1)],
                                        y[:, t, P * (c % 4):P * (c % 4 + 1)], ident[:, :])
                last.then_inc(y_turned, 1)
            out_pe(pe, 0)

        def even_act(act, chain):
            act.wait_ge(taps_done, 1)
            nc.scalar.activation(tapw[:, :, :], PS[:, 5, 0:NT * 32].rearrange("p (j k) -> p j k", j=NT)[:, :, 0:TAPS],
                                 ACT.Copy).then_inc(taps_copied, 1)
            act.dma_start(ws_raw[:, :, :], a["gmlp_w_s"][0].rearrange("g t s -> t g s")).then_inc(ws_loaded, 16)

            def copy(b, dst, func=ACT.Copy):
                for t in range(NT):
                    act.wait_ge(z_done, NT * b + t + 1)
                    nc.scalar.activation(dst[:, t, :], PS[:, (NT * b + t) % 4, :],
                                         func).then_inc(z_copied, 1)

            copy(0, zk)
            act.wait_ge(f_abs, 1)
            chain.link(nc.scalar.activation(junk8[:, 1, :], junk8[:, 1, :], ACT.Exp, scale=-1.0))
            nc.scalar.activation(junk8[:, 1, :], junk8[:, 1, :], ACT.Ln, bias=ones[0:HEADS, 0:1]).then_inc(f_log, 1)
            copy(1, zq)
            copy(2, zv)
            act.wait_ge(qk_summed, 2)
            nc.scalar.activation(qk_ss[:, :, :], qk_ss[:, :, :], ACT.Sqrt, bias=eps[:, :],
                                 scale=1.0 / DH).then_inc(qk_root, 1)
            copy(3, zg, ACT.Gelu_apprx_tanh)
            copy(4, zu, ACT.Gelu_apprx_tanh)
            act.wait_ge(g_stats, 1)
            nc.scalar.activation(lnr[:, :], stat2[:, :, 1], ACT.Sqrt, bias=eps[:, :]).then_inc(g_root, 1)
            act.wait_ge(ws_turned, 1)
            chain.step(nc.scalar.activation(wsT[:, 0:4, :], PS[:, 6, :].rearrange("p (g s) -> p g s", g=4), ACT.Copy))
            nc.scalar.activation(wsT[:, 4:8, :], PS[:, 7, :].rearrange("p (g s) -> p g s", g=4), ACT.Copy).then_inc(ws_copied, 1)
            att[0].act(act)
            y_act(act, 0, (5, 7, 1, 3))

        Y_ORDER = ((4, 5, 6, 7, 0, 1, 2, 3), (0, 1, 2, 3))

        def y_act(act, l, cs):
            for c in cs:
                act.wait_ge(y_turned, 8 * l + Y_ORDER[l].index(c) + 1)
                nc.scalar.activation(yT[:, c, :], PS[:, c, :], ACT.Copy).then_inc(yT_act, 1)

        def y_dve(dve, l, cs):
            for c in cs:
                dve.wait_ge(y_turned, 8 * l + Y_ORDER[l].index(c) + 1)
                nc.vector.tensor_copy(yT[:, c, :], PS[:, c, :]).then_inc(yT_dve, 1)

        junk8 = area(20, 26)[0:HEADS, :].rearrange("p (b s) -> p b s", b=3)
        k_sq, q_sq = area(52, 60), area(44, 52)

        def even_dve(dve, chain):
            dve.wait_ge(f_done, 1)
            x, e, c_ = junk8[:, 0, :], junk8[:, 1, :], junk8[:, 2, :]
            chain.link(nc.vector.tensor_scalar(x, PS[0:HEADS, 4, :], bf8[:, :], None, ALU.add))
            chain.link(nc.vector.tensor_scalar(e, x, -1.0, None, ALU.mult))
            nc.vector.tensor_tensor(e, x, e, ALU.max).then_inc(f_abs, 1)
            chain.link(nc.vector.tensor_scalar(x, x, 0.0, None, ALU.min))
            dve.wait_ge(f_log, 1)
            chain.link(nc.vector.tensor_tensor(x, e, x, ALU.subtract))
            chain.link(nc.vector.memset(e, 1.0))
            chain.link(nc.vector.tensor_tensor_scan(c_, e, x, 0.0, ALU.mult, ALU.add))
            for part in range(3):
                r = decay[32 * part:32 * part + HEADS, :]
                if part < 2:
                    chain.link(nc.vector.tensor_copy(r, c_))
                    chain.link(nc.vector.tensor_copy(x, r))
                    chain.link(nc.vector.tensor_tensor(c_, c_, x, ALU.subtract))
                else:
                    nc.vector.tensor_copy(r, c_).then_inc(decay_ready, 1)
            for x_, s in enumerate((k_sq, q_sq)):
                dve.wait_ge(qk_squared, x_ + 1)
                nc.vector.tensor_reduce(qk_ss[:, x_, :], s.rearrange("p (g d) -> p g d", d=DH),
                                        AX.X, ALU.add).then_inc(qk_summed, 1)
            dve.wait_ge(qk_root, 1)
            chain.link(nc.vector.reciprocal(qk_ss[:, :, :], qk_ss[:, :, :]))
            for x_, z in enumerate((zk, zq)):
                v = z[:, :, :].rearrange("p t (g d) -> p (t g) d", d=DH)
                nc.vector.tensor_tensor(v, v, qk_ss[:, x_, :].unsqueeze(2).to_broadcast([P, 32, DH]),
                                        ALU.mult).then_inc(qk_normed, 1)
            for x_, (dst, gcol) in enumerate(((kT, cols[:, FK:FK + 1]), (qT, gq8[:, :]))):
                for j in range(4):
                    dve.wait_ge(qk_turned, 4 * x_ + j + 1)
                    nc.vector.tensor_scalar(dst[:, j, :], PS[:, 4 + j, :], gcol, None,
                                            ALU.mult).then_inc(qk_copied, 1)
            for t in range(NT):
                dve.wait_ge(z_copied, 3 * NT + t + 1)
                chain.link(nc.vector.bn_stats(stat6[:, t, :], zg[:, t, :]))
                ins = nc.vector.bn_aggr(stat2[:, t, :], stat6[:, t, :])
                if t == NT - 1:
                    ins.then_inc(g_stats, 1)
                else:
                    chain.link(ins)
            dve.wait_ge(g_root, 1)
            chain.link(nc.vector.reciprocal(lnr[:, :], lnr[:, :]))
            for t in range(NT):
                ins = nc.vector.tensor_scalar(zg[:, t, :], zg[:, t, :], stat2[:, t, 0:1],
                                              lnr[:, t:t + 1], ALU.subtract, ALU.mult)
                ins.then_inc(g_scaled, 1)
            att[0].dve(dve, chain, yb)
            for g in range(GMLP):
                dve.wait_ge(g_mixed, g + 2 - g % 2)
                u = zu[:, :, DH * g:DH * (g + 1)]
                nc.vector.scalar_tensor_tensor(
                    out=u, in0=PS[:, g // 2, 256 * (g % 2):256 * (g % 2 + 1)].rearrange(
                        "p (c d) -> p c d", c=NT),
                    scalar=cols[:, BS + g:BS + g + 1], in1=u, op0=ALU.add, op1=ALU.mult).then_inc(ya_done, 1)
            y_dve(dve, 0, (4, 6, 0, 2))
            out_dve(dve, 0)

        def even_pool(pool, chain):
            for x_, (z, s) in enumerate(((zk, k_sq), (zq, q_sq))):
                pool.wait_ge(z_copied, NT * (x_ + 1))
                v = z[:, :, :].rearrange("p t d -> p (t d)")
                nc.gpsimd.tensor_tensor(s, v, v, ALU.mult).then_inc(qk_squared, 1)
            pool.wait_ge(g_scaled, NT)
            for t in range(NT):
                chain.link(nc.gpsimd.tensor_tensor(zg[:, t, :], zg[:, t, :], lng[:, :], ALU.mult))
                ins = nc.gpsimd.tensor_tensor(zg[:, t, :], zg[:, t, :], lnb[:, :], ALU.add)
                if t == NT - 1:
                    ins.then_inc(g_normed, 1)
                else:
                    chain.step(ins)
            pool.wait_ge(ws_copied, 1)
            nc.gpsimd.affine_select(out=wsT[:, :, :], in_=wsT[:, :, :], pattern=[[0, HEADS], [1, P]],
                                    compare_op=ALU.is_ge, fill=0.0, base=0,
                                    channel_multiplier=-1).then_inc(ws_masked, 1)

        c_done = sem("c_done")
        c_sig = sem("c_sig")
        c_glu = sem("c_glu")
        c_conv = sem("c_conv")
        z1_done, z1_copied = sem("z1_done"), sem("z1_copied")
        s1_squared, s1_summed, s1_root, s1_ready = sem("s1_squared"), sem("s1_summed"), sem("s1_root"), sem("s1_ready")
        t1_turned, t1_copied = sem("t1_turned"), sem("t1_copied")
        m_done, m_sub, m_sq, v_done, v_root, c_scaled = sem("m_done"), sem("m_sub"), sem("m_sq"), sem("v_done"), sem("v_root"), sem("c_scaled")
        c_padded = sem("c_padded")

        def odd_pe(pe):
            wait_aT(pe, 3)
            n0 = first["odd_conv"]
            for x in range(4):
                landed(pe, n0 + x)
            for j in range(4):
                for g in range(2):
                    for c in range(KC):
                        last = pe.matmul(PS[:, 2 * j + g, :], slot(n0 + 2 * g + c // 4, 4)[:, c % 4, P * j:P * (j + 1)],
                                         aT[:, c, :], start=(c == 0), stop=(c == KC - 1))
                    last.then_inc(c_done, 1)
            for b, (name, k, w) in enumerate((("odd_q", 2, HALF), ("odd_kv", 1, 256))):
                n0 = first[name]
                for x in range(k):
                    landed(pe, n0 + x)
                for t in range(NT):
                    if b:
                        pe.wait_ge(z1_copied, t + 1)
                    else:
                        pe.wait_ge(c_glu, t // 2 + 1)
                    for c in range(KC):
                        rhs = slot(n0 + c // 4, 4)[:, c % 4, :] if k == 2 else slot(n0, KC)[:, c, :]
                        last = pe.matmul(PS[:, t, 0:w], aT[:, c, P * t:P * (t + 1)], rhs,
                                         start=(c == 0), stop=(c == KC - 1))
                    last.then_inc(z1_done, 1)
            pe.wait_ge(c_glu, 4)
            for j in range(4):
                pe.wait_ge(c_conv, j + 1)
                last = pe.matmul(PS[:, 4, :], mean_w[:, :], cacc[:, j, :], start=(j == 0), stop=(j == 3))
            last.then_inc(m_done, 1)
            pe.wait_ge(z1_copied, 2 * NT)
            pe.wait_ge(s1_ready, 1)
            for j in range(5):
                if j == 4:
                    pe.wait_ge(t1_copied, 1)
                for t in range(NT):
                    if j < 4:
                        src = qp[:, t, P * j:P * (j + 1)]
                    else:
                        src = kv[:, t, 0:P]
                    last = pe.transpose(PS[:, j % 4, P * t:P * (t + 1)], src, ident[:, :])
                last.then_inc(t1_turned, 1)
            for j in range(4):
                pe.wait_ge(m_sq, j + 1)
                last = pe.matmul(PS[:, 5, :], mean_w[:, :], cacc[:, j, :], start=(j == 0), stop=(j == 3))
            last.then_inc(v_done, 1)
            pe.wait_ge(t1_copied, 5)
            pe.wait_ge(v_root, 1)
            att[1].pe(pe)
            pe.wait_ge(att[1].written, len(UNITS))
            for c in range(4):
                for t in range(NT):
                    last = pe.transpose(PS[:, c, P * t:P * (t + 1)], y1[:, t, P * c:P * (c + 1)], ident[:, :])
                last.then_inc(y_turned, 1)
            out_pe(pe, 1)

        def odd_act(act, chain):
            for j in range(4):
                act.wait_ge(c_done, 2 * j + 2)
                if j >= 2:
                    act.wait_ge(c_glu, j - 1)
                nc.scalar.activation(sgc[:, j % 2, :], PS[:, 2 * j + 1, :], ACT.Sigmoid).then_inc(c_sig, 1)
            for b, dst in enumerate((zq, kv)):
                for t in range(NT):
                    act.wait_ge(z1_done, NT * b + t + 1)
                    nc.scalar.activation(dst[:, t, :], PS[:, t, 0:(HALF, 256)[b]], ACT.Copy).then_inc(z1_copied, 1)
            act.wait_ge(s1_summed, 2)
            nc.scalar.activation(qk_ss[:, :, :], qk_ss[:, :, :], ACT.Sqrt, bias=eps[:, :],
                                 scale=1.0 / DH).then_inc(s1_root, 1)
            for j in range(4):
                act.wait_ge(m_sub, j + 1)
                nc.scalar.activation(cacc[:, j, :], cd[:, j, :], ACT.Square).then_inc(m_sq, 1)
            for j in range(5):
                act.wait_ge(t1_turned, j + 1)
                dst = qT1[:, j, :] if j < 4 else kT1
                nc.scalar.activation(dst, PS[:, j % 4, :], ACT.Copy,
                                     scale=DH ** -0.5 if j < 4 else 1.0).then_inc(t1_copied, 1)
            act.wait_ge(v_done, 1)
            nc.scalar.activation(sgc[:, 0, :], PS[:, 5, :], ACT.Sqrt, bias=eps[:, :]).then_inc(v_root, 1)
            for j in range(4):
                act.wait_ge(c_scaled, j + 1)
                nc.scalar.activation(yT[:, 4 + j, :], cd[:, j, :], ACT.Silu, bias=cols[:, CLB + j:CLB + j + 1],
                                     scale=cols[:, CLG + j:CLG + j + 1]).then_inc(yT_act, 1)
            att[1].act(act)
            y_act(act, 1, (1, 3))

        def odd_dve(dve, chain):
            chain.link(nc.vector.memset(cin[:, :, 0:TAPS - 1], 0.0))
            for j in range(4):
                dve.wait_ge(c_sig, j + 1)
                nc.vector.tensor_tensor(cin[:, j, TAPS - 1:TAPS - 1 + SEQ], PS[:, 2 * j, :],
                                        sgc[:, j % 2, :], ALU.mult).then_inc(c_glu, 1)
                dve.wait_ge(c_glu, j + 1)
                for k in range(TAPS):
                    acc = cacc[:, j, :] if k % 2 == 0 else cacc2
                    src, w = cin[:, j, k:k + SEQ], tapw[:, j, k:k + 1]
                    if k < 2:
                        chain.step(nc.vector.tensor_scalar(acc, src, w, None, ALU.mult))
                    else:
                        chain.wait(behind=1)
                        chain.step(nc.vector.scalar_tensor_tensor(out=acc, in0=src, scalar=w, in1=acc,
                                                                  op0=ALU.mult, op1=ALU.add))
                chain.wait()
                nc.vector.tensor_tensor(cacc[:, j, :], cacc[:, j, :], cacc2, ALU.add).then_inc(c_conv, 1)
                dve.wait_ge(c_conv, j + 1)
            dve.wait_ge(s1_squared, 1)
            nc.vector.tensor_reduce(qk_ss[:, 0, :], sq1.rearrange("p (g d) -> p g d", d=DH),
                                    AX.X, ALU.add).then_inc(s1_summed, 1)
            dve.wait_ge(s1_squared, 2)
            chain.link(nc.vector.memset(qk_ss[:, 1, 8:32], 1.0))
            nc.vector.tensor_reduce(qk_ss[:, 1, 0:8], sq1[:, 0:512].rearrange("p (g d) -> p g d", d=DH),
                                    AX.X, ALU.add).then_inc(s1_summed, 1)
            dve.wait_ge(s1_root, 1)
            chain.link(nc.vector.reciprocal(qk_ss[:, :, :], qk_ss[:, :, :]))
            for x_, (heads, z) in enumerate(((8, zq[:, :, :]), (2, kv[:, :, 0:P]))):
                for t in range(NT):
                    v = z[:, t].rearrange("p (g d) -> p g d", d=DH)
                    r = qk_ss[:, x_, heads * t:heads * (t + 1)].unsqueeze(2).to_broadcast([P, heads, DH])
                    chain.link(nc.vector.tensor_tensor(v, v, r, ALU.mult))
                    g = gq1[:, x_, :].unsqueeze(1).to_broadcast([P, heads, DH])
                    if x_:
                        chain.link(nc.vector.tensor_tensor(v, v, g, ALU.mult))
                    else:
                        w = qp[:, t, :]
                        chain.link(nc.vector.tensor_tensor(
                            w.rearrange("p (j f d) -> p f j d", f=2, j=4), v.rearrange("p (f j) d -> p f j d", f=2),
                            gq1[:, 0, :].unsqueeze(1).unsqueeze(1).to_broadcast([P, 2, 4, DH]), ALU.mult))
                        v = w.rearrange("p (g d) -> p g d", d=DH)
                    x1, x2 = v[:, :, 0:8], v[:, :, 8:16]
                    cos = rope[:, 0, t, :].unsqueeze(1).to_broadcast([P, heads, 8])
                    sin = rope[:, 1, t, :].unsqueeze(1).to_broadcast([P, heads, 8])
                    tm = [junk_r[:, 64 * i_:64 * i_ + 8 * heads].rearrange("p (g d) -> p g d", d=8) for i_ in range(4)]
                    chain.step(nc.vector.tensor_tensor(tm[0], x1, cos, ALU.mult))
                    chain.step(nc.vector.tensor_tensor(tm[1], x2, sin, ALU.mult))
                    chain.step(nc.vector.tensor_tensor(tm[2], x2, cos, ALU.mult))
                    chain.link(nc.vector.tensor_tensor(tm[3], x1, sin, ALU.mult))
                    chain.step(nc.vector.tensor_tensor(x1, tm[0], tm[1], ALU.subtract))
                    ins = nc.vector.tensor_tensor(x2, tm[2], tm[3], ALU.add)
                    if x_ == 1 and t == NT - 1:
                        ins.then_inc(s1_ready, 1)
                    else:
                        chain.link(ins)
            dve.wait_ge(m_done, 1)
            for j in range(4):
                nc.vector.tensor_tensor(cd[:, j, :], cacc[:, j, :], PS[:, 4, :], ALU.subtract).then_inc(m_sub, 1)
            dve.wait_ge(v_root, 1)
            chain.link(nc.vector.reciprocal(sgc[:, 1, :], sgc[:, 0, :]))
            for j in range(4):
                nc.vector.tensor_tensor(cd[:, j, :], cd[:, j, :], sgc[:, 1, :], ALU.mult).then_inc(c_scaled, 1)
            att[1].dve(dve, chain, y1)
            y_dve(dve, 1, (0, 2))
            out_dve(dve, 1)


        def odd_pool(pool, chain):
            pool.wait_ge(z1_copied, NT)
            v = zq[:, :, :].rearrange("p t d -> p (t d)")
            nc.gpsimd.tensor_tensor(sq1, v, v, ALU.mult).then_inc(s1_squared, 1)
            pool.wait_ge(z1_copied, 2 * NT)
            pool.wait_ge(s1_summed, 1)
            v = kv[:, :, 0:P]
            nc.gpsimd.tensor_tensor(sq1[:, 0:512].rearrange("p (t d) -> p t d", t=NT), v, v,
                                    ALU.mult).then_inc(s1_squared, 1)

        logits_done = sem("logits_done")
        r_exp, r_exped = sem("r_exp"), sem("r_exped")
        chosen, ranked = sem("chosen"), sem("ranked")
        most_ready = sem("most_ready")
        pos_ready = sem("pos_ready")
        sel_ready, gathered, xT_ready = sem("sel_ready"), sem("gathered"), sem("xT_ready")
        gateup, silu_ready, hid_ready = sem("gateup"), sem("silu_ready"), sem("hid_ready")
        hid_turned, hidT_ready = sem("hid_turned"), sem("hidT_ready")
        down_lo, down_hi, y_lo, y_hi = sem("down_lo"), sem("down_hi"), sem("y_lo"), sem("y_hi")
        y_stored = [sem("y_stored0"), sem("y_stored1")]
        row_loaded = [sem(f"row_loaded{b}") for b in range(NT)]
        row_used = sem("row_used")

        o = 0
        def rt(n):
            nonlocal o
            o += n
            return rtmp[:, o - n:o]
        logit = rt(NT * 36).rearrange("p (t e) -> p t e", t=NT)
        cpad = rt(NT * 8).rearrange("p (t e) -> p t e", t=NT)
        top_c = rt(NT * 8).rearrange("p (t e) -> p t e", t=NT)
        idx_c = rt(NT * 8).rearrange("p (t e) -> p t e", t=NT).bitcast(U32)
        gid = rt(NT)
        goh = rt(NT * GROUPS).rearrange("p (t g) -> p t g", t=NT)
        fprod = rt(NT * 32).rearrange("p (t g e) -> p t g e", t=NT, g=GROUPS)
        fsel = rt(NT * 8).rearrange("p (t e) -> p t e", t=NT)
        top_f = rt(NT * 8).rearrange("p (t e) -> p t e", t=NT)
        idx_f = rt(NT * 8).rearrange("p (t e) -> p t e", t=NT).bitcast(U32)
        eid = rt(NT * 2).rearrange("p (t k) -> p t k", t=NT)
        cexp = rt(NT * GROUPS).rearrange("p (t g) -> p t g", t=NT)
        psum_ = rt(NT)
        e2 = rt(NT)
        one1 = rt(NT * 32).rearrange("p (t e) -> p t e", t=NT)
        one2 = rt(NT * 32).rearrange("p (t e) -> p t e", t=NT)
        both = rt(NT * 32).rearrange("p (t e) -> p t e", t=NT)
        rank = rt(NT * 32).rearrange("p (t e) -> p t e", t=NT)
        prod = rt(NT * 32).rearrange("p (t e) -> p t e", t=NT)
        rk = rt(NT * 2).rearrange("p (t k) -> p t k", t=NT)
        over = rt(NT * 2 * (ROUNDS - 1)).rearrange("p (t j) -> p t j", j=ROUNDS - 1)
        mostf = rt(1)

        lT = hid_area
        lT_ready, logits_turned = sem("lT_ready"), sem("logits_turned")

        def router_pe(pe, l):
            u = 3 * l + 1
            wait_aT(pe, u)
            for c in range(KC // 2):
                for b in range(2):
                    last = pe.matmul(PS[CAP * b:CAP * b + 36, 0, :], wr[:, l, 4 * b + c, :], aT[:, 4 * b + c, :],
                                     start=(c == 0), stop=(c == KC // 2 - 1))
            last.then_inc(logits_done, 1)
            embed_pe(pe, l)
            pe.wait_ge(lT_ready, 2 * (l + 1))
            for b in range(2):
                for t in range(NT):
                    last = pe.transpose(PS[:, 4 + b, 36 * t:36 * (t + 1)],
                                        lT[CAP * b:CAP * b + 36, P * t:P * (t + 1)],
                                        ident[CAP * b:CAP * b + 36, CAP * b:CAP * b + 36])
            last.then_inc(logits_turned, 1)
            pe.wait_ge(chosen, l + 1)
            for t in range(NT + 1):
                for s in range(min(t + 1, NT)):
                    last = pe.matmul(PS[:, 1, 32 * t:32 * (t + 1)], (upper if s == t else ones)[:, :],
                                     both[:, s, :], start=(s == 0), stop=(s == min(t, NT - 1)))
            last.then_inc(ranked, 1)

        def router_dve(dve, chain, l):
            v = nc.vector
            chain.link(v.memset(cpad[:, :, :], NEG * 1e8))
            dve.wait_ge(logits_done, l + 1)
            for b in range(2):
                v.tensor_copy(lT[CAP * b:CAP * b + 36, :], PS[CAP * b:CAP * b + 36, 0, :]).then_inc(lT_ready, 1)
            dve.wait_ge(logits_turned, l + 1)
            lg = [PS[:, 4 + b, 0:36 * NT].rearrange("p (t e) -> p t e", t=NT) for b in range(2)]
            chain.link(v.tensor_tensor(logit, lg[0], rbias[:, l, :].unsqueeze(1).to_broadcast([P, NT, 36]), ALU.add))
            chain.link(v.tensor_tensor(logit, logit, lg[1], ALU.add))
            chain.link(v.tensor_copy(cpad[:, :, 0:GROUPS], logit[:, :, 0:GROUPS]))
            for t in range(NT):
                chain.step(v.max(top_c[:, t, :], cpad[:, t, :]))
            chain.wait()
            for t in range(NT):
                chain.step(v.max_index(idx_c[:, t, :], top_c[:, t, :], cpad[:, t, :]))
            chain.wait()
            chain.link(v.tensor_copy(gid, idx_c[:, :, 0]))
            chain.link(v.tensor_tensor(goh, iota[:, 0:GROUPS].unsqueeze(1).to_broadcast([P, NT, GROUPS]),
                                       gid.unsqueeze(2).to_broadcast([P, NT, GROUPS]), ALU.is_equal))
            chain.link(v.tensor_tensor(fprod, logit[:, :, GROUPS:36].rearrange("p t (g e) -> p t g e", g=GROUPS),
                                       goh.unsqueeze(3).to_broadcast([P, NT, GROUPS, PER_GROUP]), ALU.mult))
            chain.link(v.tensor_reduce(fsel, fprod.rearrange("p t g e -> p t e g"), AX.X, ALU.add))
            for t in range(NT):
                chain.step(v.max(top_f[:, t, :], fsel[:, t, :]))
            chain.wait()
            for t in range(NT):
                chain.step(v.max_index(idx_f[:, t, :], top_f[:, t, :], fsel[:, t, :]))
            chain.wait()
            chain.link(v.tensor_copy(eid, idx_f[:, :, 0:2]))
            chain.link(v.scalar_tensor_tensor(out=eid, in0=gid.unsqueeze(2).to_broadcast([P, NT, 2]),
                                              scalar=float(PER_GROUP), in1=eid, op0=ALU.mult, op1=ALU.add))
            ids = iota[:, 0:32].unsqueeze(1).to_broadcast([P, NT, 32])
            for k, one in enumerate((one1, one2)):
                chain.step(v.tensor_tensor(one, ids, eid[:, :, k:k + 1].to_broadcast([P, NT, 32]), ALU.is_equal))
            chain.wait()
            v.tensor_tensor(both, one1, one2, ALU.add).then_inc(chosen, 1)
            ple_dve(dve, l, True)
            chain.step(v.tensor_tensor(cexp, logit[:, :, 0:GROUPS], top_c[:, :, 0:1].to_broadcast([P, NT, GROUPS]),
                                       ALU.subtract))
            chain.link(v.tensor_tensor(e2, top_f[:, :, 1], top_f[:, :, 0], ALU.subtract))
            dve.sem_inc(r_exp, 1)
            dve.wait_ge(ranked, l + 1)
            chain.link(v.tensor_copy(rank, PS[:, 1, 0:NT * 32].rearrange("p (t e) -> p t e", t=NT)))
            chain.link(v.scalar_tensor_tensor(out=prod, in0=rank, scalar=1.0, in1=both, op0=ALU.add, op1=ALU.mult))
            chain.link(v.tensor_scalar(rsel[:, :, :], prod, -1.0, None, ALU.add))

        def router_tail_dve(dve, chain, l):
            v = nc.vector
            chain.link(v.tensor_reduce(mostf, PS[:, 1, NT * 32:NT * 32 + 32], AX.X, ALU.max))
            v.tensor_copy(most[:, :], mostf).then_inc(most_ready, 1)
            dve.wait_ge(r_exped, l + 1)
            chain.link(v.tensor_reduce(psum_, cexp, AX.X, ALU.add))
            chain.link(v.tensor_scalar(prob[:, :, 1], e2, 1.0, None, ALU.add))
            chain.link(v.tensor_tensor(psum_, psum_, prob[:, :, 1], ALU.mult))
            chain.link(v.reciprocal(prob[:, :, 0], psum_))
            chain.link(v.tensor_tensor(prob[:, :, 1], prob[:, :, 0], e2, ALU.mult))
            for k, one in enumerate((one1, one2)):
                chain.link(v.tensor_tensor(prod, one, rank, ALU.mult))
                chain.link(v.tensor_reduce(rk[:, :, k], prod, AX.X, ALU.add))
            flat = rk.rearrange("p t k -> p (t k)")
            chain.link(v.tensor_tensor(over, flat.unsqueeze(2).to_broadcast([P, 2 * NT, ROUNDS - 1]),
                                       steps64[:, :].unsqueeze(1).to_broadcast([P, 2 * NT, ROUNDS - 1]), ALU.is_ge))
            chain.link(v.scalar_tensor_tensor(out=rk, in0=eid, scalar=float(CAP), in1=rk, op0=ALU.mult, op1=ALU.add))
            rnd = prod[:, 0, 0:2 * NT]
            chain.link(v.tensor_reduce(rnd, over, AX.X, ALU.add))
            chain.link(v.scalar_tensor_tensor(out=flat, in0=rnd, scalar=float(EXPERTS * CAP - CAP), in1=flat,
                                              op0=ALU.mult, op1=ALU.add))
            v.tensor_copy(posn[:, :, :], rk).then_inc(pos_ready, 1)

        def router_act(act, chain, l):
            act.wait_ge(r_exp, l + 1)
            chain.link(nc.scalar.activation(cexp, cexp, ACT.Exp))
            nc.scalar.activation(e2, e2, ACT.Exp).then_inc(r_exped, 1)

        def pair_items(l, q):
            return [first[f"moe{l}"] + 6 * q + x for x in range(6)]

        def gather_pe(pe, l, it, q):
            g = PAIRS * l + 2 * it + q
            pe.wait_ge(sel_ready, NT * (g + 1))
            if not isinstance(it, int) or g >= 1:
                pe.wait_ge(xT_ready, g)
            gather_half(pe, q, 0)

        def gather_half(pe, q, b):
            for c in range(4 * b, 4 * b + 4):
                for t in range(NT):
                    last = pe.matmul(PS[:, 2 + b, P * (c % 4):P * (c % 4 + 1)],
                                     xn[:, t, P * c:P * (c + 1)], sel[:, q, t, :],
                                     start=(t == 0), stop=(t == NT - 1))
            last.then_inc((gather_lo, gathered)[b], 1)

        def pair_pe(pe, l, it, q, more):
            g = PAIRS * l + 2 * it + q
            ns = pair_items(l, q)
            pe.wait_ge(xT_ready, g + 1)
            if isinstance(it, int) and 2 * it + q == 0:
                pe.wait_ge(p_copied, 2 * (l + 1))
            if not isinstance(it, int) or g >= 1:
                pe.wait_ge(hid_ready, g)
            for part in range(2):
                for e in range(2):
                    n = ns[3 * e + part]
                    pe.wait_ge(slot_loaded[n % SLOTS], 16 * (n // SLOTS + 1) + 16 * it)
                for c in range(KC):
                    for e in range(2):
                        last = pe.matmul(PS[CAP * e:CAP * (e + 1), 4, FE * part:FE * (part + 1)],
                                         xT[:, q, c, CAP * e:CAP * (e + 1)],
                                         slot(ns[3 * e + part], KC)[:, c, :],
                                         start=(c == 0), stop=(c == KC - 1))
            last.then_inc(gateup, 1)
            if more:
                gather_pe(pe, l, it + q, 1 - q)
            pe.wait_ge(hid_ready, g + 1)
            if not isinstance(it, int) or g >= 1:
                pe.wait_ge(hidT_ready, g)
            for f in range(2):
                last = pe.transpose(PS[:, 5, P * f:P * (f + 1)], hid[:, q, P * f:P * (f + 1)], ident[:, :])
            last.then_inc(hid_turned, 1)
            if more:
                gather_half(pe, 1 - q, 1)
            pe.wait_ge(hidT_ready, g + 1)
            for e in range(2):
                n = ns[3 * e + 2]
                pe.wait_ge(slot_loaded[n % SLOTS], 16 * (n // SLOTS + 1) + 16 * it)
            for n in range(2):
                if not isinstance(it, int) or g >= 1:
                    pe.wait_ge((y_lo, y_hi)[n], g)
                for f in range(2):
                    for e in range(2):
                        last = pe.matmul(PS[CAP * e:CAP * (e + 1), 6 + n, :],
                                         hidT[:, q, f, CAP * e:CAP * (e + 1)],
                                         slot(ns[3 * e + 2], 2)[:, f, HALF * n:HALF * (n + 1)],
                                         start=(f == 0), stop=(f == 1))
                last.then_inc((down_lo, down_hi)[n], 1)

        def sel_dve(l, it, q, dve):
            g = PAIRS * l + 2 * it + q
            if not isinstance(it, int) or g >= 2:
                dve.wait_ge(gathered, g - 1)
            for t in range(NT):
                r = rsel[:, t, bass.ds(4 * it + 2 * q, 2)]
                ins = nc.vector.tensor_tensor(sel[:, q, t, :].rearrange("p (e s) -> p e s", e=2),
                                              iota[:, :].unsqueeze(1).to_broadcast([P, 2, CAP]),
                                              r.unsqueeze(2).to_broadcast([P, 2, CAP]), ALU.is_equal)
                ins.then_inc(sel_ready, 1)

        xT_lo, gather_lo = sem("xT_lo"), sem("gather_lo")

        def copy_xT(l, it, q, b, dve):
            g = PAIRS * l + 2 * it + q
            dve.wait_ge((gather_lo, gathered)[b], g + 1)
            base = FFN + KC * l
            nc.vector.tensor_tensor(
                xT[:, q, 4 * b:4 * (b + 1), :], PS[:, 2 + b, :].rearrange("p (c s) -> p c s", c=4),
                cols[:, base + 4 * b:base + 4 * (b + 1)].unsqueeze(2).to_broadcast([P, 4, P]),
                ALU.mult).then_inc((xT_lo, xT_ready)[b], 1)

        def pair_dve(dve, l, it, q, more, more_sel):
            g = PAIRS * l + 2 * it + q
            dve.wait_ge(silu_ready, g + 1)
            nc.vector.tensor_tensor(hid[:, q, :], sgate[:, q, :], PS[:, 4, FE:2 * FE],
                                    ALU.mult).then_inc(hid_ready, 1)
            if more:
                copy_xT(l, it + q, 1 - q, 0, dve)
            dve.wait_ge(hid_turned, g + 1)
            nc.vector.tensor_copy(hidT[:, q, :, :], PS[:, 5, 0:2 * P].rearrange("p (f s) -> p f s", f=2)).then_inc(hidT_ready, 1)
            if more:
                copy_xT(l, it + q, 1 - q, 1, dve)
            if more_sel:
                sel_dve(l, it + 1, q, dve)
            dve.wait_ge(down_hi, g + 1)
            if not isinstance(it, int) or g >= 2:
                dve.wait_ge(y_stored[q], 16 * (PAIRS // 2 * l + it))
            nc.vector.tensor_copy(ysb[:, q, HALF:D], PS[:, 7, :]).then_inc(y_hi, 1)

        def pair_act(act, l, it, q):
            g = PAIRS * l + 2 * it + q
            act.wait_ge(gateup, g + 1)
            if not isinstance(it, int) or g >= 2:
                act.wait_ge(hid_ready, g - 1)
            nc.scalar.activation(sgate[:, q, :], PS[:, 4, 0:FE], ACT.Silu).then_inc(silu_ready, 1)
            act.wait_ge(down_lo, g + 1)
            if not isinstance(it, int) or g >= 2:
                act.wait_ge(y_stored[q], 16 * (PAIRS // 2 * l + it))
            nc.scalar.activation(ysb[:, q, 0:HALF], PS[:, 6, :], ACT.Copy).then_inc(y_lo, 1)
            act.wait_ge(y_lo, g + 1)
            act.wait_ge(y_hi, g + 1)
            act.dma_start(table.rearrange("(r s) d -> r s d", s=P)[bass.ds(2 * it + q, 1)].rearrange("r s d -> (r s) d"),
                          ysb[:, q, :]).then_inc(y_stored[q], 16)

        STEPS = PAIRS // 2
        cold = [{n: sem(f"over{l}_{n}") for n in ("loaded", "used", "shifted", "pe", "dve", "act", "stored")}
                for l in range(DEPTH)]
        OVER_PE = ("gathered", "gateup", "turned", "down")
        OVER_DVE = ("sel0", "sel1", "sel2", "sel3", "xT", "hid", "hidT", "y_hi")
        OVER_ACT = ("silu", "y_lo")

        def over_wait(eng, l, u, what):
            for name, steps in (("pe", OVER_PE), ("dve", OVER_DVE), ("act", OVER_ACT)):
                if what in steps:
                    eng.wait_ge(cold[l][name], u * len(steps) + (steps.index(what) + 1))

        def overflow(eng, l, body, before_round=None):
            n = eng.value_load(most[0:1, 0:1], min_val=0, max_val=SEQ)
            with eng.If(n > CAP):
                for q in range(2):
                    eng.wait_ge(y_stored[q], 16 * STEPS * (l + 1))
                with eng.Fori(0, ROUNDS - 1) as r:
                    if before_round:
                        before_round(r)
                    with eng.Fori(0, EXPERTS) as e:
                        body(r * EXPERTS + e, r, e)
                overflow_end(eng, l)
            eng.end_ifs()

        UNITS_OVER = (ROUNDS - 1) * EXPERTS

        def overflow_end(eng, l):
            eng.wait_ge(cold[l]["stored"], 16 * UNITS_OVER)

        def over_sp(sp, l):
            s = cold[l]
            sp.wait_ge(most_ready, l + 1)

            def body(u, r, e):
                sp.wait_ge(s["used"], u + 1)
                sp.dma_start(cold_gate.rearrange("p (c f) -> p c f", c=KC),
                             a["moe_w_gate"][l, bass.ds(e, 1)].rearrange("e (c p) f -> p (e c) f", p=P)).then_inc(s["loaded"], 16)
                sp.dma_start(cold_up.rearrange("p (c f) -> p c f", c=KC),
                             a["moe_w_up"][l, bass.ds(e, 1)].rearrange("e (c p) f -> p (e c) f", p=P)).then_inc(s["loaded"], 16)
                for f in range(2):
                    sp.dma_start(cold_down[f], a["moe_w_down"][l, bass.ds(e, 1), P * f:P * (f + 1), :].rearrange(
                        "e p f -> (e p) f")).then_inc(s["loaded"], 16)
            overflow(sp, l, body)

        def over_dve(dve, l, chain):
            s = cold[l]

            def shift(r):
                nc.vector.tensor_scalar(rsel[:, :, :], rsel[:, :, :], -float(CAP), None, ALU.add).then_inc(s["shifted"], 1)

            def body(u, r, e):
                dve.wait_ge(s["shifted"], r + 1)
                for t in range(NT):
                    nc.vector.tensor_tensor(sel[:, 0, t, 0:CAP], iota[:, :],
                                            rsel[:, t, bass.ds(e, 1)].to_broadcast([P, CAP]),
                                            ALU.is_equal).then_inc(s["dve"], 1)
                over_wait(dve, l, u, "gathered")
                nc.vector.tensor_tensor(
                    xT[:, 0, :, 0:CAP], PS[:, 2, :].rearrange("p (c s) -> p c s", c=KC),
                    cols[:, FFN + KC * l:FFN + KC * (l + 1)].unsqueeze(2).to_broadcast([P, KC, CAP]),
                    ALU.mult).then_inc(s["dve"], 1)
                over_wait(dve, l, u, "silu")
                nc.vector.tensor_tensor(hid[0:CAP, 0, :], sgate[0:CAP, 0, :], PS[0:CAP, 4, FE:2 * FE],
                                        ALU.mult).then_inc(s["dve"], 1)
                over_wait(dve, l, u, "turned")
                nc.vector.tensor_copy(hidT[:, 0, :, :], PS[:, 5, 0:2 * P].rearrange("p (f s) -> p f s", f=2)).then_inc(s["dve"], 1)
                over_wait(dve, l, u, "down")
                nc.vector.tensor_copy(ysb[0:CAP, 0, HALF:D], PS[0:CAP, 7, :]).then_inc(s["dve"], 1)
                dve.wait_ge(s["stored"], 16 * u + 16)
                dve.sem_inc(s["used"], 1)
            dve.wait_ge(sel_ready, NT * PAIRS * (l + 1))
            dve.wait_ge(y_hi, PAIRS * (l + 1))
            dve.sem_inc(s["used"], 1)
            overflow(dve, l, body, shift)

        def over_act(act, l):
            s = cold[l]

            def body(u, r, e):
                over_wait(act, l, u, "gateup")
                nc.scalar.activation(sgate[0:CAP, 0, :], PS[0:CAP, 4, 0:FE], ACT.Silu).then_inc(s["act"], 1)
                over_wait(act, l, u, "down")
                nc.scalar.activation(ysb[0:CAP, 0, 0:HALF], PS[0:CAP, 6, :], ACT.Copy).then_inc(s["act"], 1)
                over_wait(act, l, u, "y_lo")
                over_wait(act, l, u, "y_hi")
                act.dma_start(table.rearrange("(n s) d -> n s d", s=CAP)[bass.ds(u + EXPERTS, 1)].rearrange("n s d -> (n s) d"),
                              ysb[0:CAP, 0, :]).then_inc(s["stored"], 16)
                act.wait_ge(s["stored"], 16 * u + 16)
            overflow(act, l, body)

        def over_pe(pe, l):
            s = cold[l]

            def body(u, r, e):
                over_wait(pe, l, u, "sel3")
                for c in range(KC):
                    for t in range(NT):
                        last = pe.matmul(PS[:, 2, CAP * c:CAP * (c + 1)], xn[:, t, P * c:P * (c + 1)],
                                         sel[:, 0, t, 0:CAP], start=(t == 0), stop=(t == NT - 1))
                last.then_inc(s["pe"], 1)
                over_wait(pe, l, u, "xT")
                pe.wait_ge(s["loaded"], 64 * u + 64)
                for part, w in enumerate((cold_gate, cold_up)):
                    for c in range(KC):
                        last = pe.matmul(PS[0:CAP, 4, FE * part:FE * (part + 1)], xT[:, 0, c, 0:CAP],
                                         w.rearrange("p (c f) -> p c f", c=KC)[:, c, :],
                                         start=(c == 0), stop=(c == KC - 1))
                last.then_inc(s["pe"], 1)
                over_wait(pe, l, u, "hid")
                for f in range(2):
                    last = pe.transpose(PS[:, 5, P * f:P * (f + 1)], hid[:, 0, P * f:P * (f + 1)], ident[:, :])
                last.then_inc(s["pe"], 1)
                over_wait(pe, l, u, "hidT")
                for n in range(2):
                    for f in range(2):
                        last = pe.matmul(PS[0:CAP, 6 + n, :], hidT[:, 0, f, 0:CAP],
                                         cold_down[f][:, HALF * n:HALF * (n + 1)],
                                         start=(f == 0), stop=(f == 1))
                last.then_inc(s["pe"], 1)
            overflow(pe, l, body)

        def combine_pool(pool, l):
            pool.wait_ge(most_ready, l + 1)
            pool.wait_ge(pos_ready, l + 1)
            for q in range(2):
                pool.wait_ge(y_stored[q], 16 * STEPS * (l + 1))
            n = pool.value_load(most[0:1, 0:1], min_val=0, max_val=SEQ)

            def gathers(rows_of):
                for m in range(2 * NT):
                    t, k = m // 2, m % 2
                    if m >= NT:
                        pool.wait_ge(*row_added(l, m - NT))
                    nc.gpsimd.indirect_dma_start(
                        out=gath[:, m % NT, :], out_offset=None, in_=rows_of,
                        in_offset=bass.IndirectOffsetOnAxis(ap=posn[:, t, k:k + 1], axis=0)
                    ).then_inc(row_loaded[m % NT], 16)

            with pool.If(n > CAP):
                overflow_end(pool, l)
                gathers(table)
            with pool.Else():
                gathers(table[0:EXPERTS * CAP])
            pool.end_ifs()

        def row_added(l, m):
            t, k = m // 2, m % 2
            return (h_ready, NT * (3 * l + 1) + t + 1) if k else (row_used, NT * l + t + 1)

        def combine_dve(dve, l):
            for m in range(2 * NT):
                t, k = m // 2, m % 2
                dve.wait_ge(row_loaded[m % NT], 16 * (2 * l + m // NT + 1))
                if k:
                    dve.wait_ge(*row_added(l, m - 1))
                nc.vector.scalar_tensor_tensor(out=h[:, t, :], in0=gath[:, m % NT, :], scalar=prob[:, t, k:k + 1],
                                               in1=h[:, t, :], op0=ALU.mult, op1=ALU.add
                                               ).then_inc(row_added(l, m)[0], 1)

        p_loaded, p_turned, p_copied = sem("p_loaded"), sem("p_turned"), sem("p_copied")
        gate_done, emb_done = sem("gate_done"), sem("emb_done")
        sig_ready, gated = sem("sig_ready"), sem("gated")

        def embed_pe(pe, l):
            pe.wait_ge(p_loaded, 16 * (l + 1))
            for k in range(2):
                for t in range(NT):
                    last = pe.transpose(PS[:, 6 + k, P * t:P * (t + 1)], psb[:, t, P * k:P * (k + 1)], ident[:, :])
            last.then_inc(p_turned, 1)

        def added(l, m):
            t, n = m // 2, m % 2
            return (h_ready, NT * (3 * l + 2) + t + 1) if n else (gated, NT * l + t + 1)

        def ple_pe(pe, l):
            u = 3 * l + 2
            ng, np_ = first[f"pgate{l}"], first[f"pproj{l}"]
            wait_aT(pe, u)
            for x in range(4):
                landed(pe, ng + x)
            landed(pe, np_)
            for t in range(NT):
                for n in range(2):
                    m = 2 * t + n
                    if m >= 4:
                        pe.wait_ge(*added(l, m - 4))
                    for c in range(KC):
                        last = pe.matmul(PS[:, m % 4, :], aT[:, c, P * t:P * (t + 1)],
                                         slot(ng + 2 * n + c // 4, 4)[:, c % 4, :],
                                         start=(c == 0), stop=(c == KC - 1))
                    last.then_inc(gate_done, 1)
                    for k in range(2):
                        last = pe.matmul(PS[:, 4 + m % 4, :], pT[:, k, P * t:P * (t + 1)],
                                         slot(np_, 2)[:, k, HALF * n:HALF * (n + 1)],
                                         start=(k == 0), stop=(k == 1))
                    last.then_inc(emb_done, 1)

        def ple_act(act, l):
            for m in range(2 * NT):
                act.wait_ge(gate_done, 8 * l + m + 1)
                if m >= 2:
                    act.wait_ge(*added(l, m - 2))
                nc.scalar.activation(sgp[:, m % 2, :], PS[:, m % 4, :], ACT.Sigmoid).then_inc(sig_ready, 1)

        def ple_dve(dve, l, copy):
            if copy:
                dve.wait_ge(p_turned, l + 1)
                for k in range(2):
                    nc.vector.tensor_copy(pT[:, k, :], PS[:, 6 + k, :]).then_inc(p_copied, 1)
                return
            for m in range(2 * NT):
                t, n = m // 2, m % 2
                part = h[:, t, HALF * n:HALF * (n + 1)]
                dve.wait_ge(sig_ready, 8 * l + m + 1)
                dve.wait_ge(emb_done, 8 * l + m + 1)
                nc.vector.tensor_tensor(sgp[:, m % 2, :], sgp[:, m % 2, :], PS[:, 4 + m % 4, :],
                                        ALU.mult).then_inc(gated_mul, 1)
                dve.wait_ge(gated_mul, 8 * l + m + 1)
                nc.vector.tensor_tensor(part, part, sgp[:, m % 2, :], ALU.add).then_inc(added(l, m)[0], 1)

        gated_mul = sem("gated_mul")

        def released(n):
            for l in range(DEPTH):
                k = n - first[f"out{l}"]
                if 0 <= k < 4:
                    return proj_done, 8 * (l + 1)
                k = n - first[f"pgate{l}"]
                if 0 <= k < 5:
                    return emb_done, 8 * (l + 1)
                k = n - first[f"moe{l}"]
                if 0 <= k < 3 * EXPERTS:
                    return expert_released(l, 0, k)
            k = n - first["even_in"]
            if 0 <= k < 10:
                return z_done, NT * (k // 2 + 1)
            k = n - first["odd_conv"]
            return (c_done, 8) if k < 4 else (z1_done, NT) if k < 6 else (z1_done, 2 * NT)

        def expert_released(l, it, k):
            pair = PAIRS * l + 2 * it + k // 6
            return (down_hi if k % 3 == 2 else gateup), pair + 1

        @block.sync
        def _(sp):
            for t in range(NT):
                sp.dma_start(h[:, t, :], a["x"][0, P * t:P * (t + 1), :]).then_inc(x_loaded[t], 16)

            def load(n):
                src, c = items[n]
                if n >= SLOTS:
                    sp.wait_ge(*released(n - SLOTS))
                sp.dma_start(slot(n, c), src).then_inc(slot_loaded[n % SLOTS], 16)

            n = 0
            for l in range(DEPTH):
                m0 = first[f"moe{l}"]
                while n < m0 + SLOTS:
                    load(n)
                    n += 1
                if 3 * l + 1 >= stages:
                    break
                with sp.Fori(1, STEPS) as it:
                    for x in range(4):
                        e = bass.ds(4 * it + x, 1)
                        for y, (w, c) in enumerate((("moe_w_gate", KC), ("moe_w_up", KC), ("moe_w_down", 2))):
                            k = 3 * x + y
                            s_, v_ = expert_released(l, it - 1, k)
                            sp.wait_ge(s_, v_)
                            sp.dma_start(slot(m0 + k, c), a[w][l, e].rearrange("e (c p) f -> p (e c) f", p=P)
                                         ).then_inc(slot_loaded[(m0 + k) % SLOTS], 16)
                n = m0 + 3 * EXPERTS
                over_sp(sp, l)
                if 3 * l + 2 >= stages:
                    break
                while n < first[f"pproj{l}"] + 1:
                    load(n)
                    n += 1
                if 3 * l + 3 >= stages:
                    break
                sp.wait_ge(row_loaded[NT - 1], 32 * (l + 1))
            for t in range(NT):
                sp.wait_ge(h_ready, NT * (stages - 1) + t + 1)
                sp.dma_start(out[0, P * t:P * (t + 1), :], h[:, t, :]).then_inc(out_stored, 16)
            sp.wait_ge(out_stored, 16 * NT)

        def small_loads(eng):
            loads = [
                (tap_rows, a["conv_w"][0]),
                (bf8[:, :], a["fox_b_f"].rearrange("o h -> h o")),
                (wf[:, :, :], kblocks(even_w, 0, KC, 2560, 2568)),
                (lng[:, :], a["gmlp_ln_g"].to_broadcast([P, HALF])),
                (lnb[:, :], a["gmlp_ln_b"].to_broadcast([P, HALF])),
                (rope[:, :, :, :], a["rope"].rearrange("f (t q) d -> q f t d", q=P)),
                (gq1[:, 0, :], a["swa_q_norm"].to_broadcast([P, DH])),
                (gq1[:, 1, :], a["swa_k_norm"].to_broadcast([P, DH])),
                (sinks[:, :], a["swa_sinks"].to_broadcast([P, HEADS])),
            ]
            for l in range(DEPTH):
                loads += [(wr[:, l, :, 0:4], kblocks(a["moe_w_coarse"][l], 0, KC, 0, 4)),
                          (rbias[:, l, 0:4], a["moe_b_coarse"][l:l + 1].to_broadcast([P, 4])),
                          (rbias[:, l, 4:36], a["moe_b_fine"][l:l + 1].rearrange("l g e -> l (g e)").to_broadcast([P, 32]))]
                loads += [(wr[:, l, :, 4 + 8 * g:12 + 8 * g], kblocks(a["moe_w_fine"][l, g], 0, KC, 0, 8))
                          for g in range(GROUPS)]
            assert len(loads) == N_SMALL
            for dst, src in loads:
                eng.dma_start(dst, src).then_inc(small_loaded, 16)

        def row_loads(eng):
            loads = [
                (rows[MIX:MIX + 16, :], a["norm_mix"].rearrange("l (c p) -> (l c) p", p=P)),
                (rows[FFN:FFN + 16, :], a["norm_ffn"].rearrange("l (c p) -> (l c) p", p=P)),
                (rows[PNORM:PNORM + 16, :], a["ple_norm"].rearrange("l (c p) -> (l c) p", p=P)),
                (rows[BS:BS + 8, :], a["gmlp_b_s"][0]),
                (rows[CLG:CLG + 4, :], a["conv_ln_g"][0].rearrange("(c p) -> c p", p=P)),
                (rows[CLB:CLB + 4, :], a["conv_ln_b"][0].rearrange("(c p) -> c p", p=P)),
                (rows[FQ:FQ + 1, 0:DH], a["fox_q_norm"]), (rows[FQ:FQ + 1, DH:P], a["fox_q_norm"]),
                (rows[FK:FK + 1, 0:DH], a["fox_k_norm"]), (rows[FK:FK + 1, DH:P], a["fox_k_norm"]),
            ]
            assert len(loads) == N_ROWS
            for dst, src in loads:
                eng.dma_start(dst, src).then_inc(rows_loaded, 16)

        rows_loaded = sem("rows_loaded")
        N_ROWS, N_SMALL = 10, 9 + DEPTH * (3 + GROUPS)

        @block.scalar
        def _(act):
            row_loads(act)
            chain = Chain(act, act_chain)
            act.wait_ge(const_ready, 1)
            act.wait_ge(cols_done, 1)
            chain.link(nc.scalar.activation(cols[:, 0:NROWS], PS[:, 0, 0:NROWS], ACT.Copy))
            nc.scalar.activation(gq8[:, :], cols[:, FQ:FQ + 1], ACT.Copy, scale=DH ** -0.5).then_inc(cols_ready, 1)
            for l in range(DEPTH):
                if stages > 3 * l:
                    norm_act(act, chain, 3 * l)
                    (even_act, odd_act)[l](act, chain)
                if stages > 3 * l + 1:
                    act.wait_ge(h_ready, 3 * NT * l + 1)
                    act.dma_start(psb[:, :, :], a["p"][l, 0].rearrange("(t q) d -> q t d", q=P)).then_inc(p_loaded, 16)
                    norm_act(act, chain, 3 * l + 1)
                    router_act(act, chain, l)
                    for q in range(2):
                        pair_act(act, l, 0, q)
                    with act.Fori(1, STEPS) as it:
                        for q in range(2):
                            pair_act(act, l, it, q)
                    act.wait_ge(most_ready, l + 1)
                    over_act(act, l)
                if stages > 3 * l + 2:
                    norm_act(act, chain, 3 * l + 2)
                    ple_act(act, l)

        @block.vector
        def _(dve):
            chain = Chain(dve, dve_chain)
            dve.wait_ge(const_ready, 1)
            dve.wait_ge(cols_ready, 1)
            for l in range(DEPTH):
                if stages > 3 * l:
                    norm_dve(dve, chain, 3 * l)
                    (even_dve, odd_dve)[l](dve, chain)
                if stages <= 3 * l + 1:
                    break
                norm_dve(dve, chain, 3 * l + 1)
                router_dve(dve, chain, l)
                sel_dve(l, 0, 0, dve)
                sel_dve(l, 0, 1, dve)
                copy_xT(l, 0, 0, 0, dve)
                copy_xT(l, 0, 0, 1, dve)
                router_tail_dve(dve, chain, l)
                for q in range(2):
                    pair_dve(dve, l, 0, q, True, True)
                with dve.Fori(1, STEPS - 1) as it:
                    for q in range(2):
                        pair_dve(dve, l, it, q, True, True)
                pair_dve(dve, l, STEPS - 1, 0, True, False)
                pair_dve(dve, l, STEPS - 1, 1, False, False)
                over_dve(dve, l, chain)
                combine_dve(dve, l)
                if stages <= 3 * l + 2:
                    break
                norm_dve(dve, chain, 3 * l + 2)
                ple_dve(dve, l, False)

        @block.tensor
        def _(pe):
            pe.wait_ge(const_ready, 1)
            pe.wait_ge(rows_loaded, 16 * N_ROWS)
            pe.transpose(PS[:, 0, 0:NROWS], rows[0:NROWS, :], ident[0:NROWS, 0:NROWS]).then_inc(cols_done, 1)
            for l in range(DEPTH):
                if stages > 3 * l:
                    norm_pe(pe, 3 * l)
                    (even_pe, odd_pe)[l](pe)
                if stages <= 3 * l + 1:
                    break
                norm_pe(pe, 3 * l + 1)
                router_pe(pe, l)
                gather_pe(pe, l, 0, 0)
                gather_half(pe, 0, 1)
                for q in range(2):
                    pair_pe(pe, l, 0, q, True)
                with pe.Fori(1, STEPS - 1) as it:
                    for q in range(2):
                        pair_pe(pe, l, it, q, True)
                pair_pe(pe, l, STEPS - 1, 0, True)
                pair_pe(pe, l, STEPS - 1, 1, False)
                pe.wait_ge(most_ready, l + 1)
                over_pe(pe, l)
                if stages <= 3 * l + 2:
                    break
                norm_pe(pe, 3 * l + 2)
                ple_pe(pe, l)

        @block.gpsimd
        def _(pool):
            g = nc.gpsimd
            chain = Chain(pool, pool_chain)
            chain.step(g.memset(ident[:, :], 0.0))
            chain.step(g.memset(ones[:, :], 1.0))
            chain.step(g.memset(mean_w[:, :], 1.0 / 512))
            chain.step(g.memset(mask[:, :], 0.0))
            chain.step(g.memset(pick[:, :, :], 0.0))
            chain.step(g.memset(decay[:, :], 0.0))
            chain.step(g.memset(eps[:, :], EPS))
            chain.step(g.iota(iota[:, :], pattern=[[1, CAP]], base=0, channel_multiplier=0,
                              allow_small_or_imprecise_dtypes=True))
            chain.link(g.iota(steps64[:, :], pattern=[[CAP, ROUNDS - 1]], base=CAP, channel_multiplier=0,
                              allow_small_or_imprecise_dtypes=True))
            chain.step(g.affine_select(out=ident[:, :], in_=ident[:, :], compare_op=ALU.not_equal, fill=1.0,
                                       base=0, pattern=[[-1, P]], channel_multiplier=1))
            chain.step(g.affine_select(out=upper[:, :], in_=ones[:, :], compare_op=ALU.is_gt, fill=0.0,
                                       base=0, pattern=[[1, P]], channel_multiplier=-1))
            chain.step(g.affine_select(out=mask[:, 0:P], in_=mask[:, 0:P], compare_op=ALU.is_gt, fill=NEG,
                                       base=0, pattern=[[1, P]], channel_multiplier=-1))
            chain.step(g.affine_select(out=mask[:, P:2 * P], in_=mask[:, P:2 * P], compare_op=ALU.is_ge, fill=NEG,
                                       base=0, pattern=[[-1, P]], channel_multiplier=1))
            for part in range(3):
                v = pick[32 * part:32 * part + HEADS, :, :]
                chain.link(g.affine_select(out=v, in_=v, compare_op=ALU.not_equal, fill=1.0, base=0,
                                           pattern=[[-1, HEADS], [0, P]], channel_multiplier=1))
            g.tensor_copy(ident_b[:, :], ident[:, :]).then_inc(const_ready, 1)
            small_loads(pool)
            for l in range(DEPTH):
                if stages > 3 * l:
                    (even_pool, odd_pool)[l](pool, chain)
                if stages > 3 * l + 1:
                    combine_pool(pool, l)



_INS = ['x', 'p', 'norm_mix', 'even_w_in', 'fox_b_f', 'gmlp_ln_g', 'gmlp_ln_b', 'gmlp_w_s', 'gmlp_b_s',
        'fox_q_norm', 'fox_k_norm', 'even_w_out', 'odd_w_in', 'swa_q_norm', 'swa_k_norm', 'swa_sinks',
        'conv_w', 'conv_ln_g', 'conv_ln_b', 'odd_w_out', 'norm_ffn', 'moe_w_coarse', 'moe_b_coarse',
        'moe_w_fine', 'moe_b_fine', 'moe_w_gate', 'moe_w_up', 'moe_w_down', 'ple_w_proj', 'ple_norm',
        'ple_w_gate']


def rope_table():
    inv = np.float32(500000.0) ** (-np.arange(ROT // 2, dtype=np.float32) * np.float32(2.0) / np.float32(ROT))
    ang = np.arange(SEQ, dtype=np.float32)[:, None] * inv[None, :].astype(np.float32)
    return np.stack([np.cos(ang), np.sin(ang)]).astype(np.float32)


def kernel(**inputs):
    import numpy as _np
    import concourse.bacc as _bacc
    from concourse import mybir as _mybir
    from concourse.bass_utils import run_bass_kernel_spmd as _run

    nc = _bacc.Bacc("TRN2", target_bir_lowering=False, num_devices=1)
    arrays, args = {}, {}
    for name in _INS:
        arrays[f"in_{name}_dram"] = _np.ascontiguousarray(inputs[name])
    arrays["in_rope_dram"] = rope_table()
    for name in _INS + ["rope"]:
        v = arrays[f"in_{name}_dram"]
        args[name] = nc.dram_tensor(f"in_{name}_dram", v.shape, _mybir.dt.from_np(v.dtype), kind="ExternalInput").ap()
    out = nc.dram_tensor("out_0_dram", (1, SEQ, D), F32, kind="ExternalOutput").ap()
    build(nc, args, out)
    r = _run(nc, [arrays], core_ids=[0])
    return r.results[0]["out_0_dram"]
```

```python
from contextlib import ExitStack

import numpy as np
import concourse.bass as bass
from concourse import mybir

F32 = mybir.dt.float32
BF16 = mybir.dt.bfloat16
I32 = mybir.dt.int32
U32 = mybir.dt.uint32
ALU = mybir.AluOpType
ACT = mybir.ActivationFunctionType
AX = mybir.AxisListType

P = 128
SEQ, D, DEPTH = 512, 1024, 2
NT, KC = SEQ // P, D // P
HALF = 512
HEADS, DH = 8, 64
GMLP = 8
GROUPS, PER_GROUP, EXPERTS, FE = 4, 8, 32, 256
CAP = 64
ROUNDS = SEQ // CAP
PAIRS = EXPERTS // 2
TAPS = 31
PLE = 256
EPS = 1e-6
NEG = -1e30
SLOTS, SLOT = 12, 2048
ROT = 16
KB = 256


class Chain:

    def __init__(self, eng, sem):
        self.eng, self.sem, self.count = eng, sem, 0

    def step(self, ins):
        ins.then_inc(self.sem, 1)
        self.count += 1

    def link(self, ins):
        self.step(ins)
        self.wait()

    def wait(self, behind=0):
        if self.count > behind:
            self.eng.wait_ge(self.sem, self.count - behind)


def build(nc, a, out, stages=3 * DEPTH):
    with ExitStack() as ctx:
        def sb(name, shape, dt=F32):
            return ctx.enter_context(nc.sbuf_tensor(name, shape, dt))

        def sem(name):
            return ctx.enter_context(nc.semaphore(name))

        PS = ctx.enter_context(nc.psum_tensor("psum_banks", [P, 8, HALF], F32))
        ring = sb("ring", [P, SLOTS, SLOT])
        h = sb("h_res", [P, NT, D])
        aT = sb("aT", [P, KC, SEQ])
        work = sb("work", [P, 60 * KB])

        def area(kb0, kb1, **dims):
            return work[:, int(kb0 * KB):int(kb1 * KB)]

        xn = area(0, 16).rearrange("p (t d) -> p t d", t=NT)
        junk = area(16, 20)
        zq = area(0, 8).rearrange("p (t d) -> p t d", t=NT)
        zk = area(8, 16).rearrange("p (t d) -> p t d", t=NT)
        ws_raw = area(16, 20).rearrange("p (g s) -> p g s", g=HEADS)
        qT = [area(k, k + 8).rearrange("p (j s) -> p j s", j=4) for k in (20, 8)]
        kT = area(28, 36).rearrange("p (j s) -> p j s", j=4)
        zv = area(36, 44).rearrange("p (t d) -> p t d", t=NT)
        zu = area(44, 52).rearrange("p (t d) -> p t d", t=NT)
        zg = area(52, 60).rearrange("p (t d) -> p t d", t=NT)
        yb = zq
        yT = area(20, 36).rearrange("p (c s) -> p c s", c=KC)
        aflat = aT[:, :, :].rearrange("p c s -> p (c s)")
        wsT = aflat[:, 0:1024].rearrange("p (g s) -> p g s", g=HEADS)
        ebuf = aflat[:, 1024:2048].rearrange("p (b s) -> p b s", b=2)
        ptbuf = aflat[:, 2048:3072].rearrange("p (b s) -> p b s", b=2)
        cin = area(36, 45).rearrange("p (j s) -> p j s", j=4)
        cacc = area(45, 53).rearrange("p (j s) -> p j s", j=4)
        cacc2 = area(53, 55)
        sgc = area(55, 59).rearrange("p (b s) -> p b s", b=2)
        kv = area(8, 12).rearrange("p (t d) -> p t d", t=NT)
        qT1 = [area(k, k + 8).rearrange("p (j s) -> p j s", j=4) for k in (0, 28)]
        sq1 = area(12, 20)
        qp = area(12, 20).rearrange("p (t d) -> p t d", t=NT)
        y1 = qp
        kT1 = area(20, 22)
        junk_r = area(22, 23)
        sq_k = area(25, 27)
        tap_out = {2: (area(20, 22), area(23, 25)), 3: (area(25, 27), area(23, 25))}
        cd = cin[:, :, 0:SEQ]
        xT = area(20, 28).rearrange("p (b c s) -> p b c s", b=2, c=KC)
        sel = area(28, 32).rearrange("p (b t s) -> p b t s", b=2, t=NT)
        sgate = area(32, 34).rearrange("p (b s) -> p b s", b=2)
        hid_area = area(34, 36)
        hid = area(34, 36).rearrange("p (b s) -> p b s", b=2)
        hidT = area(36, 38).rearrange("p (b f s) -> p b f s", b=2, f=2)
        ysb = area(38, 46).rearrange("p (b d) -> p b d", b=2)
        rtmp = area(46, 52)
        cold_down = (area(24, 28), area(42, 46))
        cold_up = aflat[:, 2048:4096]
        cold_gate = aflat[:, 0:2048]
        gath = area(0, 16).rearrange("p (b d) -> p b d", b=NT)
        psb = area(52, 56).rearrange("p (t d) -> p t d", t=NT)
        pT = area(56, 60).rearrange("p (k s) -> p k s", k=2)
        sgp = area(46, 50).rearrange("p (b s) -> p b s", b=2)
        emb = area(20, 36).rearrange("p (m s) -> p m s", m=2 * NT)

        ident = sb("ident", [P, P])
        ones = sb("ones", [P, P])
        mean_w = sb("mean_w", [P, P])
        upper = sb("upper", [P, P])
        ident_b = sb("ident_b", [P, P], BF16)
        mask = sb("mask", [P, 2 * P], BF16)
        pick = sb("pick", [96, HEADS, P], BF16)
        decay = sb("decay", [96, SEQ], BF16)
        iota = sb("iota", [P, CAP])
        steps64 = sb("steps64", [P, ROUNDS - 1])
        eps = sb("eps", [P, 1])
        rows = sb("rows", [P, P])
        cols = sb("cols", [P, P])
        lng = sb("lng", [P, HALF])
        lnb = sb("lnb", [P, HALF])
        wf = sb("wf", [P, KC, HEADS])
        wr = sb("wr", [P, DEPTH, KC, 36])
        rbias = sb("rbias", [P, DEPTH, 36])
        bf8 = sb("bf8", [HEADS, 1])
        rope = sb("rope_sb", [P, 2, NT, ROT // 2])
        gq1 = sb("gq1", [P, 2, DH])
        sinks = sb("sinks", [P, HEADS])
        tapw = sb("tapw", [P, NT, TAPS])
        tap_rows = work[0:TAPS, int(36 * KB):int(38 * KB)]
        ss = sb("ss", [P, 6 * NT])
        root = sb("root", [P, 6 * NT])
        rstd = sb("rstd", [P, 6 * NT])
        qk_ss = sb("qk_ss", [P, 2, 32])
        stat6 = sb("stat6", [P, NT, 6])
        stat2 = sb("stat2", [P, NT, 2])
        lnr = sb("lnr", [P, NT])
        gq8 = sb("gq8", [P, 1])
        nmax = sb("nmax", [P, 32])
        rsum = sb("rsum", [P, 32])
        esink = sb("esink", [P, 32])
        rinv = sb("rinv", [P, 32])
        rsel = sb("rsel", [P, NT, EXPERTS])
        prob = sb("prob", [P, NT, 2])
        posn = sb("posn", [P, NT, 2], I32)
        most = sb("most", [P, 1], I32)
        table = nc.dram_tensor("expert_rows", [ROUNDS * EXPERTS * CAP, D], F32).ap()

        const_ready = sem("const_ready")
        small_loaded = sem("small_loaded")
        x_loaded = [sem(f"x_loaded{t}") for t in range(NT)]
        slot_loaded = [sem(f"slot_loaded{s}") for s in range(SLOTS)]
        cols_done = sem("cols_done")
        cols_ready = sem("cols_ready")
        h_ready = sem("h_ready")
        out_half = sem("out_half")
        act_chain, dve_chain, pool_chain = sem("act_chain"), sem("dve_chain"), sem("pool_chain")
        root_ready = sem("root_ready")
        xn_ready = sem("xn_ready")
        turned = sem("turned")
        aT_act, aT_dve = sem("aT_act"), sem("aT_dve")
        out_stored = sem("out_stored")
        proj_done = sem("proj_done")
        z_done, z_copied = sem("z_done"), sem("z_copied")

        def kblocks(w, c0, c1, n0, n1):
            return w.rearrange("(c p) n -> p c n", p=P)[:, c0:c1, n0:n1]

        def dense_blocks(w, col_list):
            for n0 in col_list:
                for k0 in (0, KC // 2):
                    yield kblocks(w, k0, k0 + KC // 2, n0, n0 + HALF), KC // 2

        even_w, odd_w = a["even_w_in"][0], a["odd_w_in"][0]
        EVEN_COLS = (1536, 1024, 2048, 512, 0)
        ODD_A, ODD_GATE, ODD_Q, ODD_KV = 768, 1280, 0, 512
        items, first = [], {}

        def add(name, its):
            first[name] = len(items)
            items.extend(its)

        def add_tail(l):
            first[f"moe{l}"] = len(items)
            for e in range(EXPERTS):
                items.extend([
                    (a["moe_w_gate"][l, e].rearrange("(c p) f -> p c f", p=P), KC),
                    (a["moe_w_up"][l, e].rearrange("(c p) f -> p c f", p=P), KC),
                    (a["moe_w_down"][l, e].rearrange("(c p) n -> p c n", p=P), 2)])
            add(f"pproj{l}", [(a["ple_w_proj"][l].rearrange("(c p) n -> p c n", p=P), 2)])
            add(f"pgate{l}", dense_blocks(a["ple_w_gate"][l], (0, HALF)))

        add("even_in", dense_blocks(even_w, EVEN_COLS))
        add("out0", dense_blocks(a["even_w_out"][0], (0, HALF)))
        add_tail(0)
        add("odd_conv", dense_blocks(odd_w, (ODD_A, ODD_GATE)))
        add("odd_q", dense_blocks(odd_w, (ODD_Q,)))
        add("odd_kv", [(kblocks(odd_w, 0, KC, ODD_KV, ODD_KV + 256), KC)])
        add("out1", dense_blocks(a["odd_w_out"][0], (0, HALF)))
        add_tail(1)

        def slot(n, c):
            return ring[:, n % SLOTS, :].rearrange("p (c n) -> p c n", c=c)

        def landed(pe, n):
            pe.wait_ge(slot_loaded[n % SLOTS], 16 * (n // SLOTS + 1))

        MIX, FFN, PNORM, BS, CLG, CLB, FQ, FK = 0, 16, 32, 48, 56, 60, 64, 65
        NROWS = 66

        def gain_col(u, c):
            l, kind = u // 3, u % 3
            return cols[:, (MIX, FFN, PNORM)[kind] + KC * l + c:][:, 0:1]

        block = ctx.enter_context(nc.Block())

        UNITS = [(hd, i) for hd in range(HEADS) for i in range(NT)]

        class Attention:

            def __init__(self, layer):
                n = f"att{layer}_"
                self.layer = layer
                self.scored = sem(n + "scored")
                self.maxed = sem(n + "maxed")
                self.exped = sem(n + "exped")
                self.turned = sem(n + "turned")
                self.copied = sem(n + "copied")
                self.summed = sem(n + "summed")
                self.written = sem(n + "written")

            def blocks(self, i):
                return range(i + 1) if self.layer == 0 else range(max(i - 1, 0), i + 1)

            def scores(self, pe, u):
                hd, i = UNITS[u]
                ks = self.blocks(i)
                n = P * len(ks)
                S = PS[:, u % 3, 0:n]
                if self.layer == 0:
                    j, q, k = hd // 2, qT[hd % 2], kT[:, hd // 2, :]
                else:
                    j, q, k = hd % 4, qT1[hd // 4], kT1
                if u >= 3:
                    pe.wait_ge(self.exped, u - 2)
                pe.matmul(S, q[:, j, P * i:P * (i + 1)], k[:, P * ks[0]:P * (i + 1)],
                          start=True, stop=False)
                if self.layer == 0:
                    pe.matmul(S, pick[:, hd, :], decay[:, 0:n], start=False, stop=False)
                    m = mask[:, P:2 * P]
                    S = PS[:, u % 3, n - P:n]
                else:
                    m = mask[:, 2 * P - n:2 * P]
                pe.matmul(S, ident_b[:, :], m, start=False, stop=True).then_inc(self.scored, 1)

            def turn(self, pe, u):
                hd, i = UNITS[u]
                pe.wait_ge(self.exped, u + 1)
                if u >= 2:
                    pe.wait_ge(self.copied, u - 1)
                for x in range(len(self.blocks(i))):
                    last = pe.transpose(PS[:, 3 + u % 2, P * x:P * (x + 1)],
                                        ebuf[:, u % 2, P * x:P * (x + 1)], ident[:, :])
                last.then_inc(self.turned, 1)

            def values(self, pe, u):
                hd, i = UNITS[u]
                ks = self.blocks(i)
                pe.wait_ge(self.copied, u + 1)
                if u >= 2:
                    pe.wait_ge(self.written, u - 1)
                for x, kb in enumerate(ks):
                    v = zv[:, kb, DH * hd:DH * (hd + 1)] if self.layer == 0 else \
                        kv[:, kb, P + DH * (hd // 4):P + DH * (hd // 4 + 1)]
                    last = pe.matmul(PS[:, 5 + u % 2, 0:DH], ptbuf[:, u % 2, P * x:P * (x + 1)], v,
                                     start=(x == 0), stop=(x == len(ks) - 1))
                last.then_inc(self.summed, 1)

            def pe(self, pe, between=None):
                n = len(UNITS)
                self.scores(pe, 0)
                self.scores(pe, 1)
                for u in range(n + 1):
                    if u + 2 < n:
                        self.scores(pe, u + 2)
                    if u < n:
                        self.turn(pe, u)
                    if u >= 1:
                        self.values(pe, u - 1)
                    if between:
                        between(u)

            def copy_turned(self, eng, u):
                w = P * len(self.blocks(UNITS[u][1]))
                eng.wait_ge(self.turned, u + 1)
                if u >= 2:
                    eng.wait_ge(self.summed, u - 1)
                dst, src = ptbuf[:, u % 2, 0:w], PS[:, 3 + u % 2, 0:w]
                if self.layer == 0:
                    nc.vector.tensor_copy(dst, src).then_inc(self.copied, 1)
                else:
                    nc.scalar.activation(dst, src, ACT.Copy).then_inc(self.copied, 1)

            def act(self, act, between=None):
                for u, (hd, i) in enumerate(UNITS):
                    n = P * len(self.blocks(i))
                    act.wait_ge(self.maxed, u + 1)
                    if u >= 2:
                        act.wait_ge(self.turned, u - 1)
                    if self.layer == 1:
                        nc.scalar.activation(esink[:, u:u + 1], sinks[:, hd:hd + 1], ACT.Exp,
                                             bias=nmax[:, u:u + 1])
                    nc.scalar.activation(ebuf[:, u % 2, 0:n], PS[:, u % 3, 0:n], ACT.Exp,
                                         bias=nmax[:, u:u + 1],
                                         accum_out=rsum[:, u:u + 1]).then_inc(self.exped, 1)
                    if self.layer == 1 and u >= 1:
                        self.copy_turned(act, u - 1)
                    if between:
                        between(u)
                if self.layer == 1:
                    self.copy_turned(act, len(UNITS) - 1)

            def dve(self, dve, chain, y, between=None):
                n = len(UNITS)

                def maxima(u):
                    hd, i = UNITS[u]
                    S = PS[:, u % 3, 0:P * len(self.blocks(i))]
                    dve.wait_ge(self.scored, u + 1)
                    if self.layer == 0:
                        nc.vector.tensor_reduce(nmax[:, u:u + 1], S, AX.X, ALU.max,
                                                negate=True).then_inc(self.maxed, 1)
                    else:
                        chain.link(nc.vector.tensor_reduce(rinv[:, u:u + 1], S, AX.X, ALU.max))
                        nc.vector.tensor_scalar(nmax[:, u:u + 1], rinv[:, u:u + 1],
                                                sinks[:, hd:hd + 1], -1.0, ALU.max,
                                                ALU.mult).then_inc(self.maxed, 1)

                maxima(0)
                for u in range(n + 1):
                    if u + 1 < n:
                        maxima(u + 1)
                    if u < n and self.layer == 0:
                        self.copy_turned(dve, u)
                    if u >= 1:
                        v = u - 1
                        hd, i = UNITS[v]
                        if self.layer == 1:
                            dve.wait_ge(self.exped, v + 1)
                            chain.link(nc.vector.tensor_tensor(rsum[:, v:v + 1], rsum[:, v:v + 1],
                                                               esink[:, v:v + 1], ALU.add))
                        chain.link(nc.vector.reciprocal(rinv[:, v:v + 1], rsum[:, v:v + 1]))
                        dve.wait_ge(self.summed, v + 1)
                        nc.vector.tensor_scalar(y[:, i, DH * hd:DH * (hd + 1)],
                                                PS[:, 5 + v % 2, 0:DH], rinv[:, v:v + 1], None,
                                                ALU.mult).then_inc(self.written, 1)
                    if between:
                        between(u)

        att = [Attention(0), Attention(1)]

        def wait_h(eng, u, t):
            if u == 0:
                eng.wait_ge(x_loaded[t], 16)
            else:
                eng.wait_ge(h_ready, NT * (u - 1) + t + 1)

        def norm_act(act, chain, u):
            for t in range(NT):
                if u % 3 == 2 and t < 3:
                    project_act(act, u // 3, ((0, 1, 2, 3), (4, 5), (6, 7))[t])
                k = NT * u + t
                wait_h(act, u, t)
                chain.link(nc.scalar.activation(junk[:, 0:D], h[:, t, :], ACT.Square,
                                                accum_out=ss[:, k:k + 1]))
                nc.scalar.activation(root[:, k:k + 1], ss[:, k:k + 1], ACT.Sqrt, bias=eps[:, :],
                                     scale=1.0 / D).then_inc(root_ready, 1)
            if u == 0:
                cols_act(act, chain)
            for c in range(1, KC, 2):
                act.wait_ge(turned, KC * u + c + 1)
                nc.scalar.activation(aT[:, c, :], PS[:, turn_bank(c), :], ACT.Copy,
                                     scale=gain_col(u, c)).then_inc(aT_act, 1)

        def cols_act(act, chain):
            act.wait_ge(cols_done, 1)
            chain.link(nc.scalar.activation(cols[:, 0:NROWS], PS[:, 3, 0:NROWS], ACT.Copy))
            nc.scalar.activation(gq8[:, :], cols[:, FQ:FQ + 1], ACT.Copy, scale=DH ** -0.5).then_inc(cols_ready, 1)
            act.wait_ge(cols_ready, 1)

        def turn_bank(c):
            return (c + 4) % 8

        def norm_dve(dve, chain, u):
            for t in range(NT):
                k = NT * u + t
                dve.wait_ge(root_ready, k + 1)
                chain.link(nc.vector.reciprocal(rstd[:, k:k + 1], root[:, k:k + 1]))
                wait_h(dve, u, t)
                nc.vector.tensor_scalar(xn[:, t, :], h[:, t, :], rstd[:, k:k + 1], None,
                                        ALU.mult).then_inc(xn_ready, 1)
            if u == 0:
                dve.wait_ge(cols_ready, 1)
            for c in range(0, KC, 2):
                dve.wait_ge(turned, KC * u + c + 1)
                nc.vector.tensor_scalar(aT[:, c, :], PS[:, turn_bank(c), :], gain_col(u, c), None,
                                        ALU.mult).then_inc(aT_dve, 1)

        def norm_pe(pe, u):
            if u % 3 == 0:
                pe.wait_ge(xn_ready, NT * (u + 1))
            for t in range(NT):
                pe.wait_ge(xn_ready, NT * u + t + 1)
                for c in range(4):
                    ins = pe.transpose(PS[:, turn_bank(c), P * t:P * (t + 1)],
                                       xn[:, t, P * c:P * (c + 1)], ident[:, :])
                    if t == NT - 1:
                        ins.then_inc(turned, 1)
            if u == 0:
                pe.wait_ge(rows_loaded, 16 * N_ROWS)
                pe.transpose(PS[:, 3, 0:NROWS], rows[0:NROWS, :], ident[0:NROWS, 0:NROWS]).then_inc(cols_done, 1)
            if u % 3 == 2:
                pe.wait_ge(emb_copied, 8 * (u // 3 + 1))
            for c in range(4, KC):
                if u == 0 and c == 7:
                    pe.wait_ge(cols_ready, 1)
                for t in range(NT):
                    ins = pe.transpose(PS[:, turn_bank(c), P * t:P * (t + 1)],
                                       xn[:, t, P * c:P * (c + 1)], ident[:, :])
                ins.then_inc(turned, 1)

        def wait_aT(pe, u):
            pe.wait_ge(aT_act, KC // 2 * (u + 1))
            pe.wait_ge(aT_dve, KC // 2 * (u + 1))

        y_turned = sem("y_turned")
        yT_act, yT_dve = sem("yT_act"), sem("yT_dve")

        def out_pe(pe, l):
            n0 = first[f"out{l}"]
            pe.wait_ge(yT_act, Y_ACT[l])
            pe.wait_ge(yT_dve, Y_DVE[l])
            for x in range(4):
                landed(pe, n0 + x)
            for t in range(NT):
                if t >= 2:
                    pe.wait_ge(h_ready, 3 * NT * l + t - 1)
                for n in range(2):
                    for c in range(KC):
                        last = pe.matmul(PS[:, (2 * t + n) % 4, :], yT[:, c, P * t:P * (t + 1)],
                                         slot(n0 + 2 * n + c // 4, 4)[:, c % 4, :],
                                         start=(c == 0), stop=(c == KC - 1))
                    last.then_inc(proj_done, 1)

        def out_dve(dve, l):
            for t in range(NT):
                for n in range(2):
                    dve.wait_ge(proj_done, 8 * l + 2 * t + n + 1)
                    part = h[:, t, HALF * n:HALF * (n + 1)]
                    nc.vector.tensor_tensor(part, part, PS[:, (2 * t + n) % 4, :],
                                            ALU.add).then_inc(h_ready if n else out_half, 1)

        Y_ACT, Y_DVE = (4, 4 + 6), (4, 4 + 2)

        f_done, f_root = sem("f_done"), sem("f_root")
        f_abs, f_log = sem("f_abs"), sem("f_log")
        taps_done, taps_copied = sem("taps_done"), sem("taps_copied")
        decay_ready = sem("decay_ready")
        qk_squared = sem("qk_squared")
        qk_summed = sem("qk_summed")
        qk_root = sem("qk_root")
        qk_normed = sem("qk_normed")
        qk_turned = sem("qk_turned")
        qk_copied = sem("qk_copied")
        ws_loaded = sem("ws_loaded")
        ws_turned, ws_copied, ws_masked = sem("ws_turned"), sem("ws_copied"), sem("ws_masked")
        g_stats, g_root, g_scaled, g_normed = sem("g_stats"), sem("g_root"), sem("g_scaled"), sem("g_normed")
        q_padded = sem("q_padded")
        g_mixed, ya_done = sem("g_mixed"), sem("ya_done")

        def forget_pe(pe):
            pe.wait_ge(small_loaded, 16 * N_SMALL)
            pe.wait_ge(const_ready, 2)
            for j in range(NT):
                last = pe.transpose(PS[:, 5, 32 * j:32 * j + TAPS], tap_rows[:, P * j:P * (j + 1)],
                                    ident[0:TAPS, 0:TAPS])
            last.then_inc(taps_done, 1)
            for c in range(KC):
                last = pe.matmul(PS[0:HEADS, 4, :], wf[:, c, :], aT[:, c, :], start=(c == 0),
                                 stop=(c == KC - 1))
            last.then_inc(f_done, 1)

        def even_pe(pe):
            wait_aT(pe, 0)
            n0 = first["even_in"]
            for b in range(5):
                if b == 1:
                    forget_pe(pe)
                for x in range(2):
                    landed(pe, n0 + 2 * b + x)
                for t in range(NT):
                    m = NT * b + t
                    if m >= 4:
                        pe.wait_ge(z_copied, m - 3)
                    for c in range(KC):
                        last = pe.matmul(PS[:, m % 4, :], aT[:, c, P * t:P * (t + 1)],
                                         slot(n0 + 2 * b + c // 4, 4)[:, c % 4, :],
                                         start=(c == 0), stop=(c == KC - 1))
                    last.then_inc(z_done, 1)
                if b == 3:
                    for x, z in enumerate((zk, zq)):
                        pe.wait_ge(qk_normed, x + 1)
                        for j in range(4):
                            if x:
                                pe.wait_ge(qk_copied, j + 1)
                            else:
                                pe.wait_ge(f_abs, 1)
                                pe.wait_ge(taps_copied, 1)
                            for t in range(NT):
                                last = pe.transpose(PS[:, 4 + j, P * t:P * (t + 1)],
                                                    z[:, t, P * j:P * (j + 1)], ident[:, :])
                            last.then_inc(qk_turned, 1)
            pe.wait_ge(ws_loaded, 16)
            pe.wait_ge(qk_copied, 12)
            for g in range(HEADS):
                last = pe.transpose(PS[:, 6 + g // 4, P * (g % 4):P * (g % 4 + 1)], ws_raw[:, g, :],
                                    ident[:, :])
            last.then_inc(ws_turned, 1)
            pe.wait_ge(z_copied, 5 * NT)
            pe.wait_ge(decay_ready, 1)
            pe.wait_ge(q_padded, 2)
            pe.wait_ge(ws_copied, 1)
            att[0].pe(pe)
            pe.wait_ge(ws_masked, 1)
            pe.wait_ge(g_normed, 1)
            pe.wait_ge(att[0].written, len(UNITS))
            for g in range(GMLP):
                pe.matmul(PS[:, g // 2, 256 * (g % 2):256 * (g % 2 + 1)].rearrange(
                    "p (c d) -> p c d", c=NT), wsT[:, g, :],
                    zg[:, :, DH * g:DH * (g + 1)], start=True, stop=True).then_inc(g_mixed, 1)
            for n, c in enumerate((4, 5, 6, 7, 0, 1, 2, 3)):
                if c < 4:
                    pe.wait_ge(ya_done, GMLP)
                y = yb if c >= 4 else zu
                for t in range(NT):
                    last = pe.transpose(PS[:, c, P * t:P * (t + 1)],
                                        y[:, t, P * (c % 4):P * (c % 4 + 1)], ident[:, :])
                last.then_inc(y_turned, 1)
            out_pe(pe, 0)

        def even_act(act, chain):
            def copy(b, dst, func=ACT.Copy):
                for t in range(NT):
                    act.wait_ge(z_done, NT * b + t + 1)
                    nc.scalar.activation(dst[:, t, :], PS[:, (NT * b + t) % 4, :],
                                         func).then_inc(z_copied, 1)

            copy(0, zk)
            act.wait_ge(taps_done, 1)
            nc.scalar.activation(tapw[:, :, :], PS[:, 5, 0:NT * 32].rearrange("p (j k) -> p j k", j=NT)[:, :, 0:TAPS],
                                 ACT.Copy).then_inc(taps_copied, 1)
            act.dma_start(ws_raw[:, :, :], a["gmlp_w_s"][0].rearrange("g t s -> t g s")).then_inc(ws_loaded, 16)

            act.wait_ge(const_ready, 2)
            act.wait_ge(f_abs, 1)
            chain.link(nc.scalar.activation(junk8[:, 1, :], junk8[:, 1, :], ACT.Exp, scale=-1.0))
            nc.scalar.activation(junk8[:, 1, :], junk8[:, 1, :], ACT.Ln, bias=ones[0:HEADS, 0:1]).then_inc(f_log, 1)
            copy(1, zq)
            copy(2, zv)
            act.wait_ge(qk_summed, 2)
            nc.scalar.activation(qk_ss[:, :, :], qk_ss[:, :, :], ACT.Sqrt, bias=eps[:, :],
                                 scale=1.0 / DH).then_inc(qk_root, 1)
            copy(3, zg, ACT.Gelu_apprx_tanh)
            copy(4, zu, ACT.Gelu_apprx_tanh)
            act.wait_ge(g_stats, 1)
            nc.scalar.activation(lnr[:, :], stat2[:, :, 1], ACT.Sqrt, bias=eps[:, :]).then_inc(g_root, 1)
            act.wait_ge(ws_turned, 1)
            chain.step(nc.scalar.activation(wsT[:, 0:4, :], PS[:, 6, :].rearrange("p (g s) -> p g s", g=4), ACT.Copy))
            nc.scalar.activation(wsT[:, 4:8, :], PS[:, 7, :].rearrange("p (g s) -> p g s", g=4), ACT.Copy).then_inc(ws_copied, 1)
            att[0].act(act)
            y_act(act, 0, (5, 7, 1, 3))

        Y_ORDER = ((4, 5, 6, 7, 0, 1, 2, 3), (0, 1, 2, 3))

        def y_act(act, l, cs):
            for c in cs:
                act.wait_ge(y_turned, 8 * l + Y_ORDER[l].index(c) + 1)
                nc.scalar.activation(yT[:, c, :], PS[:, c, :], ACT.Copy).then_inc(yT_act, 1)

        def y_dve(dve, l, cs):
            for c in cs:
                dve.wait_ge(y_turned, 8 * l + Y_ORDER[l].index(c) + 1)
                nc.vector.tensor_copy(yT[:, c, :], PS[:, c, :]).then_inc(yT_dve, 1)

        junk8 = area(20, 26)[0:HEADS, :].rearrange("p (b s) -> p b s", b=3)
        k_sq, q_sq = area(52, 60), area(44, 52)

        def even_dve(dve, chain):
            dve.wait_ge(const_ready, 2)
            dve.wait_ge(f_done, 1)
            x, e, c_ = junk8[:, 0, :], junk8[:, 1, :], junk8[:, 2, :]
            chain.link(nc.vector.tensor_scalar(x, PS[0:HEADS, 4, :], bf8[:, :], None, ALU.add))
            chain.link(nc.vector.tensor_scalar(e, x, -1.0, None, ALU.mult))
            nc.vector.tensor_tensor(e, x, e, ALU.max).then_inc(f_abs, 1)
            chain.link(nc.vector.tensor_scalar(x, x, 0.0, None, ALU.min))
            dve.wait_ge(f_log, 1)
            chain.link(nc.vector.tensor_tensor(x, e, x, ALU.subtract))
            chain.link(nc.vector.memset(e, 1.0))
            chain.link(nc.vector.tensor_tensor_scan(c_, e, x, 0.0, ALU.mult, ALU.add))
            for part in range(3):
                r = decay[32 * part:32 * part + HEADS, :]
                if part < 2:
                    chain.link(nc.vector.tensor_copy(r, c_))
                    chain.link(nc.vector.tensor_copy(x, r))
                    chain.link(nc.vector.tensor_tensor(c_, c_, x, ALU.subtract))
                else:
                    nc.vector.tensor_copy(r, c_).then_inc(decay_ready, 1)
            for x_, s in enumerate((k_sq, q_sq)):
                dve.wait_ge(qk_squared, x_ + 1)
                nc.vector.tensor_reduce(qk_ss[:, x_, :], s.rearrange("p (g d) -> p g d", d=DH),
                                        AX.X, ALU.add).then_inc(qk_summed, 1)
            dve.wait_ge(qk_root, 1)
            chain.link(nc.vector.reciprocal(qk_ss[:, :, :], qk_ss[:, :, :]))
            for x_, z in enumerate((zk, zq)):
                v = z[:, :, :].rearrange("p t (g d) -> p (t g) d", d=DH)
                nc.vector.tensor_tensor(v, v, qk_ss[:, x_, :].unsqueeze(2).to_broadcast([P, 32, DH]),
                                        ALU.mult).then_inc(qk_normed, 1)
            for j in range(4):
                dve.wait_ge(qk_turned, j + 1)
                nc.vector.tensor_scalar(kT[:, j, :], PS[:, 4 + j, :], cols[:, FK:FK + 1], None,
                                        ALU.mult).then_inc(qk_copied, 1)
            for j in range(4):
                dve.wait_ge(qk_turned, 4 + j + 1)
                nc.vector.tensor_scalar(qT[0][0:DH, j, :], PS[0:DH, 4 + j, :], gq8[0:DH, :], None,
                                        ALU.mult).then_inc(qk_copied, 1)
                nc.vector.tensor_scalar(qT[1][DH:P, j, :], PS[DH:P, 4 + j, :], gq8[DH:P, :], None,
                                        ALU.mult).then_inc(qk_copied, 1)
            for t in range(NT):
                dve.wait_ge(z_copied, 3 * NT + t + 1)
                chain.link(nc.vector.bn_stats(stat6[:, t, :], zg[:, t, :]))
                ins = nc.vector.bn_aggr(stat2[:, t, :], stat6[:, t, :])
                if t == NT - 1:
                    ins.then_inc(g_stats, 1)
                else:
                    chain.link(ins)
            dve.wait_ge(g_root, 1)
            chain.link(nc.vector.reciprocal(lnr[:, :], lnr[:, :]))
            for t in range(NT):
                ins = nc.vector.tensor_scalar(zg[:, t, :], zg[:, t, :], stat2[:, t, 0:1],
                                              lnr[:, t:t + 1], ALU.subtract, ALU.mult)
                ins.then_inc(g_scaled, 1)
            att[0].dve(dve, chain, yb)
            for g in range(GMLP):
                dve.wait_ge(g_mixed, g + 2 - g % 2)
                u = zu[:, :, DH * g:DH * (g + 1)]
                nc.vector.scalar_tensor_tensor(
                    out=u, in0=PS[:, g // 2, 256 * (g % 2):256 * (g % 2 + 1)].rearrange(
                        "p (c d) -> p c d", c=NT),
                    scalar=cols[:, BS + g:BS + g + 1], in1=u, op0=ALU.add, op1=ALU.mult).then_inc(ya_done, 1)
            y_dve(dve, 0, (4, 6, 0, 2))
            out_dve(dve, 0)

        def even_pool(pool, chain):
            for x_, (z, s) in enumerate(((zk, k_sq), (zq, q_sq))):
                pool.wait_ge(z_copied, NT * (x_ + 1))
                v = z[:, :, :].rearrange("p t d -> p (t d)")
                nc.gpsimd.tensor_tensor(s, v, v, ALU.mult).then_inc(qk_squared, 1)
            pool.wait_ge(qk_squared, 2)
            nc.gpsimd.memset(qT[0][DH:P, :, :], 0.0).then_inc(q_padded, 1)
            pool.wait_ge(q_padded, 1)
            pool.wait_ge(qk_turned, 4)
            nc.gpsimd.memset(qT[1][0:DH, :, :], 0.0).then_inc(q_padded, 1)
            pool.wait_ge(q_padded, 2)
            pool.wait_ge(g_scaled, NT)
            for t in range(NT):
                chain.link(nc.gpsimd.tensor_tensor(zg[:, t, :], zg[:, t, :], lng[:, :], ALU.mult))
                ins = nc.gpsimd.tensor_tensor(zg[:, t, :], zg[:, t, :], lnb[:, :], ALU.add)
                if t == NT - 1:
                    ins.then_inc(g_normed, 1)
                else:
                    chain.step(ins)
            pool.wait_ge(ws_copied, 1)
            nc.gpsimd.affine_select(out=wsT[:, :, :], in_=wsT[:, :, :], pattern=[[0, HEADS], [1, P]],
                                    compare_op=ALU.is_ge, fill=0.0, base=0,
                                    channel_multiplier=-1).then_inc(ws_masked, 1)

        c_done = sem("c_done")
        c_sig = sem("c_sig")
        c_glu = sem("c_glu")
        c_conv = sem("c_conv")
        z1_done, z1_copied = sem("z1_done"), sem("z1_copied")
        s1_squared, s1_summed, s1_root, s1_ready = sem("s1_squared"), sem("s1_summed"), sem("s1_root"), sem("s1_ready")
        t1_turned, t1_half, t1_copied = sem("t1_turned"), sem("t1_half"), sem("t1_copied")
        m_done, m_sub, m_sq, v_done, v_root, v_inverse, c_scaled = sem("m_done"), sem("m_sub"), sem("m_sq"), sem("v_done"), sem("v_root"), sem("v_inverse"), sem("c_scaled")
        c_conv_pool = sem("c_conv_pool")
        tap_scaled, tap_added = sem("tap_scaled"), sem("tap_added")
        tap_summed = sem("tap_summed")

        POOL_TAPS = [k for k in range(TAPS) if k % 3]
        DVE_TAPS = [k for k in range(TAPS) if k % 3 == 0]
        AT_MEAN, AT_SUB, AT_SQUARE, AT_VAR, AT_ROOT, AT_SCALE = 21, 22, 23, 27, 28, 29

        def conv_pe(pe, j, g):
            n0 = first["odd_conv"]
            for c in range(KC):
                last = pe.matmul(PS[:, (2 * j + g) % 6, :],
                                 slot(n0 + 2 * g + c // 4, 4)[:, c % 4, P * j:P * (j + 1)],
                                 aT[:, c, :], start=(c == 0), stop=(c == KC - 1))
            last.then_inc(c_done, 1)

        def turn_qk_pe(pe):
            pe.wait_ge(z1_copied, 2 * NT)
            pe.wait_ge(s1_ready, 1)
            for j in range(5):
                if j >= 2:
                    pe.wait_ge(t1_copied, j - 1)
                    pe.wait_ge(t1_half, j - 1)
                for t in range(NT):
                    src = qp[:, t, P * j:P * (j + 1)] if j < 4 else kv[:, t, 0:P]
                    last = pe.transpose(PS[:, 6 + j % 2, P * t:P * (t + 1)], src, ident[:, :])
                last.then_inc(t1_turned, 1)

        def z1_bank(b, t):
            return (6 + NT * b + t) % 8

        def odd_pe(pe):
            wait_aT(pe, 3)
            for x in range(4):
                landed(pe, first["odd_conv"] + x)
            for j in range(3):
                for g in range(2):
                    conv_pe(pe, j, g)
            for b, (name, k, w) in enumerate((("odd_q", 2, HALF), ("odd_kv", 1, 256))):
                n0 = first[name]
                for x in range(k):
                    landed(pe, n0 + x)
                for t in range(NT):
                    if b or t == 2:
                        pe.wait_ge(c_glu, (1, 3)[b])
                    for c in range(KC):
                        rhs = slot(n0 + c // 4, 4)[:, c % 4, :] if k == 2 else slot(n0, KC)[:, c, :]
                        last = pe.matmul(PS[:, z1_bank(b, t), 0:w], aT[:, c, P * t:P * (t + 1)], rhs,
                                         start=(c == 0), stop=(c == KC - 1))
                    last.then_inc(z1_done, 1)
            pe.wait_ge(z1_copied, NT)
            conv_pe(pe, 3, 0)
            turn_qk_pe(pe)
            conv_pe(pe, 3, 1)
            pe.wait_ge(t1_copied, 5)
            pe.wait_ge(t1_half, 4)
            pe.wait_ge(q_padded, 4)
            pe.wait_ge(c_glu, 4)

            def between(u):
                if u == AT_MEAN:
                    pe.wait_ge(c_conv, 2)
                    pe.wait_ge(c_conv_pool, 1)
                    pe.wait_ge(tap_added, TAPS)
                    for j in range(4):
                        last = pe.matmul(PS[:, 7, :], mean_w[:, :], cacc[:, j, :], start=(j == 0), stop=(j == 3))
                    last.then_inc(m_done, 1)
                if u == AT_VAR:
                    for j in range(4):
                        pe.wait_ge(m_sq, j + 1)
                        last = pe.matmul(PS[:, 7, :], mean_w[:, :], cacc[:, j, :], start=(j == 0), stop=(j == 3))
                    last.then_inc(v_done, 1)
            att[1].pe(pe, between)
            pe.wait_ge(att[1].written, len(UNITS))
            for c in range(4):
                for t in range(NT):
                    last = pe.transpose(PS[:, c, P * t:P * (t + 1)], y1[:, t, P * c:P * (c + 1)], ident[:, :])
                last.then_inc(y_turned, 1)
            out_pe(pe, 1)

        def odd_act(act, chain):
            def sigmoid(j):
                act.wait_ge(c_done, 2 * j + 2)
                if j >= 2:
                    act.wait_ge(c_glu, j - 1)
                nc.scalar.activation(sgc[:, j % 2, :], PS[:, (2 * j + 1) % 6, :], ACT.Sigmoid).then_inc(c_sig, 1)

            def taps_out(j, ks):
                base = TAPS if j == 3 else 0
                for k in ks:
                    n = base + (POOL_TAPS.index(k) if j == 3 else k)
                    if n - base >= 2:
                        act.wait_ge(tap_added, n - 1)
                    nc.scalar.activation(tap_out[j][n % 2], cin[:, j, k:k + SEQ], ACT.Copy,
                                         scale=tapw[:, j, k:k + 1]).then_inc(tap_scaled, 1)

            sigmoid(0)
            sigmoid(1)
            sigmoid(2)
            act.wait_ge(c_glu, 3)
            for b, (dst, sq, n) in enumerate(((zq, sq1.rearrange("p (t d) -> p t d", t=NT), HALF),
                                              (kv, sq_k.rearrange("p (t d) -> p t d", t=NT), P))):
                for t in range(NT):
                    k0, k1 = (5 * t, 5 * t + 5) if b == 0 else (20 + 3 * t, min(23 + 3 * t, TAPS))
                    taps_out(2, range(k0, k1))
                    act.wait_ge(z1_done, NT * b + t + 1)
                    nc.scalar.activation(sq[:, t, :], PS[:, z1_bank(b, t), 0:n], ACT.Square).then_inc(s1_squared, 1)
                    nc.scalar.activation(dst[:, t, :], PS[:, z1_bank(b, t), 0:(HALF, 256)[b]],
                                         ACT.Copy).then_inc(z1_copied, 1)
                act.wait_ge(s1_summed, b + 1)
                ssum = qk_ss[:, b, 0:(32, 8)[b]]
                nc.scalar.activation(ssum, ssum, ACT.Sqrt, bias=eps[:, :], scale=1.0 / DH).then_inc(s1_root, 1)
            act.wait_ge(tap_added, TAPS)
            for j in range(5):
                act.wait_ge(t1_turned, j + 1)
                if j < 4:
                    for b in range(2):
                        half = slice(DH * b, DH * (b + 1))
                        ins = nc.scalar.activation(qT1[b][half, j, :], PS[half, 6 + j % 2, :], ACT.Copy,
                                                   scale=DH ** -0.5)
                        ins.then_inc((t1_half, t1_copied)[b], 1)
                else:
                    nc.scalar.activation(kT1, PS[:, 6 + j % 2, :], ACT.Copy).then_inc(t1_copied, 1)
            sigmoid(3)
            act.wait_ge(c_glu, 4)

            def between(u):
                if u < len(POOL_TAPS):
                    taps_out(3, POOL_TAPS[u:u + 1])
                if 0 <= u - AT_SQUARE < 4:
                    j = u - AT_SQUARE
                    act.wait_ge(m_sub, j + 1)
                    nc.scalar.activation(cacc[:, j, :], cd[:, j, :], ACT.Square).then_inc(m_sq, 1)
                if u == AT_ROOT:
                    act.wait_ge(v_done, 1)
                    nc.scalar.activation(sgc[:, 0, :], PS[:, 7, :], ACT.Sqrt, bias=eps[:, :]).then_inc(v_root, 1)
            att[1].act(act, between)
            for j in range(4):
                act.wait_ge(c_scaled, j + 1)
                nc.scalar.activation(yT[:, 4 + j, :], cd[:, j, :], ACT.Silu, bias=cols[:, CLB + j:CLB + j + 1],
                                     scale=cols[:, CLG + j:CLG + j + 1]).then_inc(yT_act, 1)
            y_act(act, 1, (1, 3))

        def taps(engine, chain, j, sums, ks):
            for n, k in enumerate(ks):
                acc, src, w = sums[n % 2], cin[:, j, k:k + SEQ], tapw[:, j, k:k + 1]
                if n < 2:
                    chain.step(engine.tensor_scalar(acc, src, w, None, ALU.mult))
                else:
                    chain.wait(behind=1)
                    chain.step(engine.scalar_tensor_tensor(out=acc, in0=src, scalar=w, in1=acc,
                                                           op0=ALU.mult, op1=ALU.add))
            chain.wait()
            return engine.tensor_tensor(sums[0], sums[0], sums[1], ALU.add)

        def odd_dve(dve, chain):
            chain.link(nc.vector.memset(cin[:, :, 0:TAPS - 1], 0.0))

            def qk_norm(x_, heads, z, sq):
                for t in range(NT):
                    dve.wait_ge(s1_squared, NT * x_ + t + 1)
                    ins = nc.vector.tensor_reduce(qk_ss[:, x_, heads * t:heads * (t + 1)],
                                                  sq.rearrange("p (t g d) -> p t g d", t=NT, d=DH)[:, t],
                                                  AX.X, ALU.add)
                    if t == NT - 1:
                        ins.then_inc(s1_summed, 1)
                    else:
                        chain.step(ins)
                dve.wait_ge(s1_root, x_ + 1)
                inv = qk_ss[:, x_, 0:heads * NT]
                chain.link(nc.vector.reciprocal(inv, inv))
                dve.wait_ge(z1_copied, NT * (x_ + 1))
                for t in range(NT):
                    v = z[:, t].rearrange("p (g d) -> p g d", d=DH)
                    r = qk_ss[:, x_, heads * t:heads * (t + 1)].unsqueeze(2).to_broadcast([P, heads, DH])
                    chain.link(nc.vector.tensor_tensor(v, v, r, ALU.mult))
                    g = gq1[:, x_, :].unsqueeze(1).to_broadcast([P, heads, DH])
                    if x_:
                        chain.link(nc.vector.tensor_tensor(v, v, g, ALU.mult))
                    else:
                        w = qp[:, t, :]
                        chain.link(nc.vector.tensor_tensor(
                            w.rearrange("p (j f d) -> p f j d", f=2, j=4), v.rearrange("p (f j) d -> p f j d", f=2),
                            gq1[:, 0, :].unsqueeze(1).unsqueeze(1).to_broadcast([P, 2, 4, DH]), ALU.mult))
                        v = w.rearrange("p (g d) -> p g d", d=DH)
                    x1, x2 = v[:, :, 0:8], v[:, :, 8:16]
                    cos = rope[:, 0, t, :].unsqueeze(1).to_broadcast([P, heads, 8])
                    sin = rope[:, 1, t, :].unsqueeze(1).to_broadcast([P, heads, 8])
                    tm = [junk_r[:, 64 * i_:64 * i_ + 8 * heads].rearrange("p (g d) -> p g d", d=8) for i_ in range(4)]
                    chain.step(nc.vector.tensor_tensor(tm[0], x1, cos, ALU.mult))
                    chain.step(nc.vector.tensor_tensor(tm[1], x2, sin, ALU.mult))
                    chain.step(nc.vector.tensor_tensor(tm[2], x2, cos, ALU.mult))
                    chain.link(nc.vector.tensor_tensor(tm[3], x1, sin, ALU.mult))
                    chain.step(nc.vector.tensor_tensor(x1, tm[0], tm[1], ALU.subtract))
                    ins = nc.vector.tensor_tensor(x2, tm[2], tm[3], ALU.add)
                    if x_ == 1 and t == NT - 1:
                        ins.then_inc(s1_ready, 1)
                    else:
                        chain.link(ins)

            def glu(j):
                dve.wait_ge(c_sig, j + 1)
                nc.vector.tensor_tensor(cin[:, j, TAPS - 1:TAPS - 1 + SEQ], PS[:, (2 * j) % 6, :],
                                        sgc[:, j % 2, :], ALU.mult).then_inc(c_glu, 1)

            glu(0)
            dve.wait_ge(c_glu, 1)
            taps(nc.vector, chain, 0, (cacc[:, 0, :], cacc2), range(TAPS)).then_inc(c_conv, 1)
            glu(1)
            dve.wait_ge(c_glu, 2)
            glu(2)
            dve.wait_ge(c_conv, 1)
            taps(nc.vector, chain, 1, (cacc[:, 1, :], cacc2), range(TAPS)).then_inc(c_conv, 1)
            qk_norm(0, 8, zq[:, :, :], sq1)
            qk_norm(1, 2, kv[:, :, 0:P], sq_k)
            glu(3)
            dve.wait_ge(c_glu, 4)

            def between(u):
                if u < len(DVE_TAPS):
                    k = DVE_TAPS[u]
                    acc, src, w = cacc[:, 3, :], cin[:, 3, k:k + SEQ], tapw[:, 3, k:k + 1]
                    if u == 0:
                        ins = nc.vector.tensor_scalar(acc, src, w, None, ALU.mult)
                    else:
                        dve.wait_ge(tap_summed, u)
                        ins = nc.vector.scalar_tensor_tensor(out=acc, in0=src, scalar=w, in1=acc,
                                                             op0=ALU.mult, op1=ALU.add)
                    ins.then_inc(tap_summed, 1)
                if 0 <= u - AT_SUB < 4:
                    j = u - AT_SUB
                    dve.wait_ge(m_done, 1)
                    nc.vector.tensor_tensor(cd[:, j, :], cacc[:, j, :], PS[:, 7, :], ALU.subtract).then_inc(m_sub, 1)
                if u == AT_SCALE:
                    dve.wait_ge(v_root, 1)
                    nc.vector.reciprocal(sgc[:, 1, :], sgc[:, 0, :]).then_inc(v_inverse, 1)
            att[1].dve(dve, chain, y1, between)
            y_dve(dve, 1, (0, 2))
            out_dve(dve, 1)

        def odd_pool(pool, chain):
            def add_taps(j, acc, n0, n1):
                for n in range(n0, n1):
                    pool.wait_ge(tap_scaled, n + 1)
                    if n == n0:
                        ins = nc.gpsimd.tensor_copy(acc, tap_out[j][n % 2])
                    else:
                        pool.wait_ge(tap_added, n)
                        ins = nc.gpsimd.tensor_tensor(acc, acc, tap_out[j][n % 2], ALU.add)
                    ins.then_inc(tap_added, 1)

            add_taps(2, cacc[:, 2, :], 0, TAPS)
            pool.wait_ge(tap_added, TAPS)
            pool.wait_ge(s1_ready, 1)
            nc.gpsimd.memset(qT1[0][DH:P, :, :], 0.0).then_inc(q_padded, 1)
            pool.wait_ge(q_padded, 3)
            nc.gpsimd.memset(qT1[1][0:DH, :, :], 0.0).then_inc(q_padded, 1)
            pool.wait_ge(q_padded, 4)
            pool.wait_ge(c_conv, 2)
            add_taps(3, cacc2, TAPS, TAPS + len(POOL_TAPS))
            pool.wait_ge(tap_added, TAPS + len(POOL_TAPS))
            pool.wait_ge(tap_summed, len(DVE_TAPS))
            block3 = cacc[:, 3, :]
            nc.gpsimd.tensor_tensor(block3, block3, cacc2, ALU.add).then_inc(c_conv_pool, 1)
            pool.wait_ge(m_sub, 4)
            pool.wait_ge(m_sq, 4)
            pool.wait_ge(v_inverse, 1)
            for j in range(4):
                nc.gpsimd.tensor_tensor(cd[:, j, :], cd[:, j, :], sgc[:, 1, :], ALU.mult).then_inc(c_scaled, 1)

        logits_done = sem("logits_done")
        r_exp, r_exped = sem("r_exp"), sem("r_exped")
        chosen, ranked = sem("chosen"), sem("ranked")
        most_ready = sem("most_ready")
        pos_ready = sem("pos_ready")
        sel_ready, gathered, xT_ready = sem("sel_ready"), sem("gathered"), sem("xT_ready")
        gateup, silu_ready, hid_ready = sem("gateup"), sem("silu_ready"), sem("hid_ready")
        hid_turned, hidT_ready = sem("hid_turned"), sem("hidT_ready")
        down_lo, down_hi, y_lo, y_hi = sem("down_lo"), sem("down_hi"), sem("y_lo"), sem("y_hi")
        y_stored = [sem("y_stored0"), sem("y_stored1")]
        row_loaded = [sem(f"row_loaded{b}") for b in range(NT)]
        row_used = sem("row_used")

        o = 0
        def rt(n):
            nonlocal o
            o += n
            return rtmp[:, o - n:o]
        logit = rt(NT * 36).rearrange("p (t e) -> p t e", t=NT)
        cpad = rt(NT * 8).rearrange("p (t e) -> p t e", t=NT)
        top_c = rt(NT * 8).rearrange("p (t e) -> p t e", t=NT)
        idx_c = rt(NT * 8).rearrange("p (t e) -> p t e", t=NT).bitcast(U32)
        gid = rt(NT)
        goh = rt(NT * GROUPS).rearrange("p (t g) -> p t g", t=NT)
        fprod = rt(NT * 32).rearrange("p (t g e) -> p t g e", t=NT, g=GROUPS)
        fsel = rt(NT * 8).rearrange("p (t e) -> p t e", t=NT)
        top_f = rt(NT * 8).rearrange("p (t e) -> p t e", t=NT)
        idx_f = rt(NT * 8).rearrange("p (t e) -> p t e", t=NT).bitcast(U32)
        eid = rt(NT * 2).rearrange("p (t k) -> p t k", t=NT)
        cexp = rt(NT * GROUPS).rearrange("p (t g) -> p t g", t=NT)
        psum_ = rt(NT)
        e2 = rt(NT)
        one1 = rt(NT * 32).rearrange("p (t e) -> p t e", t=NT)
        one2 = rt(NT * 32).rearrange("p (t e) -> p t e", t=NT)
        both = rt(NT * 32).rearrange("p (t e) -> p t e", t=NT)
        rank = rt(NT * 32).rearrange("p (t e) -> p t e", t=NT)
        prod = rt(NT * 32).rearrange("p (t e) -> p t e", t=NT)
        rk = rt(NT * 2).rearrange("p (t k) -> p t k", t=NT)
        over = rt(NT * 2 * (ROUNDS - 1)).rearrange("p (t j) -> p t j", j=ROUNDS - 1)
        mostf = rt(1)

        lT = hid_area
        lT_ready, logits_turned = sem("lT_ready"), sem("logits_turned")

        def router_pe(pe, l):
            u = 3 * l + 1
            wait_aT(pe, u)
            for c in range(KC // 2):
                for b in range(2):
                    last = pe.matmul(PS[CAP * b:CAP * b + 36, 0, :], wr[:, l, 4 * b + c, :], aT[:, 4 * b + c, :],
                                     start=(c == 0), stop=(c == KC // 2 - 1))
            last.then_inc(logits_done, 1)
            embed_pe(pe, l)
            pe.wait_ge(lT_ready, 2 * (l + 1))
            for b in range(2):
                for t in range(NT):
                    last = pe.transpose(PS[:, 4 + b, 36 * t:36 * (t + 1)],
                                        lT[CAP * b:CAP * b + 36, P * t:P * (t + 1)],
                                        ident[CAP * b:CAP * b + 36, CAP * b:CAP * b + 36])
            last.then_inc(logits_turned, 1)
            pe.wait_ge(chosen, l + 1)
            for t in range(NT + 1):
                for s in range(min(t + 1, NT)):
                    last = pe.matmul(PS[:, 1, 32 * t:32 * (t + 1)], (upper if s == t else ones)[:, :],
                                     both[:, s, :], start=(s == 0), stop=(s == min(t, NT - 1)))
            last.then_inc(ranked, 1)

        def router_dve(dve, chain, l):
            v = nc.vector
            chain.link(v.memset(cpad[:, :, :], NEG * 1e8))
            dve.wait_ge(logits_done, l + 1)
            for b in range(2):
                v.tensor_copy(lT[CAP * b:CAP * b + 36, :], PS[CAP * b:CAP * b + 36, 0, :]).then_inc(lT_ready, 1)
            dve.wait_ge(logits_turned, l + 1)
            lg = [PS[:, 4 + b, 0:36 * NT].rearrange("p (t e) -> p t e", t=NT) for b in range(2)]
            chain.link(v.tensor_tensor(logit, lg[0], rbias[:, l, :].unsqueeze(1).to_broadcast([P, NT, 36]), ALU.add))
            chain.link(v.tensor_tensor(logit, logit, lg[1], ALU.add))
            chain.link(v.tensor_copy(cpad[:, :, 0:GROUPS], logit[:, :, 0:GROUPS]))
            for t in range(NT):
                chain.step(v.max(top_c[:, t, :], cpad[:, t, :]))
            chain.wait()
            for t in range(NT):
                chain.step(v.max_index(idx_c[:, t, :], top_c[:, t, :], cpad[:, t, :]))
            chain.wait()
            chain.link(v.tensor_copy(gid, idx_c[:, :, 0]))
            chain.link(v.tensor_tensor(goh, iota[:, 0:GROUPS].unsqueeze(1).to_broadcast([P, NT, GROUPS]),
                                       gid.unsqueeze(2).to_broadcast([P, NT, GROUPS]), ALU.is_equal))
            chain.link(v.tensor_tensor(fprod, logit[:, :, GROUPS:36].rearrange("p t (g e) -> p t g e", g=GROUPS),
                                       goh.unsqueeze(3).to_broadcast([P, NT, GROUPS, PER_GROUP]), ALU.mult))
            chain.link(v.tensor_reduce(fsel, fprod.rearrange("p t g e -> p t e g"), AX.X, ALU.add))
            for t in range(NT):
                chain.step(v.max(top_f[:, t, :], fsel[:, t, :]))
            chain.wait()
            for t in range(NT):
                chain.step(v.max_index(idx_f[:, t, :], top_f[:, t, :], fsel[:, t, :]))
            chain.wait()
            chain.link(v.tensor_copy(eid, idx_f[:, :, 0:2]))
            chain.link(v.scalar_tensor_tensor(out=eid, in0=gid.unsqueeze(2).to_broadcast([P, NT, 2]),
                                              scalar=float(PER_GROUP), in1=eid, op0=ALU.mult, op1=ALU.add))
            ids = iota[:, 0:32].unsqueeze(1).to_broadcast([P, NT, 32])
            for k, one in enumerate((one1, one2)):
                chain.step(v.tensor_tensor(one, ids, eid[:, :, k:k + 1].to_broadcast([P, NT, 32]), ALU.is_equal))
            chain.wait()
            v.tensor_tensor(both, one1, one2, ALU.add).then_inc(chosen, 1)
            ple_dve(dve, l, True)
            chain.step(v.tensor_tensor(cexp, logit[:, :, 0:GROUPS], top_c[:, :, 0:1].to_broadcast([P, NT, GROUPS]),
                                       ALU.subtract))
            chain.link(v.tensor_tensor(e2, top_f[:, :, 1], top_f[:, :, 0], ALU.subtract))
            dve.sem_inc(r_exp, 1)
            dve.wait_ge(ranked, l + 1)
            chain.link(v.tensor_copy(rank, PS[:, 1, 0:NT * 32].rearrange("p (t e) -> p t e", t=NT)))
            chain.link(v.scalar_tensor_tensor(out=prod, in0=rank, scalar=1.0, in1=both, op0=ALU.add, op1=ALU.mult))
            chain.link(v.tensor_scalar(rsel[:, :, :], prod, -1.0, None, ALU.add))

        def router_tail_dve(dve, chain, l):
            v = nc.vector
            chain.link(v.tensor_reduce(mostf, PS[:, 1, NT * 32:NT * 32 + 32], AX.X, ALU.max))
            v.tensor_copy(most[:, :], mostf).then_inc(most_ready, 1)
            dve.wait_ge(r_exped, l + 1)
            chain.link(v.tensor_reduce(psum_, cexp, AX.X, ALU.add))
            chain.link(v.tensor_scalar(prob[:, :, 1], e2, 1.0, None, ALU.add))
            chain.link(v.tensor_tensor(psum_, psum_, prob[:, :, 1], ALU.mult))
            chain.link(v.reciprocal(prob[:, :, 0], psum_))
            chain.link(v.tensor_tensor(prob[:, :, 1], prob[:, :, 0], e2, ALU.mult))
            for k, one in enumerate((one1, one2)):
                chain.link(v.tensor_tensor(prod, one, rank, ALU.mult))
                chain.link(v.tensor_reduce(rk[:, :, k], prod, AX.X, ALU.add))
            flat = rk.rearrange("p t k -> p (t k)")
            chain.link(v.tensor_tensor(over, flat.unsqueeze(2).to_broadcast([P, 2 * NT, ROUNDS - 1]),
                                       steps64[:, :].unsqueeze(1).to_broadcast([P, 2 * NT, ROUNDS - 1]), ALU.is_ge))
            chain.link(v.scalar_tensor_tensor(out=rk, in0=eid, scalar=float(CAP), in1=rk, op0=ALU.mult, op1=ALU.add))
            rnd = prod[:, 0, 0:2 * NT]
            chain.link(v.tensor_reduce(rnd, over, AX.X, ALU.add))
            chain.link(v.scalar_tensor_tensor(out=flat, in0=rnd, scalar=float(EXPERTS * CAP - CAP), in1=flat,
                                              op0=ALU.mult, op1=ALU.add))
            v.tensor_copy(posn[:, :, :], rk).then_inc(pos_ready, 1)

        def router_act(act, chain, l):
            act.wait_ge(r_exp, l + 1)
            chain.link(nc.scalar.activation(cexp, cexp, ACT.Exp))
            nc.scalar.activation(e2, e2, ACT.Exp).then_inc(r_exped, 1)

        def pair_items(l, q):
            return [first[f"moe{l}"] + 6 * q + x for x in range(6)]

        def gather_pe(pe, l, it, q):
            g = PAIRS * l + 2 * it + q
            pe.wait_ge(sel_ready, NT * (g + 1))
            if not isinstance(it, int) or g >= 1:
                pe.wait_ge(xT_ready, g)
            gather_half(pe, q, 0)

        def gather_half(pe, q, b):
            for c in range(4 * b, 4 * b + 4):
                for t in range(NT):
                    last = pe.matmul(PS[:, 2 + b, P * (c % 4):P * (c % 4 + 1)],
                                     xn[:, t, P * c:P * (c + 1)], sel[:, q, t, :],
                                     start=(t == 0), stop=(t == NT - 1))
            last.then_inc((gather_lo, gathered)[b], 1)

        def pair_pe(pe, l, it, q, more):
            g = PAIRS * l + 2 * it + q
            ns = pair_items(l, q)
            pe.wait_ge(xT_ready, g + 1)
            if isinstance(it, int) and 2 * it + q == 0:
                pe.wait_ge(p_copied, 2 * (l + 1))
            if not isinstance(it, int) or g >= 1:
                pe.wait_ge(hid_ready, g)
            for part in range(2):
                for e in range(2):
                    n = ns[3 * e + part]
                    pe.wait_ge(slot_loaded[n % SLOTS], 16 * (n // SLOTS + 1) + 16 * it)
                for c in range(KC):
                    for e in range(2):
                        last = pe.matmul(PS[CAP * e:CAP * (e + 1), 4, FE * part:FE * (part + 1)],
                                         xT[:, q, c, CAP * e:CAP * (e + 1)],
                                         slot(ns[3 * e + part], KC)[:, c, :],
                                         start=(c == 0), stop=(c == KC - 1))
            last.then_inc(gateup, 1)
            if more:
                gather_pe(pe, l, it + q, 1 - q)
            pe.wait_ge(hid_ready, g + 1)
            if not isinstance(it, int) or g >= 1:
                pe.wait_ge(hidT_ready, g)
            for f in range(2):
                last = pe.transpose(PS[:, 5, P * f:P * (f + 1)], hid[:, q, P * f:P * (f + 1)], ident[:, :])
            last.then_inc(hid_turned, 1)
            if more:
                gather_half(pe, 1 - q, 1)
            pe.wait_ge(hidT_ready, g + 1)
            for e in range(2):
                n = ns[3 * e + 2]
                pe.wait_ge(slot_loaded[n % SLOTS], 16 * (n // SLOTS + 1) + 16 * it)
            for n in range(2):
                if not isinstance(it, int) or g >= 1:
                    pe.wait_ge((y_lo, y_hi)[n], g)
                for f in range(2):
                    for e in range(2):
                        last = pe.matmul(PS[CAP * e:CAP * (e + 1), 6 + n, :],
                                         hidT[:, q, f, CAP * e:CAP * (e + 1)],
                                         slot(ns[3 * e + 2], 2)[:, f, HALF * n:HALF * (n + 1)],
                                         start=(f == 0), stop=(f == 1))
                last.then_inc((down_lo, down_hi)[n], 1)

        def sel_dve(l, it, q, dve):
            g = PAIRS * l + 2 * it + q
            if not isinstance(it, int) or g >= 2:
                dve.wait_ge(gathered, g - 1)
            for t in range(NT):
                r = rsel[:, t, bass.ds(4 * it + 2 * q, 2)]
                ins = nc.vector.tensor_tensor(sel[:, q, t, :].rearrange("p (e s) -> p e s", e=2),
                                              iota[:, :].unsqueeze(1).to_broadcast([P, 2, CAP]),
                                              r.unsqueeze(2).to_broadcast([P, 2, CAP]), ALU.is_equal)
                ins.then_inc(sel_ready, 1)

        xT_lo, gather_lo = sem("xT_lo"), sem("gather_lo")

        def copy_xT(l, it, q, b, dve):
            g = PAIRS * l + 2 * it + q
            dve.wait_ge((gather_lo, gathered)[b], g + 1)
            base = FFN + KC * l
            nc.vector.tensor_tensor(
                xT[:, q, 4 * b:4 * (b + 1), :], PS[:, 2 + b, :].rearrange("p (c s) -> p c s", c=4),
                cols[:, base + 4 * b:base + 4 * (b + 1)].unsqueeze(2).to_broadcast([P, 4, P]),
                ALU.mult).then_inc((xT_lo, xT_ready)[b], 1)

        def pair_dve(dve, l, it, q, more, more_sel):
            g = PAIRS * l + 2 * it + q
            dve.wait_ge(silu_ready, g + 1)
            nc.vector.tensor_tensor(hid[:, q, :], sgate[:, q, :], PS[:, 4, FE:2 * FE],
                                    ALU.mult).then_inc(hid_ready, 1)
            if more:
                copy_xT(l, it + q, 1 - q, 0, dve)
            dve.wait_ge(hid_turned, g + 1)
            nc.vector.tensor_copy(hidT[:, q, :, :], PS[:, 5, 0:2 * P].rearrange("p (f s) -> p f s", f=2)).then_inc(hidT_ready, 1)
            if more:
                copy_xT(l, it + q, 1 - q, 1, dve)
            if more_sel:
                sel_dve(l, it + 1, q, dve)
            dve.wait_ge(down_hi, g + 1)
            if not isinstance(it, int) or g >= 2:
                dve.wait_ge(y_stored[q], 16 * (PAIRS // 2 * l + it))
            nc.vector.tensor_copy(ysb[:, q, HALF:D], PS[:, 7, :]).then_inc(y_hi, 1)

        def pair_act(act, l, it, q):
            g = PAIRS * l + 2 * it + q
            act.wait_ge(gateup, g + 1)
            if not isinstance(it, int) or g >= 2:
                act.wait_ge(hid_ready, g - 1)
            nc.scalar.activation(sgate[:, q, :], PS[:, 4, 0:FE], ACT.Silu).then_inc(silu_ready, 1)
            act.wait_ge(down_lo, g + 1)
            if not isinstance(it, int) or g >= 2:
                act.wait_ge(y_stored[q], 16 * (PAIRS // 2 * l + it))
            nc.scalar.activation(ysb[:, q, 0:HALF], PS[:, 6, :], ACT.Copy).then_inc(y_lo, 1)
            act.wait_ge(y_lo, g + 1)
            act.wait_ge(y_hi, g + 1)
            act.dma_start(table.rearrange("(r s) d -> r s d", s=P)[bass.ds(2 * it + q, 1)].rearrange("r s d -> (r s) d"),
                          ysb[:, q, :]).then_inc(y_stored[q], 16)

        STEPS = PAIRS // 2
        cold = [{n: sem(f"over{l}_{n}") for n in ("loaded", "used", "shifted", "pe", "dve", "act", "stored")}
                for l in range(DEPTH)]
        OVER_PE = ("gathered", "gateup", "turned", "down")
        OVER_DVE = ("sel0", "sel1", "sel2", "sel3", "xT", "hid", "hidT", "y_hi")
        OVER_ACT = ("silu", "y_lo")

        def over_wait(eng, l, u, what):
            for name, steps in (("pe", OVER_PE), ("dve", OVER_DVE), ("act", OVER_ACT)):
                if what in steps:
                    eng.wait_ge(cold[l][name], u * len(steps) + (steps.index(what) + 1))

        def overflow(eng, l, body, before_round=None):
            n = eng.value_load(most[0:1, 0:1], min_val=0, max_val=SEQ)
            with eng.If(n > CAP):
                for q in range(2):
                    eng.wait_ge(y_stored[q], 16 * STEPS * (l + 1))
                with eng.Fori(0, ROUNDS - 1) as r:
                    if before_round:
                        before_round(r)
                    with eng.Fori(0, EXPERTS) as e:
                        body(r * EXPERTS + e, r, e)
                overflow_end(eng, l)
            eng.end_ifs()

        UNITS_OVER = (ROUNDS - 1) * EXPERTS

        def overflow_end(eng, l):
            eng.wait_ge(cold[l]["stored"], 16 * UNITS_OVER)

        def over_sp(sp, l):
            s = cold[l]
            sp.wait_ge(most_ready, l + 1)

            def body(u, r, e):
                sp.wait_ge(s["used"], u + 1)
                sp.dma_start(cold_gate.rearrange("p (c f) -> p c f", c=KC),
                             a["moe_w_gate"][l, bass.ds(e, 1)].rearrange("e (c p) f -> p (e c) f", p=P)).then_inc(s["loaded"], 16)
                sp.dma_start(cold_up.rearrange("p (c f) -> p c f", c=KC),
                             a["moe_w_up"][l, bass.ds(e, 1)].rearrange("e (c p) f -> p (e c) f", p=P)).then_inc(s["loaded"], 16)
                for f in range(2):
                    sp.dma_start(cold_down[f], a["moe_w_down"][l, bass.ds(e, 1), P * f:P * (f + 1), :].rearrange(
                        "e p f -> (e p) f")).then_inc(s["loaded"], 16)
            overflow(sp, l, body)

        def over_dve(dve, l, chain):
            s = cold[l]

            def shift(r):
                nc.vector.tensor_scalar(rsel[:, :, :], rsel[:, :, :], -float(CAP), None, ALU.add).then_inc(s["shifted"], 1)

            def body(u, r, e):
                dve.wait_ge(s["shifted"], r + 1)
                for t in range(NT):
                    nc.vector.tensor_tensor(sel[:, 0, t, 0:CAP], iota[:, :],
                                            rsel[:, t, bass.ds(e, 1)].to_broadcast([P, CAP]),
                                            ALU.is_equal).then_inc(s["dve"], 1)
                over_wait(dve, l, u, "gathered")
                nc.vector.tensor_tensor(
                    xT[:, 0, :, 0:CAP], PS[:, 2, :].rearrange("p (c s) -> p c s", c=KC),
                    cols[:, FFN + KC * l:FFN + KC * (l + 1)].unsqueeze(2).to_broadcast([P, KC, CAP]),
                    ALU.mult).then_inc(s["dve"], 1)
                over_wait(dve, l, u, "silu")
                nc.vector.tensor_tensor(hid[0:CAP, 0, :], sgate[0:CAP, 0, :], PS[0:CAP, 4, FE:2 * FE],
                                        ALU.mult).then_inc(s["dve"], 1)
                over_wait(dve, l, u, "turned")
                nc.vector.tensor_copy(hidT[:, 0, :, :], PS[:, 5, 0:2 * P].rearrange("p (f s) -> p f s", f=2)).then_inc(s["dve"], 1)
                over_wait(dve, l, u, "down")
                nc.vector.tensor_copy(ysb[0:CAP, 0, HALF:D], PS[0:CAP, 7, :]).then_inc(s["dve"], 1)
                dve.wait_ge(s["stored"], 16 * u + 16)
                dve.sem_inc(s["used"], 1)
            dve.wait_ge(sel_ready, NT * PAIRS * (l + 1))
            dve.wait_ge(y_hi, PAIRS * (l + 1))
            dve.sem_inc(s["used"], 1)
            overflow(dve, l, body, shift)

        def over_act(act, l):
            s = cold[l]

            def body(u, r, e):
                over_wait(act, l, u, "gateup")
                nc.scalar.activation(sgate[0:CAP, 0, :], PS[0:CAP, 4, 0:FE], ACT.Silu).then_inc(s["act"], 1)
                over_wait(act, l, u, "down")
                nc.scalar.activation(ysb[0:CAP, 0, 0:HALF], PS[0:CAP, 6, :], ACT.Copy).then_inc(s["act"], 1)
                over_wait(act, l, u, "y_lo")
                over_wait(act, l, u, "y_hi")
                act.dma_start(table.rearrange("(n s) d -> n s d", s=CAP)[bass.ds(u + EXPERTS, 1)].rearrange("n s d -> (n s) d"),
                              ysb[0:CAP, 0, :]).then_inc(s["stored"], 16)
                act.wait_ge(s["stored"], 16 * u + 16)
            overflow(act, l, body)

        def over_pe(pe, l):
            s = cold[l]

            def body(u, r, e):
                over_wait(pe, l, u, "sel3")
                for c in range(KC):
                    for t in range(NT):
                        last = pe.matmul(PS[:, 2, CAP * c:CAP * (c + 1)], xn[:, t, P * c:P * (c + 1)],
                                         sel[:, 0, t, 0:CAP], start=(t == 0), stop=(t == NT - 1))
                last.then_inc(s["pe"], 1)
                over_wait(pe, l, u, "xT")
                pe.wait_ge(s["loaded"], 64 * u + 64)
                for part, w in enumerate((cold_gate, cold_up)):
                    for c in range(KC):
                        last = pe.matmul(PS[0:CAP, 4, FE * part:FE * (part + 1)], xT[:, 0, c, 0:CAP],
                                         w.rearrange("p (c f) -> p c f", c=KC)[:, c, :],
                                         start=(c == 0), stop=(c == KC - 1))
                last.then_inc(s["pe"], 1)
                over_wait(pe, l, u, "hid")
                for f in range(2):
                    last = pe.transpose(PS[:, 5, P * f:P * (f + 1)], hid[:, 0, P * f:P * (f + 1)], ident[:, :])
                last.then_inc(s["pe"], 1)
                over_wait(pe, l, u, "hidT")
                for n in range(2):
                    for f in range(2):
                        last = pe.matmul(PS[0:CAP, 6 + n, :], hidT[:, 0, f, 0:CAP],
                                         cold_down[f][:, HALF * n:HALF * (n + 1)],
                                         start=(f == 0), stop=(f == 1))
                last.then_inc(s["pe"], 1)
            overflow(pe, l, body)

        def combine_pool(pool, l):
            pool.wait_ge(most_ready, l + 1)
            pool.wait_ge(pos_ready, l + 1)
            for q in range(2):
                pool.wait_ge(y_stored[q], 16 * STEPS * (l + 1))
            n = pool.value_load(most[0:1, 0:1], min_val=0, max_val=SEQ)

            def gathers(rows_of):
                for m in range(2 * NT):
                    t, k = m // 2, m % 2
                    if m >= NT:
                        pool.wait_ge(*row_added(l, m - NT))
                    nc.gpsimd.indirect_dma_start(
                        out=gath[:, m % NT, :], out_offset=None, in_=rows_of,
                        in_offset=bass.IndirectOffsetOnAxis(ap=posn[:, t, k:k + 1], axis=0)
                    ).then_inc(row_loaded[m % NT], 16)

            with pool.If(n > CAP):
                overflow_end(pool, l)
                gathers(table)
            with pool.Else():
                gathers(table[0:EXPERTS * CAP])
            pool.end_ifs()

        def row_added(l, m):
            t, k = m // 2, m % 2
            return (h_ready, NT * (3 * l + 1) + t + 1) if k else (row_used, NT * l + t + 1)

        def combine_dve(dve, l):
            for m in range(2 * NT):
                t, k = m // 2, m % 2
                dve.wait_ge(row_loaded[m % NT], 16 * (2 * l + m // NT + 1))
                if k:
                    dve.wait_ge(*row_added(l, m - 1))
                nc.vector.scalar_tensor_tensor(out=h[:, t, :], in0=gath[:, m % NT, :], scalar=prob[:, t, k:k + 1],
                                               in1=h[:, t, :], op0=ALU.mult, op1=ALU.add
                                               ).then_inc(row_added(l, m)[0], 1)

        p_loaded, p_turned, p_copied = sem("p_loaded"), sem("p_turned"), sem("p_copied")
        gate_done, emb_done, emb_copied = sem("gate_done"), sem("emb_done"), sem("emb_copied")
        sig_ready, gated = sem("sig_ready"), sem("gated")

        def embed_pe(pe, l):
            pe.wait_ge(p_loaded, 16 * (l + 1))
            for k in range(2):
                for t in range(NT):
                    last = pe.transpose(PS[:, 6 + k, P * t:P * (t + 1)], psb[:, t, P * k:P * (k + 1)], ident[:, :])
            last.then_inc(p_turned, 1)

        def added(l, m):
            t, n = m // 2, m % 2
            return (h_ready, NT * (3 * l + 2) + t + 1) if n else (gated, NT * l + t + 1)

        def project_pe(pe, l):
            np_ = first[f"pproj{l}"]
            landed(pe, np_)
            for m in range(2 * NT):
                t, n = m // 2, m % 2
                if m >= 4:
                    pe.wait_ge(emb_copied, 8 * l + m - 3)
                for k in range(2):
                    last = pe.matmul(PS[:, m % 4, :], pT[:, k, P * t:P * (t + 1)],
                                     slot(np_, 2)[:, k, HALF * n:HALF * (n + 1)],
                                     start=(k == 0), stop=(k == 1))
                last.then_inc(emb_done, 1)

        def project_act(act, l, ms):
            for m in ms:
                act.wait_ge(emb_done, 8 * l + m + 1)
                nc.scalar.activation(emb[:, m, :], PS[:, m % 4, :], ACT.Copy).then_inc(emb_copied, 1)

        def ple_pe(pe, l):
            ng = first[f"pgate{l}"]
            wait_aT(pe, 3 * l + 2)
            for x in range(4):
                landed(pe, ng + x)
            for m in range(2 * NT):
                t, n = m // 2, m % 2
                for c in range(KC):
                    last = pe.matmul(PS[:, m, :], aT[:, c, P * t:P * (t + 1)],
                                     slot(ng + 2 * n + c // 4, 4)[:, c % 4, :],
                                     start=(c == 0), stop=(c == KC - 1))
                last.then_inc(gate_done, 1)

        def ple_act(act, l):
            for m in range(2 * NT):
                act.wait_ge(gate_done, 8 * l + m + 1)
                if m >= 2:
                    act.wait_ge(*added(l, m - 2))
                nc.scalar.activation(sgp[:, m % 2, :], PS[:, m, :], ACT.Sigmoid).then_inc(sig_ready, 1)

        def ple_dve(dve, l, copy):
            if copy:
                dve.wait_ge(p_turned, l + 1)
                for k in range(2):
                    nc.vector.tensor_copy(pT[:, k, :], PS[:, 6 + k, :]).then_inc(p_copied, 1)
                return
            for m in range(2 * NT):
                t, n = m // 2, m % 2
                part = h[:, t, HALF * n:HALF * (n + 1)]
                dve.wait_ge(sig_ready, 8 * l + m + 1)
                dve.wait_ge(emb_copied, 8 * l + m + 1)
                nc.vector.tensor_tensor(sgp[:, m % 2, :], sgp[:, m % 2, :], emb[:, m, :],
                                        ALU.mult).then_inc(gated_mul, 1)
                dve.wait_ge(gated_mul, 8 * l + m + 1)
                nc.vector.tensor_tensor(part, part, sgp[:, m % 2, :], ALU.add).then_inc(added(l, m)[0], 1)

        gated_mul = sem("gated_mul")

        def released(n):
            for l in range(DEPTH):
                k = n - first[f"out{l}"]
                if 0 <= k < 4:
                    return proj_done, 8 * (l + 1)
                k = n - first[f"pproj{l}"]
                if 0 <= k < 5:
                    return (gate_done if k else emb_done), 8 * (l + 1)
                k = n - first[f"moe{l}"]
                if 0 <= k < 3 * EXPERTS:
                    return expert_released(l, 0, k)
            k = n - first["even_in"]
            if 0 <= k < 10:
                return z_done, NT * (k // 2 + 1)
            k = n - first["odd_conv"]
            return (c_done, 8) if k < 4 else (z1_done, NT) if k < 6 else (z1_done, 2 * NT)

        def expert_released(l, it, k):
            pair = PAIRS * l + 2 * it + k // 6
            return (down_hi if k % 3 == 2 else gateup), pair + 1

        def small_loads(eng):
            loads = [
                (tap_rows, a["conv_w"][0]),
                (bf8[:, :], a["fox_b_f"].rearrange("o h -> h o")),
                (wf[:, :, :], kblocks(even_w, 0, KC, 2560, 2568)),
                (lng[:, :], a["gmlp_ln_g"].to_broadcast([P, HALF])),
                (lnb[:, :], a["gmlp_ln_b"].to_broadcast([P, HALF])),
                (rope[:, :, :, :], a["rope"].rearrange("f (t q) d -> q f t d", q=P)),
                (gq1[:, 0, :], a["swa_q_norm"].to_broadcast([P, DH])),
                (gq1[:, 1, :], a["swa_k_norm"].to_broadcast([P, DH])),
                (sinks[:, :], a["swa_sinks"].to_broadcast([P, HEADS])),
            ]
            for l in range(DEPTH):
                loads += [(wr[:, l, :, 0:4], kblocks(a["moe_w_coarse"][l], 0, KC, 0, 4)),
                          (rbias[:, l, 0:4], a["moe_b_coarse"][l:l + 1].to_broadcast([P, 4])),
                          (rbias[:, l, 4:36], a["moe_b_fine"][l:l + 1].rearrange("l g e -> l (g e)").to_broadcast([P, 32]))]
                loads += [(wr[:, l, :, 4 + 8 * g:12 + 8 * g], kblocks(a["moe_w_fine"][l, g], 0, KC, 0, 8))
                          for g in range(GROUPS)]
            assert len(loads) == N_SMALL
            for dst, src in loads:
                eng.dma_start(dst, src).then_inc(small_loaded, 16)

        def row_loads(eng):
            loads = [
                (rows[MIX:MIX + 16, :], a["norm_mix"].rearrange("l (c p) -> (l c) p", p=P)),
                (rows[FFN:FFN + 16, :], a["norm_ffn"].rearrange("l (c p) -> (l c) p", p=P)),
                (rows[PNORM:PNORM + 16, :], a["ple_norm"].rearrange("l (c p) -> (l c) p", p=P)),
                (rows[BS:BS + 8, :], a["gmlp_b_s"][0]),
                (rows[CLG:CLG + 4, :], a["conv_ln_g"][0].rearrange("(c p) -> c p", p=P)),
                (rows[CLB:CLB + 4, :], a["conv_ln_b"][0].rearrange("(c p) -> c p", p=P)),
                (rows[FQ:FQ + 1, :].rearrange("o (f d) -> o f d", f=2), a["fox_q_norm"].unsqueeze(1).to_broadcast([1, 2, DH])),
                (rows[FK:FK + 1, :].rearrange("o (f d) -> o f d", f=2), a["fox_k_norm"].unsqueeze(1).to_broadcast([1, 2, DH])),
            ]
            assert len(loads) == N_ROWS
            for dst, src in loads:
                eng.dma_start(dst, src).then_inc(rows_loaded, 16)

        rows_loaded = sem("rows_loaded")
        N_ROWS, N_SMALL = 8, 9 + DEPTH * (3 + GROUPS)

        @block.sync
        def _(sp):
            for t in range(NT):
                sp.dma_start(h[:, t, :], a["x"][0, P * t:P * (t + 1), :]).then_inc(x_loaded[t], 16)
            row_loads(sp)

            def load(n):
                src, c = items[n]
                if n >= SLOTS:
                    sp.wait_ge(*released(n - SLOTS))
                sp.dma_start(slot(n, c), src).then_inc(slot_loaded[n % SLOTS], 16)

            n = 0
            for l in range(DEPTH):
                m0 = first[f"moe{l}"]
                while n < m0 + SLOTS:
                    load(n)
                    n += 1
                if 3 * l + 1 >= stages:
                    break
                with sp.Fori(1, STEPS) as it:
                    for x in range(4):
                        e = bass.ds(4 * it + x, 1)
                        for y, (w, c) in enumerate((("moe_w_gate", KC), ("moe_w_up", KC), ("moe_w_down", 2))):
                            k = 3 * x + y
                            s_, v_ = expert_released(l, it - 1, k)
                            sp.wait_ge(s_, v_)
                            sp.dma_start(slot(m0 + k, c), a[w][l, e].rearrange("e (c p) f -> p (e c) f", p=P)
                                         ).then_inc(slot_loaded[(m0 + k) % SLOTS], 16)
                n = m0 + 3 * EXPERTS
                over_sp(sp, l)
                if 3 * l + 2 >= stages:
                    break
                while n < first[f"pgate{l}"] + 4:
                    load(n)
                    n += 1
                if 3 * l + 3 >= stages:
                    break
                sp.wait_ge(row_loaded[NT - 1], 32 * (l + 1))
            for t in range(NT):
                sp.wait_ge(h_ready, NT * (stages - 1) + t + 1)
                sp.dma_start(out[0, P * t:P * (t + 1), :], h[:, t, :]).then_inc(out_stored, 16)
            sp.wait_ge(out_stored, 16 * NT)

        @block.scalar
        def _(act):
            chain = Chain(act, act_chain)
            act.wait_ge(const_ready, 1)
            for l in range(DEPTH):
                if stages > 3 * l:
                    norm_act(act, chain, 3 * l)
                    (even_act, odd_act)[l](act, chain)
                if stages > 3 * l + 1:
                    act.wait_ge(h_ready, 3 * NT * l + 1)
                    act.dma_start(psb[:, :, :], a["p"][l, 0].rearrange("(t q) d -> q t d", q=P)).then_inc(p_loaded, 16)
                    norm_act(act, chain, 3 * l + 1)
                    router_act(act, chain, l)
                    for q in range(2):
                        pair_act(act, l, 0, q)
                    with act.Fori(1, STEPS) as it:
                        for q in range(2):
                            pair_act(act, l, it, q)
                    act.wait_ge(most_ready, l + 1)
                    over_act(act, l)
                if stages > 3 * l + 2:
                    norm_act(act, chain, 3 * l + 2)
                    ple_act(act, l)

        @block.vector
        def _(dve):
            chain = Chain(dve, dve_chain)
            dve.wait_ge(const_ready, 1)
            for l in range(DEPTH):
                if stages > 3 * l:
                    norm_dve(dve, chain, 3 * l)
                    (even_dve, odd_dve)[l](dve, chain)
                if stages <= 3 * l + 1:
                    break
                norm_dve(dve, chain, 3 * l + 1)
                router_dve(dve, chain, l)
                sel_dve(l, 0, 0, dve)
                sel_dve(l, 0, 1, dve)
                copy_xT(l, 0, 0, 0, dve)
                copy_xT(l, 0, 0, 1, dve)
                router_tail_dve(dve, chain, l)
                for q in range(2):
                    pair_dve(dve, l, 0, q, True, True)
                with dve.Fori(1, STEPS - 1) as it:
                    for q in range(2):
                        pair_dve(dve, l, it, q, True, True)
                pair_dve(dve, l, STEPS - 1, 0, True, False)
                pair_dve(dve, l, STEPS - 1, 1, False, False)
                over_dve(dve, l, chain)
                combine_dve(dve, l)
                if stages <= 3 * l + 2:
                    break
                norm_dve(dve, chain, 3 * l + 2)
                ple_dve(dve, l, False)

        @block.tensor
        def _(pe):
            pe.wait_ge(const_ready, 1)
            for l in range(DEPTH):
                if stages > 3 * l:
                    norm_pe(pe, 3 * l)
                    (even_pe, odd_pe)[l](pe)
                if stages <= 3 * l + 1:
                    break
                norm_pe(pe, 3 * l + 1)
                router_pe(pe, l)
                gather_pe(pe, l, 0, 0)
                gather_half(pe, 0, 1)
                for q in range(2):
                    pair_pe(pe, l, 0, q, True)
                with pe.Fori(1, STEPS - 1) as it:
                    for q in range(2):
                        pair_pe(pe, l, it, q, True)
                pair_pe(pe, l, STEPS - 1, 0, True)
                pair_pe(pe, l, STEPS - 1, 1, False)
                pe.wait_ge(most_ready, l + 1)
                over_pe(pe, l)
                if stages <= 3 * l + 2:
                    break
                project_pe(pe, l)
                norm_pe(pe, 3 * l + 2)
                ple_pe(pe, l)

        @block.gpsimd
        def _(pool):
            g = nc.gpsimd
            chain = Chain(pool, pool_chain)
            chain.step(g.memset(eps[:, :], EPS))
            chain.link(g.memset(ident[:, :], 0.0))
            g.affine_select(out=ident[:, :], in_=ident[:, :], compare_op=ALU.not_equal, fill=1.0,
                            base=0, pattern=[[-1, P]], channel_multiplier=1).then_inc(const_ready, 1)
            chain.step(g.memset(ones[:, :], 1.0))
            chain.step(g.memset(mean_w[:, :], 1.0 / 512))
            chain.step(g.memset(mask[:, :], 0.0))
            chain.step(g.memset(pick[:, :, :], 0.0))
            chain.step(g.memset(decay[:, :], 0.0))
            chain.step(g.iota(iota[:, :], pattern=[[1, CAP]], base=0, channel_multiplier=0,
                              allow_small_or_imprecise_dtypes=True))
            chain.link(g.iota(steps64[:, :], pattern=[[CAP, ROUNDS - 1]], base=CAP, channel_multiplier=0,
                              allow_small_or_imprecise_dtypes=True))
            chain.step(g.affine_select(out=upper[:, :], in_=ones[:, :], compare_op=ALU.is_gt, fill=0.0,
                                       base=0, pattern=[[1, P]], channel_multiplier=-1))
            chain.step(g.affine_select(out=mask[:, 0:P], in_=mask[:, 0:P], compare_op=ALU.is_gt, fill=NEG,
                                       base=0, pattern=[[1, P]], channel_multiplier=-1))
            chain.step(g.affine_select(out=mask[:, P:2 * P], in_=mask[:, P:2 * P], compare_op=ALU.is_ge, fill=NEG,
                                       base=0, pattern=[[-1, P]], channel_multiplier=1))
            for part in range(3):
                v = pick[32 * part:32 * part + HEADS, :, :]
                chain.link(g.affine_select(out=v, in_=v, compare_op=ALU.not_equal, fill=1.0, base=0,
                                           pattern=[[-1, HEADS], [0, P]], channel_multiplier=1))
            pool.wait_ge(const_ready, 1)
            g.tensor_copy(ident_b[:, :], ident[:, :]).then_inc(const_ready, 1)
            small_loads(pool)
            for l in range(DEPTH):
                if stages > 3 * l:
                    (even_pool, odd_pool)[l](pool, chain)
                if stages > 3 * l + 1:
                    combine_pool(pool, l)



_INS = ['x', 'p', 'norm_mix', 'even_w_in', 'fox_b_f', 'gmlp_ln_g', 'gmlp_ln_b', 'gmlp_w_s', 'gmlp_b_s',
        'fox_q_norm', 'fox_k_norm', 'even_w_out', 'odd_w_in', 'swa_q_norm', 'swa_k_norm', 'swa_sinks',
        'conv_w', 'conv_ln_g', 'conv_ln_b', 'odd_w_out', 'norm_ffn', 'moe_w_coarse', 'moe_b_coarse',
        'moe_w_fine', 'moe_b_fine', 'moe_w_gate', 'moe_w_up', 'moe_w_down', 'ple_w_proj', 'ple_norm',
        'ple_w_gate']


def rope_table():
    inv = np.float32(500000.0) ** (-np.arange(ROT // 2, dtype=np.float32) * np.float32(2.0) / np.float32(ROT))
    ang = np.arange(SEQ, dtype=np.float32)[:, None] * inv[None, :].astype(np.float32)
    return np.stack([np.cos(ang), np.sin(ang)]).astype(np.float32)


def kernel(**inputs):
    import numpy as _np
    import concourse.bacc as _bacc
    from concourse import mybir as _mybir
    from concourse.bass_utils import run_bass_kernel_spmd as _run

    nc = _bacc.Bacc("TRN2", target_bir_lowering=False, num_devices=1)
    arrays, args = {}, {}
    for name in _INS:
        arrays[f"in_{name}_dram"] = _np.ascontiguousarray(inputs[name])
    arrays["in_rope_dram"] = rope_table()
    for name in _INS + ["rope"]:
        v = arrays[f"in_{name}_dram"]
        args[name] = nc.dram_tensor(f"in_{name}_dram", v.shape, _mybir.dt.from_np(v.dtype), kind="ExternalInput").ap()
    out = nc.dram_tensor("out_0_dram", (1, SEQ, D), F32, kind="ExternalOutput").ap()
    build(nc, args, out)
    r = _run(nc, [arrays], core_ids=[0])
    return r.results[0]["out_0_dram"]
```

```python
from contextlib import ExitStack

import numpy as np
import concourse.bass as bass
from concourse import mybir

F32 = mybir.dt.float32
BF16 = mybir.dt.bfloat16
I32 = mybir.dt.int32
U32 = mybir.dt.uint32
ALU = mybir.AluOpType
ACT = mybir.ActivationFunctionType
AX = mybir.AxisListType

P = 128
SEQ, D, DEPTH = 512, 1024, 2
NT, KC = SEQ // P, D // P
HALF = 512
HEADS, DH = 8, 64
GMLP = 8
GROUPS, PER_GROUP, EXPERTS, FE = 4, 8, 32, 256
CAP = 64
ROUNDS = SEQ // CAP
PAIRS = EXPERTS // 2
TAPS = 31
EPS = 1e-6
NEG = -1e30
SLOTS, SLOT = 12, 2048
ROT = 16
KB = 256


class Chain:

    def __init__(self, eng, sem):
        self.eng, self.sem, self.count = eng, sem, 0

    def step(self, ins):
        ins.then_inc(self.sem, 1)
        self.count += 1

    def link(self, ins):
        self.step(ins)
        self.wait()

    def wait(self, behind=0):
        if self.count > behind:
            self.eng.wait_ge(self.sem, self.count - behind)


def build(nc, a, out):
    with ExitStack() as ctx:
        def sb(name, shape, dt=F32):
            return ctx.enter_context(nc.sbuf_tensor(name, shape, dt))

        def sem(name):
            return ctx.enter_context(nc.semaphore(name))

        PS = ctx.enter_context(nc.psum_tensor("psum_banks", [P, 8, HALF], F32))
        ring = sb("ring", [P, SLOTS, SLOT])
        h = sb("h_res", [P, NT, D])
        aT = sb("aT", [P, KC, SEQ])
        work = sb("work", [P, 60 * KB])

        def area(kb0, kb1):
            return work[:, int(kb0 * KB):int(kb1 * KB)]

        xn = area(0, 16).rearrange("p (t d) -> p t d", t=NT)
        junk = area(16, 20)
        zq = area(0, 8).rearrange("p (t d) -> p t d", t=NT)
        zk = area(8, 16).rearrange("p (t d) -> p t d", t=NT)
        ws_raw = area(16, 20).rearrange("p (g s) -> p g s", g=HEADS)
        qT = [area(k, k + 8).rearrange("p (j s) -> p j s", j=4) for k in (20, 8)]
        kT = area(28, 36).rearrange("p (j s) -> p j s", j=4)
        zv = area(36, 44).rearrange("p (t d) -> p t d", t=NT)
        zu = area(44, 52).rearrange("p (t d) -> p t d", t=NT)
        zg = area(52, 60).rearrange("p (t d) -> p t d", t=NT)
        yb = zq
        yT = area(20, 36).rearrange("p (c s) -> p c s", c=KC)
        aflat = aT[:, :, :].rearrange("p c s -> p (c s)")
        wsT = aflat[:, 0:1024].rearrange("p (g s) -> p g s", g=HEADS)
        ebuf = aflat[:, 1024:2048].rearrange("p (b s) -> p b s", b=2)
        ptbuf = aflat[:, 2048:3072].rearrange("p (b s) -> p b s", b=2)
        cin = area(36, 45).rearrange("p (j s) -> p j s", j=4)
        cacc = area(45, 53).rearrange("p (j s) -> p j s", j=4)
        cacc2 = area(53, 55)
        sgc = area(55, 59).rearrange("p (b s) -> p b s", b=2)
        kv = area(8, 12).rearrange("p (t d) -> p t d", t=NT)
        qT1 = [area(k, k + 8).rearrange("p (j s) -> p j s", j=4) for k in (0, 28)]
        sq1 = area(12, 20)
        qp = area(12, 20).rearrange("p (t d) -> p t d", t=NT)
        y1 = qp
        kT1 = area(20, 22)
        junk_r = area(22, 23)
        sq_k = area(25, 27)
        cd = cin[:, :, 0:SEQ]
        xT = area(20, 28).rearrange("p (b c s) -> p b c s", b=2, c=KC)
        sel = area(28, 32).rearrange("p (b t s) -> p b t s", b=2, t=NT)
        sel_b = area(28, 30).bitcast(BF16).rearrange("p (b t s) -> p b t s", b=2, t=NT)
        split = [[area(*k).bitcast(BF16) for k in ((16, 18), (18, 20), (30, 32), (52, 54))],
                 [aflat[:, 512 * t:512 * (t + 1)].bitcast(BF16) for t in range(NT)],
                 [aflat[:, 2048 + 512 * t:2560 + 512 * t].bitcast(BF16) for t in range(NT)]]
        rest = [area(k, k + 4) for k in (20, 24, 38, 42)]
        sgate = area(32, 34).rearrange("p (b s) -> p b s", b=2)
        hid_area = area(34, 36)
        hid = area(34, 36).rearrange("p (b s) -> p b s", b=2)
        hidT = area(36, 38).rearrange("p (b f s) -> p b f s", b=2, f=2)
        ysb = area(38, 46).rearrange("p (b d) -> p b d", b=2)
        rtmp = area(46, 52)
        cold_down = (area(24, 28), area(42, 46))
        cold_up = aflat[:, 2048:4096]
        cold_gate = aflat[:, 0:2048]
        gath = [area(k, k + 4) for k in (38, 42, 46, 52)]
        psb = area(52, 56).rearrange("p (t d) -> p t d", t=NT)
        pT = area(56, 60).rearrange("p (k s) -> p k s", k=2)
        sgp = area(56, 60).rearrange("p (b s) -> p b s", b=2)
        emb = area(20, 36).rearrange("p (m s) -> p m s", m=2 * NT)

        ident = sb("ident", [P, P])
        ones = sb("ones", [P, P])
        mean_w = sb("mean_w", [P, P])
        upper = sb("upper", [P, P], BF16)
        ones_b = sb("ones_b", [P, P], BF16)
        ident_b = sb("ident_b", [P, P], BF16)
        mask = sb("mask", [P, 2 * P], BF16)
        pick = sb("pick", [96, HEADS, P], BF16)
        decay = sb("decay", [96, SEQ], BF16)
        iota = sb("iota", [P, CAP])
        steps64 = sb("steps64", [P, ROUNDS - 1])
        eps = sb("eps", [P, 1])
        rows = sb("rows", [P, P])
        cols = sb("cols", [P, P])
        lng = sb("lng", [P, HALF])
        lnb = sb("lnb", [P, HALF])
        wf = sb("wf", [P, KC, HEADS])
        wr = sb("wr", [P, DEPTH, KC, 36])
        rbias = sb("rbias", [P, DEPTH, 36])
        bf8 = sb("bf8", [HEADS, 1])
        rope = sb("rope_sb", [P, 2, NT, ROT // 2])
        gq1 = sb("gq1", [P, 2, DH])
        sinks = sb("sinks", [P, HEADS])
        tapw = sb("tapw", [P, NT, TAPS])
        tap_rows = work[0:TAPS, int(36 * KB):int(38 * KB)]
        tap_out = (lng, lnb)
        ss = sb("ss", [P, 6 * NT])
        root = sb("root", [P, 6 * NT])
        rstd = sb("rstd", [P, 6 * NT])
        qk_ss = sb("qk_ss", [P, 2, 32])
        stat6 = sb("stat6", [P, NT, 6])
        stat2 = sb("stat2", [P, NT, 2])
        lnr = sb("lnr", [P, NT])
        gq8 = sb("gq8", [P, 1])
        nmax = sb("nmax", [P, 32])
        rsum = sb("rsum", [P, 32])
        esink = sb("esink", [P, 32])
        rinv = sb("rinv", [P, 32])
        rsel = sb("rsel", [P, NT, EXPERTS])
        prob = sb("prob", [P, NT, 2])
        posn = sb("posn", [P, NT, 2], I32)
        most = sb("most", [P, 1], I32)
        table = nc.dram_tensor("expert_rows", [ROUNDS * EXPERTS * CAP, D], F32).ap()

        const_ready = sem("const_ready")
        small_loaded = sem("small_loaded")
        x_loaded = [sem(f"x_loaded{t}") for t in range(NT)]
        slot_loaded = [sem(f"slot_loaded{s}") for s in range(SLOTS)]
        cols_done = sem("cols_done")
        cols_ready = sem("cols_ready")
        h_ready = sem("h_ready")
        out_half = sem("out_half")
        act_chain, dve_chain, pool_chain = sem("act_chain"), sem("dve_chain"), sem("pool_chain")
        root_ready = sem("root_ready")
        xn_ready = sem("xn_ready")
        turned = sem("turned")
        aT_act, aT_dve = sem("aT_act"), sem("aT_dve")
        out_stored = sem("out_stored")
        proj_done = sem("proj_done")
        z_done, z_copied = sem("z_done"), sem("z_copied")

        def kblocks(w, c0, c1, n0, n1):
            return w.rearrange("(c p) n -> p c n", p=P)[:, c0:c1, n0:n1]

        def dense_blocks(w, col_list):
            for n0 in col_list:
                for k0 in (0, KC // 2):
                    yield kblocks(w, k0, k0 + KC // 2, n0, n0 + HALF), KC // 2

        even_w, odd_w = a["even_w_in"][0], a["odd_w_in"][0]
        EVEN_COLS = (1536, 1024, 2048, 512, 0)
        ODD_A, ODD_GATE, ODD_Q, ODD_KV = 768, 1280, 0, 512
        items, first = [], {}

        def add(name, its):
            first[name] = len(items)
            items.extend(its)

        def add_tail(l):
            first[f"moe{l}"] = len(items)
            for e in range(EXPERTS):
                items.extend([
                    (a["moe_w_gate"][l, e].rearrange("(c p) f -> p c f", p=P), KC),
                    (a["moe_w_up"][l, e].rearrange("(c p) f -> p c f", p=P), KC),
                    (a["moe_w_down"][l, e].rearrange("(c p) n -> p c n", p=P), 2)])
            add(f"pproj{l}", [(a["ple_w_proj"][l].rearrange("(c p) n -> p c n", p=P), 2)])
            add(f"pgate{l}", dense_blocks(a["ple_w_gate"][l], (0, HALF)))

        add("even_in", dense_blocks(even_w, EVEN_COLS))
        add("out0", dense_blocks(a["even_w_out"][0], (0, HALF)))
        add_tail(0)
        add("odd_q", dense_blocks(odd_w, (ODD_Q,)))
        add("odd_conv", dense_blocks(odd_w, (ODD_A, ODD_GATE)))
        add("odd_kv", [(kblocks(odd_w, 0, KC, ODD_KV, ODD_KV + 256), KC)])
        add("out1", dense_blocks(a["odd_w_out"][0], (0, HALF)))
        add_tail(1)

        def slot(n, c):
            return ring[:, n % SLOTS, :].rearrange("p (c n) -> p c n", c=c)

        def landed(pe, n):
            pe.wait_ge(slot_loaded[n % SLOTS], 16 * (n // SLOTS + 1))

        MIX, FFN, PNORM, BS, CLG, CLB, FQ, FK = 0, 16, 32, 48, 56, 60, 64, 65
        NROWS = 66

        def gain_col(u, c):
            l, kind = u // 3, u % 3
            return cols[:, (MIX, FFN, PNORM)[kind] + KC * l + c:][:, 0:1]

        block = ctx.enter_context(nc.Block())

        UNITS = [(hd, i) for hd in range(HEADS) for i in range(NT)]

        class Attention:

            def __init__(self, layer):
                n = f"att{layer}_"
                self.layer = layer
                self.scored = sem(n + "scored")
                self.maxed = sem(n + "maxed")
                self.exped = sem(n + "exped")
                self.turned = sem(n + "turned")
                self.copied = sem(n + "copied")
                self.summed = sem(n + "summed")
                self.written = sem(n + "written")

            def blocks(self, i):
                return range(i + 1) if self.layer == 0 else range(max(i - 1, 0), i + 1)

            def scores(self, pe, u):
                hd, i = UNITS[u]
                ks = self.blocks(i)
                n = P * len(ks)
                S = PS[:, u % 3, 0:n]
                if self.layer == 0:
                    j, q, k = hd // 2, qT[hd % 2], kT[:, hd // 2, :]
                else:
                    j, q, k = hd % 4, qT1[hd // 4], kT1
                if u >= 3:
                    pe.wait_ge(self.exped, u - 2)
                pe.matmul(S, q[:, j, P * i:P * (i + 1)], k[:, P * ks[0]:P * (i + 1)],
                          start=True, stop=False)
                if self.layer == 0:
                    pe.matmul(S, pick[:, hd, :], decay[:, 0:n], start=False, stop=False)
                    m = mask[:, P:2 * P]
                    S = PS[:, u % 3, n - P:n]
                else:
                    m = mask[:, 2 * P - n:2 * P]
                pe.matmul(S, ident_b[:, :], m, start=False, stop=True).then_inc(self.scored, 1)

            def turn(self, pe, u):
                hd, i = UNITS[u]
                pe.wait_ge(self.exped, u + 1)
                if u >= 2:
                    pe.wait_ge(self.copied, u - 1)
                for x in range(len(self.blocks(i))):
                    last = pe.transpose(PS[:, 3 + u % 2, P * x:P * (x + 1)],
                                        ebuf[:, u % 2, P * x:P * (x + 1)], ident[:, :])
                last.then_inc(self.turned, 1)

            def values(self, pe, u):
                hd, i = UNITS[u]
                ks = self.blocks(i)
                pe.wait_ge(self.copied, u + 1)
                if u >= 2:
                    pe.wait_ge(self.written, u - 1)
                for x, kb in enumerate(ks):
                    v = zv[:, kb, DH * hd:DH * (hd + 1)] if self.layer == 0 else \
                        kv[:, kb, P + DH * (hd // 4):P + DH * (hd // 4 + 1)]
                    last = pe.matmul(PS[:, 5 + u % 2, 0:DH], ptbuf[:, u % 2, P * x:P * (x + 1)], v,
                                     start=(x == 0), stop=(x == len(ks) - 1))
                last.then_inc(self.summed, 1)

            def pe(self, pe, between=None):
                n = len(UNITS)
                self.scores(pe, 0)
                self.scores(pe, 1)
                for u in range(n + 1):
                    if u + 2 < n:
                        self.scores(pe, u + 2)
                    if u < n:
                        self.turn(pe, u)
                    if u >= 1:
                        self.values(pe, u - 1)
                    if between:
                        between(u)

            def copy_turned(self, eng, u):
                w = P * len(self.blocks(UNITS[u][1]))
                eng.wait_ge(self.turned, u + 1)
                if u >= 2:
                    eng.wait_ge(self.summed, u - 1)
                dst, src = ptbuf[:, u % 2, 0:w], PS[:, 3 + u % 2, 0:w]
                if self.layer == 0:
                    nc.vector.tensor_copy(dst, src).then_inc(self.copied, 1)
                else:
                    nc.scalar.activation(dst, src, ACT.Copy).then_inc(self.copied, 1)

            def act(self, act, between=None):
                for u, (hd, i) in enumerate(UNITS):
                    n = P * len(self.blocks(i))
                    act.wait_ge(self.maxed, u + 1)
                    if u >= 2:
                        act.wait_ge(self.turned, u - 1)
                    if self.layer == 1:
                        nc.scalar.activation(esink[:, u:u + 1], sinks[:, hd:hd + 1], ACT.Exp,
                                             bias=nmax[:, u:u + 1])
                    nc.scalar.activation(ebuf[:, u % 2, 0:n], PS[:, u % 3, 0:n], ACT.Exp,
                                         bias=nmax[:, u:u + 1],
                                         accum_out=rsum[:, u:u + 1]).then_inc(self.exped, 1)
                    if self.layer == 1 and u >= 1:
                        self.copy_turned(act, u - 1)
                    if between:
                        between(u)
                if self.layer == 1:
                    self.copy_turned(act, len(UNITS) - 1)

            def dve(self, dve, chain, y, between=None):
                n = len(UNITS)

                def maxima(u):
                    hd, i = UNITS[u]
                    S = PS[:, u % 3, 0:P * len(self.blocks(i))]
                    dve.wait_ge(self.scored, u + 1)
                    if self.layer == 0:
                        nc.vector.tensor_reduce(nmax[:, u:u + 1], S, AX.X, ALU.max,
                                                negate=True).then_inc(self.maxed, 1)
                    else:
                        chain.link(nc.vector.tensor_reduce(rinv[:, u:u + 1], S, AX.X, ALU.max))
                        nc.vector.tensor_scalar(nmax[:, u:u + 1], rinv[:, u:u + 1],
                                                sinks[:, hd:hd + 1], -1.0, ALU.max,
                                                ALU.mult).then_inc(self.maxed, 1)

                maxima(0)
                for u in range(n + 1):
                    if u + 1 < n:
                        maxima(u + 1)
                    if u < n and self.layer == 0:
                        self.copy_turned(dve, u)
                    if u >= 1:
                        v = u - 1
                        hd, i = UNITS[v]
                        if self.layer == 1:
                            dve.wait_ge(self.exped, v + 1)
                            chain.link(nc.vector.tensor_tensor(rsum[:, v:v + 1], rsum[:, v:v + 1],
                                                               esink[:, v:v + 1], ALU.add))
                        chain.link(nc.vector.reciprocal(rinv[:, v:v + 1], rsum[:, v:v + 1]))
                        dve.wait_ge(self.summed, v + 1)
                        nc.vector.tensor_scalar(y[:, i, DH * hd:DH * (hd + 1)],
                                                PS[:, 5 + v % 2, 0:DH], rinv[:, v:v + 1], None,
                                                ALU.mult).then_inc(self.written, 1)
                    if between:
                        between(u)

        att = [Attention(0), Attention(1)]

        def wait_h(eng, u, t):
            if u == 0:
                eng.wait_ge(x_loaded[t], 16)
            else:
                eng.wait_ge(h_ready, NT * (u - 1) + t + 1)

        def square_act(act, chain, u, t):
            k = NT * u + t
            wait_h(act, u, t)
            chain.link(nc.scalar.activation(junk[:, 0:D], h[:, t, :], ACT.Square,
                                            accum_out=ss[:, k:k + 1]))
            nc.scalar.activation(root[:, k:k + 1], ss[:, k:k + 1], ACT.Sqrt, bias=eps[:, :],
                                 scale=1.0 / D).then_inc(root_ready, 1)

        def cols_act(act, chain):
            act.wait_ge(cols_done, 1)
            chain.link(nc.scalar.activation(cols[:, 0:NROWS], PS[:, 3, 0:NROWS], ACT.Copy))
            nc.scalar.activation(gq8[:, :], cols[:, FQ:FQ + 1], ACT.Copy, scale=DH ** -0.5).then_inc(cols_ready, 1)
            act.wait_ge(cols_ready, 1)

        def turn_bank(t, half):
            return 4 + 2 * (t % 2) + half

        def copy_aT_act(act, u, t):
            act.wait_ge(turned, NT * u + t + 1)
            for c in range(KC // 2):
                nc.scalar.activation(aT[:, c, P * t:P * (t + 1)], PS[:, turn_bank(t, 0), P * c:P * (c + 1)],
                                     ACT.Copy, scale=gain_col(u, c)).then_inc(aT_act, 1)

        def copy_aT_dve(dve, u, t):
            dve.wait_ge(turned, NT * u + t + 1)
            g0 = (MIX, FFN, PNORM)[u % 3] + KC * (u // 3) + KC // 2
            nc.vector.tensor_tensor(aT[:, KC // 2:KC, P * t:P * (t + 1)],
                                    PS[:, turn_bank(t, 1), :].rearrange("p (c s) -> p c s", c=KC // 2),
                                    cols[:, g0:g0 + KC // 2].unsqueeze(2).to_broadcast([P, KC // 2, P]),
                                    ALU.mult).then_inc(aT_dve, 1)

        def norm_act(act, chain, u):
            for t in range(NT):
                square_act(act, chain, u, t)
                if u == 0 and t >= 1:
                    if t == 1:
                        cols_act(act, chain)
                    copy_aT_act(act, u, t - 1)
            for t in range(NT - 1 if u == 0 else 0, NT):
                copy_aT_act(act, u, t)

        def xn_dve(dve, chain, u, t):
            k = NT * u + t
            dve.wait_ge(root_ready, k + 1)
            chain.link(nc.vector.reciprocal(rstd[:, k:k + 1], root[:, k:k + 1]))
            wait_h(dve, u, t)
            nc.vector.tensor_scalar(xn[:, t, :], h[:, t, :], rstd[:, k:k + 1], None,
                                    ALU.mult).then_inc(xn_ready, 1)

        def norm_dve(dve, chain, u, add):
            for t in range(NT):
                add(t)
                if u % 3 == 2:
                    xn_dve(dve, chain, u, t)
                    copy_aT_dve(dve, u, t)
                elif u == 0:
                    xn_dve(dve, chain, u, t)
                    if t == 1:
                        dve.wait_ge(cols_ready, 1)
                    if t >= 1:
                        copy_aT_dve(dve, u, t - 1)
                elif 1 <= t < NT - 1:
                    xn_dve(dve, chain, u, t - 1)
            if u == 0:
                copy_aT_dve(dve, u, NT - 1)
            elif u % 3 != 2:
                if u % 3 == 0:
                    copy_aT_dve(dve, u, 0)
                xn_dve(dve, chain, u, 2)
                if u % 3 == 1:
                    copy_aT_dve(dve, u, 0)
                copy_aT_dve(dve, u, 1)
                xn_dve(dve, chain, u, NT - 1)
                copy_aT_dve(dve, u, 2)
                copy_aT_dve(dve, u, 3)

        def turn_pe(pe, u, t):
            pe.wait_ge(xn_ready, NT * u + t + 1)
            if t >= 2:
                pe.wait_ge(aT_act, KC // 2 * (NT * u + t - 1))
                pe.wait_ge(aT_dve, NT * u + t - 1)
            for c in range(KC):
                last = pe.transpose(PS[:, turn_bank(t, c // 4), P * (c % 4):P * (c % 4 + 1)],
                                    xn[:, t, P * c:P * (c + 1)], ident[:, :])
            last.then_inc(turned, 1)

        def wait_aT(pe, u, t=NT - 1):
            pe.wait_ge(aT_act, KC // 2 * (NT * u + t + 1))
            pe.wait_ge(aT_dve, NT * u + t + 1)

        y_turned = sem("y_turned")
        yT_act, yT_dve = sem("yT_act"), sem("yT_dve")

        def out_pe(pe, l):
            n0 = first[f"out{l}"]
            pe.wait_ge(yT_act, Y_ACT[l])
            pe.wait_ge(yT_dve, Y_DVE[l])
            for x in range(4):
                landed(pe, n0 + x)
            for t in range(NT):
                if t >= 2:
                    pe.wait_ge(h_ready, 3 * NT * l + t - 1)
                for n in range(2):
                    for c in range(KC):
                        last = pe.matmul(PS[:, (2 * t + n) % 4, :], yT[:, c, P * t:P * (t + 1)],
                                         slot(n0 + 2 * n + c // 4, 4)[:, c % 4, :],
                                         start=(c == 0), stop=(c == KC - 1))
                    last.then_inc(proj_done, 1)

        def out_dve(dve, l, t):
            for n in range(2):
                dve.wait_ge(proj_done, 8 * l + 2 * t + n + 1)
                part = h[:, t, HALF * n:HALF * (n + 1)]
                nc.vector.tensor_tensor(part, part, PS[:, (2 * t + n) % 4, :],
                                        ALU.add).then_inc(h_ready if n else out_half, 1)

        Y_ACT, Y_DVE = (4, 4 + 6), (4, 4 + 2)

        f_done = sem("f_done")
        f_abs, f_log = sem("f_abs"), sem("f_log")
        taps_done, taps_copied = sem("taps_done"), sem("taps_copied")
        decay_ready = sem("decay_ready")
        qk_squared = sem("qk_squared")
        qk_summed = sem("qk_summed")
        qk_root = sem("qk_root")
        qk_normed = sem("qk_normed")
        qk_turned = sem("qk_turned")
        qk_copied = sem("qk_copied")
        ws_loaded = sem("ws_loaded")
        ws_turned, ws_copied, ws_masked = sem("ws_turned"), sem("ws_copied"), sem("ws_masked")
        g_stats, g_root, g_scaled, g_normed = sem("g_stats"), sem("g_root"), sem("g_scaled"), sem("g_normed")
        q_padded = sem("q_padded")
        g_mixed, ya_done = sem("g_mixed"), sem("ya_done")

        def forget_pe(pe):
            pe.wait_ge(small_loaded, 16 * N_SMALL)
            pe.wait_ge(const_ready, 2)
            for j in range(NT):
                last = pe.transpose(PS[:, 5, 32 * j:32 * j + TAPS], tap_rows[:, P * j:P * (j + 1)],
                                    ident[0:TAPS, 0:TAPS])
            last.then_inc(taps_done, 1)
            for c in range(KC):
                last = pe.matmul(PS[0:HEADS, 4, :], wf[:, c, :], aT[:, c, :], start=(c == 0),
                                 stop=(c == KC - 1))
            last.then_inc(f_done, 1)

        def even_pe(pe):
            turn_pe(pe, 0, 0)
            pe.wait_ge(rows_loaded, 16 * N_ROWS)
            pe.transpose(PS[:, 3, 0:NROWS], rows[0:NROWS, :], ident[0:NROWS, 0:NROWS]).then_inc(cols_done, 1)
            turn_pe(pe, 0, 1)
            n0 = first["even_in"]
            for b in range(5):
                if b == 2:
                    forget_pe(pe)
                for x in range(2):
                    landed(pe, n0 + 2 * b + x)
                for t in range(NT):
                    m = NT * b + t
                    if b == 0:
                        wait_aT(pe, 0, t)
                        if t == 3:
                            pe.wait_ge(cols_ready, 1)
                    if m >= 4:
                        pe.wait_ge(z_copied, m - 3)
                    for c in range(KC):
                        last = pe.matmul(PS[:, m % 4, :], aT[:, c, P * t:P * (t + 1)],
                                         slot(n0 + 2 * b + c // 4, 4)[:, c % 4, :],
                                         start=(c == 0), stop=(c == KC - 1))
                    last.then_inc(z_done, 1)
                    if b == 0 and t < 2:
                        turn_pe(pe, 0, t + 2)
                if b == 3:
                    for x, z in enumerate((zk, zq)):
                        pe.wait_ge(qk_normed, x + 1)
                        for j in range(4):
                            if x:
                                pe.wait_ge(qk_copied, j + 1)
                            else:
                                pe.wait_ge(f_abs, 1)
                                pe.wait_ge(taps_copied, 1)
                            for t in range(NT):
                                last = pe.transpose(PS[:, 4 + j, P * t:P * (t + 1)],
                                                    z[:, t, P * j:P * (j + 1)], ident[:, :])
                            last.then_inc(qk_turned, 1)
            pe.wait_ge(ws_loaded, 16)
            pe.wait_ge(qk_copied, 12)
            for g in range(HEADS):
                last = pe.transpose(PS[:, 6 + g // 4, P * (g % 4):P * (g % 4 + 1)], ws_raw[:, g, :],
                                    ident[:, :])
            last.then_inc(ws_turned, 1)
            pe.wait_ge(z_copied, 5 * NT)
            pe.wait_ge(decay_ready, 1)
            pe.wait_ge(q_padded, 2)
            pe.wait_ge(ws_copied, 1)
            att[0].pe(pe)
            pe.wait_ge(ws_masked, 1)
            pe.wait_ge(g_normed, 1)
            pe.wait_ge(att[0].written, len(UNITS))
            for g in range(GMLP):
                pe.matmul(PS[:, g // 2, 256 * (g % 2):256 * (g % 2 + 1)].rearrange(
                    "p (c d) -> p c d", c=NT), wsT[:, g, :],
                    zg[:, :, DH * g:DH * (g + 1)], start=True, stop=True).then_inc(g_mixed, 1)
            for n, c in enumerate((4, 5, 6, 7, 0, 1, 2, 3)):
                if c < 4:
                    pe.wait_ge(ya_done, GMLP)
                y = yb if c >= 4 else zu
                for t in range(NT):
                    last = pe.transpose(PS[:, c, P * t:P * (t + 1)],
                                        y[:, t, P * (c % 4):P * (c % 4 + 1)], ident[:, :])
                last.then_inc(y_turned, 1)
            out_pe(pe, 0)

        def even_act(act, chain):
            def copy(b, dst, func=ACT.Copy):
                for t in range(NT):
                    act.wait_ge(z_done, NT * b + t + 1)
                    nc.scalar.activation(dst[:, t, :], PS[:, (NT * b + t) % 4, :],
                                         func).then_inc(z_copied, 1)

            copy(0, zk)
            copy(1, zq)
            act.wait_ge(taps_done, 1)
            nc.scalar.activation(tapw[:, :, :], PS[:, 5, 0:NT * 32].rearrange("p (j k) -> p j k", j=NT)[:, :, 0:TAPS],
                                 ACT.Copy).then_inc(taps_copied, 1)
            act.dma_start(ws_raw[:, :, :], a["gmlp_w_s"][0].rearrange("g t s -> t g s")).then_inc(ws_loaded, 16)

            act.wait_ge(const_ready, 2)
            act.wait_ge(f_abs, 1)
            chain.link(nc.scalar.activation(junk8[:, 1, :], junk8[:, 1, :], ACT.Exp, scale=-1.0))
            nc.scalar.activation(junk8[:, 1, :], junk8[:, 1, :], ACT.Ln, bias=ones[0:HEADS, 0:1]).then_inc(f_log, 1)
            copy(2, zv)
            act.wait_ge(qk_summed, 2)
            nc.scalar.activation(qk_ss[:, :, :], qk_ss[:, :, :], ACT.Sqrt, bias=eps[:, :],
                                 scale=1.0 / DH).then_inc(qk_root, 1)
            copy(3, zg, ACT.Gelu_apprx_tanh)
            copy(4, zu, ACT.Gelu_apprx_tanh)
            act.wait_ge(g_stats, 1)
            nc.scalar.activation(lnr[:, :], stat2[:, :, 1], ACT.Sqrt, bias=eps[:, :]).then_inc(g_root, 1)
            act.wait_ge(ws_turned, 1)
            chain.step(nc.scalar.activation(wsT[:, 0:4, :], PS[:, 6, :].rearrange("p (g s) -> p g s", g=4), ACT.Copy))
            nc.scalar.activation(wsT[:, 4:8, :], PS[:, 7, :].rearrange("p (g s) -> p g s", g=4), ACT.Copy).then_inc(ws_copied, 1)
            att[0].act(act)
            y_act(act, 0, (5, 7, 1, 3))

        Y_ORDER = ((4, 5, 6, 7, 0, 1, 2, 3), (0, 1, 2, 3))

        def y_act(act, l, cs):
            for c in cs:
                act.wait_ge(y_turned, 8 * l + Y_ORDER[l].index(c) + 1)
                nc.scalar.activation(yT[:, c, :], PS[:, c, :], ACT.Copy).then_inc(yT_act, 1)

        def y_dve(dve, l, cs):
            for c in cs:
                dve.wait_ge(y_turned, 8 * l + Y_ORDER[l].index(c) + 1)
                nc.vector.tensor_copy(yT[:, c, :], PS[:, c, :]).then_inc(yT_dve, 1)

        junk8 = area(20, 26)[0:HEADS, :].rearrange("p (b s) -> p b s", b=3)
        k_sq, q_sq = area(52, 60), area(44, 52)

        def even_dve(dve, chain):
            dve.wait_ge(const_ready, 2)
            dve.wait_ge(f_done, 1)
            x, e, c_ = junk8[:, 0, :], junk8[:, 1, :], junk8[:, 2, :]
            chain.link(nc.vector.tensor_scalar(x, PS[0:HEADS, 4, :], bf8[:, :], None, ALU.add))
            chain.link(nc.vector.tensor_scalar(e, x, -1.0, None, ALU.mult))
            nc.vector.tensor_tensor(e, x, e, ALU.max).then_inc(f_abs, 1)
            chain.link(nc.vector.tensor_scalar(x, x, 0.0, None, ALU.min))
            dve.wait_ge(f_log, 1)
            chain.link(nc.vector.tensor_tensor(x, e, x, ALU.subtract))
            chain.link(nc.vector.memset(e, 1.0))
            chain.link(nc.vector.tensor_tensor_scan(c_, e, x, 0.0, ALU.mult, ALU.add))
            for part in range(3):
                r = decay[32 * part:32 * part + HEADS, :]
                if part < 2:
                    chain.link(nc.vector.tensor_copy(r, c_))
                    chain.link(nc.vector.tensor_copy(x, r))
                    chain.link(nc.vector.tensor_tensor(c_, c_, x, ALU.subtract))
                else:
                    nc.vector.tensor_copy(r, c_).then_inc(decay_ready, 1)
            for x_, s in enumerate((k_sq, q_sq)):
                dve.wait_ge(qk_squared, x_ + 1)
                nc.vector.tensor_reduce(qk_ss[:, x_, :], s.rearrange("p (g d) -> p g d", d=DH),
                                        AX.X, ALU.add).then_inc(qk_summed, 1)
            dve.wait_ge(qk_root, 1)
            chain.link(nc.vector.reciprocal(qk_ss[:, :, :], qk_ss[:, :, :]))
            for x_, z in enumerate((zk, zq)):
                v = z[:, :, :].rearrange("p t (g d) -> p (t g) d", d=DH)
                nc.vector.tensor_tensor(v, v, qk_ss[:, x_, :].unsqueeze(2).to_broadcast([P, 32, DH]),
                                        ALU.mult).then_inc(qk_normed, 1)
            for j in range(4):
                dve.wait_ge(qk_turned, j + 1)
                nc.vector.tensor_scalar(kT[:, j, :], PS[:, 4 + j, :], cols[:, FK:FK + 1], None,
                                        ALU.mult).then_inc(qk_copied, 1)
            for j in range(4):
                dve.wait_ge(qk_turned, 4 + j + 1)
                nc.vector.tensor_scalar(qT[0][0:DH, j, :], PS[0:DH, 4 + j, :], gq8[0:DH, :], None,
                                        ALU.mult).then_inc(qk_copied, 1)
                nc.vector.tensor_scalar(qT[1][DH:P, j, :], PS[DH:P, 4 + j, :], gq8[DH:P, :], None,
                                        ALU.mult).then_inc(qk_copied, 1)
            for t in range(NT):
                dve.wait_ge(z_copied, 3 * NT + t + 1)
                chain.link(nc.vector.bn_stats(stat6[:, t, :], zg[:, t, :]))
                ins = nc.vector.bn_aggr(stat2[:, t, :], stat6[:, t, :])
                if t == NT - 1:
                    ins.then_inc(g_stats, 1)
                else:
                    chain.link(ins)
            dve.wait_ge(g_root, 1)
            chain.link(nc.vector.reciprocal(lnr[:, :], lnr[:, :]))
            for t in range(NT):
                ins = nc.vector.tensor_scalar(zg[:, t, :], zg[:, t, :], stat2[:, t, 0:1],
                                              lnr[:, t:t + 1], ALU.subtract, ALU.mult)
                ins.then_inc(g_scaled, 1)
            att[0].dve(dve, chain, yb)
            for g in range(GMLP):
                dve.wait_ge(g_mixed, g + 2 - g % 2)
                u = zu[:, :, DH * g:DH * (g + 1)]
                nc.vector.scalar_tensor_tensor(
                    out=u, in0=PS[:, g // 2, 256 * (g % 2):256 * (g % 2 + 1)].rearrange(
                        "p (c d) -> p c d", c=NT),
                    scalar=cols[:, BS + g:BS + g + 1], in1=u, op0=ALU.add, op1=ALU.mult).then_inc(ya_done, 1)
            y_dve(dve, 0, (4, 6, 0, 2))

        def even_pool(pool, chain):
            for x_, (z, s) in enumerate(((zk, k_sq), (zq, q_sq))):
                pool.wait_ge(z_copied, NT * (x_ + 1))
                v = z[:, :, :].rearrange("p t d -> p (t d)")
                nc.gpsimd.tensor_tensor(s, v, v, ALU.mult).then_inc(qk_squared, 1)
            pool.wait_ge(qk_squared, 2)
            nc.gpsimd.memset(qT[0][DH:P, :, :], 0.0).then_inc(q_padded, 1)
            pool.wait_ge(q_padded, 1)
            pool.wait_ge(qk_turned, 4)
            nc.gpsimd.memset(qT[1][0:DH, :, :], 0.0).then_inc(q_padded, 1)
            pool.wait_ge(q_padded, 2)
            pool.wait_ge(g_scaled, NT)
            for t in range(NT):
                chain.link(nc.gpsimd.tensor_tensor(zg[:, t, :], zg[:, t, :], lng[:, :], ALU.mult))
                ins = nc.gpsimd.tensor_tensor(zg[:, t, :], zg[:, t, :], lnb[:, :], ALU.add)
                if t == NT - 1:
                    ins.then_inc(g_normed, 1)
                else:
                    chain.step(ins)
            pool.wait_ge(ws_copied, 1)
            nc.gpsimd.affine_select(out=wsT[:, :, :], in_=wsT[:, :, :], pattern=[[0, HEADS], [1, P]],
                                    compare_op=ALU.is_ge, fill=0.0, base=0,
                                    channel_multiplier=-1).then_inc(ws_masked, 1)

        c_done = sem("c_done")
        c_sig = sem("c_sig")
        c_glu = sem("c_glu")
        c_conv = sem("c_conv")
        z1_done, z1_copied = sem("z1_done"), sem("z1_copied")
        s1_squared, s1_summed, s1_root, s1_ready = sem("s1_squared"), sem("s1_summed"), sem("s1_root"), sem("s1_ready")
        t1_turned, t1_half, t1_copied = sem("t1_turned"), sem("t1_half"), sem("t1_copied")
        m_done, m_sub, m_sq, v_done, v_root, v_inverse, c_scaled = sem("m_done"), sem("m_sub"), sem("m_sq"), sem("v_done"), sem("v_root"), sem("v_inverse"), sem("c_scaled")
        c_conv_pool = sem("c_conv_pool")
        tap_scaled, tap_added = sem("tap_scaled"), sem("tap_added")
        tap_summed = sem("tap_summed")

        POOL_TAPS = range(1, TAPS, 2)
        DVE_TAPS = range(0, TAPS, 2)
        EARLY = 26
        AT_MEAN, AT_SUB, AT_SQUARE, AT_VAR, AT_ROOT, AT_SCALE = 21, 22, 23, 27, 28, 29

        def conv_bank(j, g):
            return 1 + (2 * j + g) % 6

        def conv_pe(pe, j, g):
            n0 = first["odd_conv"]
            for c in range(KC):
                last = pe.matmul(PS[:, conv_bank(j, g), :],
                                 slot(n0 + 2 * g + c // 4, 4)[:, c % 4, P * j:P * (j + 1)],
                                 aT[:, c, :], start=(c == 0), stop=(c == KC - 1))
            last.then_inc(c_done, 1)

        def turn_qk_pe(pe):
            pe.wait_ge(z1_copied, 2 * NT)
            pe.wait_ge(s1_ready, 1)
            for j in range(5):
                if j >= 2:
                    pe.wait_ge(t1_copied, j - 1)
                    pe.wait_ge(t1_half, j - 1)
                for t in range(NT):
                    src = qp[:, t, P * j:P * (j + 1)] if j < 4 else kv[:, t, 0:P]
                    last = pe.transpose(PS[:, turned_bank(j), P * t:P * (t + 1)], src, ident[:, :])
                last.then_inc(t1_turned, 1)

        def z1_bank(b, t):
            return ((0, 7, 1, 2), (3, 4, 5, 6))[b][t]

        def z1_pe(pe, b, t):
            n0, w = first[("odd_q", "odd_kv")[b]], (HALF, 256)[b]
            for c in range(KC):
                rhs = slot(n0, KC)[:, c, :] if b else slot(n0 + c // 4, 4)[:, c % 4, :]
                last = pe.matmul(PS[:, z1_bank(b, t), 0:w], aT[:, c, P * t:P * (t + 1)], rhs,
                                 start=(c == 0), stop=(c == KC - 1))
            last.then_inc(z1_done, 1)

        def turned_bank(j):
            return (7, 0)[j % 2]

        def odd_pe(pe):
            turn_pe(pe, 3, 0)
            turn_pe(pe, 3, 1)
            landed(pe, first["odd_q"])
            landed(pe, first["odd_q"] + 1)
            wait_aT(pe, 3, 0)
            pe.wait_ge(*added(0, 4))
            z1_pe(pe, 0, 0)
            turn_pe(pe, 3, 2)
            turn_pe(pe, 3, 3)
            wait_aT(pe, 3, 3)
            z1_pe(pe, 0, 1)
            pe.wait_ge(*added(0, 2 * NT - 1))
            for x in range(4):
                landed(pe, first["odd_conv"] + x)
            for j in range(3):
                for g in range(2):
                    conv_pe(pe, j, g)
            for t in range(2, NT):
                pe.wait_ge(c_glu, 1)
                z1_pe(pe, 0, t)
            landed(pe, first["odd_kv"])
            for t in range(NT):
                pe.wait_ge(c_glu, 3)
                z1_pe(pe, 1, t)
            pe.wait_ge(z1_copied, NT)
            conv_pe(pe, 3, 0)
            conv_pe(pe, 3, 1)
            turn_qk_pe(pe)
            pe.wait_ge(t1_copied, 5)
            pe.wait_ge(t1_half, 4)
            pe.wait_ge(q_padded, 4)
            pe.wait_ge(c_glu, 4)

            def between(u):
                if u == AT_MEAN:
                    pe.wait_ge(c_conv, 2)
                    pe.wait_ge(c_conv_pool, 1)
                    pe.wait_ge(tap_added, TAPS)
                    for j in range(4):
                        last = pe.matmul(PS[:, 7, :], mean_w[:, :], cacc[:, j, :], start=(j == 0), stop=(j == 3))
                    last.then_inc(m_done, 1)
                if u == AT_VAR:
                    for j in range(4):
                        pe.wait_ge(m_sq, j + 1)
                        last = pe.matmul(PS[:, 7, :], mean_w[:, :], cacc[:, j, :], start=(j == 0), stop=(j == 3))
                    last.then_inc(v_done, 1)
            att[1].pe(pe, between)
            pe.wait_ge(att[1].written, len(UNITS))
            for c in range(4):
                for t in range(NT):
                    last = pe.transpose(PS[:, c, P * t:P * (t + 1)], y1[:, t, P * c:P * (c + 1)], ident[:, :])
                last.then_inc(y_turned, 1)
            out_pe(pe, 1)

        def odd_act(act, chain):
            def sigmoid(j):
                act.wait_ge(c_done, 2 * j + 2)
                if j >= 2:
                    act.wait_ge(c_glu, j - 1)
                nc.scalar.activation(sgc[:, j % 2, :], PS[:, conv_bank(j, 1), :], ACT.Sigmoid).then_inc(c_sig, 1)

            def tap_out_act(n):
                j, k = (2, n) if n < TAPS else (3, POOL_TAPS[n - TAPS])
                if n >= 2:
                    act.wait_ge(tap_added, n - 1)
                nc.scalar.activation(tap_out[n % 2][:, :], cin[:, j, k:k + SEQ], ACT.Copy,
                                     scale=tapw[:, j, k:k + 1]).then_inc(tap_scaled, 1)

            def taps_out(n0, n1):
                for n in range(n0, n1):
                    tap_out_act(n)

            def copy_z1(b, t):
                dst, sq, n, w = ((zq, sq1, HALF, HALF), (kv, sq_k, P, 256))[b]
                act.wait_ge(z1_done, NT * b + t + 1)
                nc.scalar.activation(sq.rearrange("p (t d) -> p t d", t=NT)[:, t, :], PS[:, z1_bank(b, t), 0:n],
                                     ACT.Square).then_inc(s1_squared, 1)
                nc.scalar.activation(dst[:, t, :], PS[:, z1_bank(b, t), 0:w], ACT.Copy).then_inc(z1_copied, 1)

            def root_z1(b):
                act.wait_ge(s1_summed, b + 1)
                ssum = qk_ss[:, b, 0:(32, 8)[b]]
                nc.scalar.activation(ssum, ssum, ACT.Sqrt, bias=eps[:, :], scale=1.0 / DH).then_inc(s1_root, 1)

            copy_z1(0, 0)
            copy_z1(0, 1)
            sigmoid(0)
            sigmoid(1)
            sigmoid(2)
            act.wait_ge(c_glu, 3)
            taps_out(0, 8)
            copy_z1(0, 2)
            taps_out(8, 10)
            copy_z1(0, 3)
            root_z1(0)
            for t in range(NT):
                taps_out(10 + 3 * t, 13 + 3 * t)
                copy_z1(1, t)
            taps_out(22, EARLY)
            root_z1(1)
            sigmoid(3)
            for j in range(5):
                act.wait_ge(t1_turned, j + 1)
                if j < 4:
                    for b in range(2):
                        half = slice(DH * b, DH * (b + 1))
                        ins = nc.scalar.activation(qT1[b][half, j, :], PS[half, turned_bank(j), :], ACT.Copy,
                                                   scale=DH ** -0.5)
                        ins.then_inc((t1_half, t1_copied)[b], 1)
                else:
                    nc.scalar.activation(kT1, PS[:, turned_bank(j), :], ACT.Copy).then_inc(t1_copied, 1)

            def between(u):
                if EARLY + u < TAPS + len(POOL_TAPS):
                    if EARLY + u == TAPS:
                        act.wait_ge(c_glu, 4)
                    tap_out_act(EARLY + u)
                if 0 <= u - AT_SQUARE < 4:
                    j = u - AT_SQUARE
                    act.wait_ge(m_sub, j + 1)
                    nc.scalar.activation(cacc[:, j, :], cd[:, j, :], ACT.Square).then_inc(m_sq, 1)
                if u == AT_ROOT:
                    act.wait_ge(v_done, 1)
                    nc.scalar.activation(sgc[:, 0, :], PS[:, 7, :], ACT.Sqrt, bias=eps[:, :]).then_inc(v_root, 1)
            att[1].act(act, between)
            for j in range(4):
                act.wait_ge(c_scaled, j + 1)
                nc.scalar.activation(yT[:, 4 + j, :], cd[:, j, :], ACT.Silu, bias=cols[:, CLB + j:CLB + j + 1],
                                     scale=cols[:, CLG + j:CLG + j + 1]).then_inc(yT_act, 1)
            y_act(act, 1, (1, 3))

        def taps(chain, j, k0, k1):
            sums = cacc[:, j, :], cacc2
            for k in range(k0, k1):
                acc, src, w = sums[k % 2], cin[:, j, k:k + SEQ], tapw[:, j, k:k + 1]
                if k < 2:
                    chain.step(nc.vector.tensor_scalar(acc, src, w, None, ALU.mult))
                else:
                    chain.wait(behind=1)
                    chain.step(nc.vector.scalar_tensor_tensor(out=acc, in0=src, scalar=w, in1=acc,
                                                              op0=ALU.mult, op1=ALU.add))
            if k1 == TAPS:
                chain.wait()
                nc.vector.tensor_tensor(sums[0], sums[0], sums[1], ALU.add).then_inc(c_conv, 1)

        def odd_dve(dve, chain):
            chain.link(nc.vector.memset(cin[:, :, 0:TAPS - 1], 0.0))

            def qk_norm(x_, heads, z, sq):
                for t in range(NT):
                    dve.wait_ge(s1_squared, NT * x_ + t + 1)
                    ins = nc.vector.tensor_reduce(qk_ss[:, x_, heads * t:heads * (t + 1)],
                                                  sq.rearrange("p (t g d) -> p t g d", t=NT, d=DH)[:, t],
                                                  AX.X, ALU.add)
                    if t == NT - 1:
                        ins.then_inc(s1_summed, 1)
                    else:
                        chain.step(ins)
                dve.wait_ge(s1_root, x_ + 1)
                inv = qk_ss[:, x_, 0:heads * NT]
                chain.link(nc.vector.reciprocal(inv, inv))
                dve.wait_ge(z1_copied, NT * (x_ + 1))
                for t in range(NT):
                    v = z[:, t].rearrange("p (g d) -> p g d", d=DH)
                    r = qk_ss[:, x_, heads * t:heads * (t + 1)].unsqueeze(2).to_broadcast([P, heads, DH])
                    chain.link(nc.vector.tensor_tensor(v, v, r, ALU.mult))
                    g = gq1[:, x_, :].unsqueeze(1).to_broadcast([P, heads, DH])
                    if x_:
                        chain.link(nc.vector.tensor_tensor(v, v, g, ALU.mult))
                    else:
                        w = qp[:, t, :]
                        chain.link(nc.vector.tensor_tensor(
                            w.rearrange("p (j f d) -> p f j d", f=2, j=4), v.rearrange("p (f j) d -> p f j d", f=2),
                            gq1[:, 0, :].unsqueeze(1).unsqueeze(1).to_broadcast([P, 2, 4, DH]), ALU.mult))
                        v = w.rearrange("p (g d) -> p g d", d=DH)
                    x1, x2 = v[:, :, 0:8], v[:, :, 8:16]
                    cos = rope[:, 0, t, :].unsqueeze(1).to_broadcast([P, heads, 8])
                    sin = rope[:, 1, t, :].unsqueeze(1).to_broadcast([P, heads, 8])
                    tm = [junk_r[:, 64 * i_:64 * i_ + 8 * heads].rearrange("p (g d) -> p g d", d=8) for i_ in range(4)]
                    chain.step(nc.vector.tensor_tensor(tm[0], x1, cos, ALU.mult))
                    chain.step(nc.vector.tensor_tensor(tm[1], x2, sin, ALU.mult))
                    chain.step(nc.vector.tensor_tensor(tm[2], x2, cos, ALU.mult))
                    chain.link(nc.vector.tensor_tensor(tm[3], x1, sin, ALU.mult))
                    chain.step(nc.vector.tensor_tensor(x1, tm[0], tm[1], ALU.subtract))
                    ins = nc.vector.tensor_tensor(x2, tm[2], tm[3], ALU.add)
                    if x_ == 1 and t == NT - 1:
                        ins.then_inc(s1_ready, 1)
                    else:
                        chain.link(ins)

            def glu(j):
                dve.wait_ge(c_sig, j + 1)
                nc.vector.tensor_tensor(cin[:, j, TAPS - 1:TAPS - 1 + SEQ], PS[:, conv_bank(j, 0), :],
                                        sgc[:, j % 2, :], ALU.mult).then_inc(c_glu, 1)

            glu(0)
            dve.wait_ge(c_glu, 1)
            taps(chain, 0, 0, TAPS)
            glu(1)
            dve.wait_ge(c_glu, 2)
            dve.wait_ge(c_conv, 1)
            taps(chain, 1, 0, 10)
            glu(2)
            taps(chain, 1, 10, TAPS)
            qk_norm(0, 8, zq[:, :, :], sq1)
            qk_norm(1, 2, kv[:, :, 0:P], sq_k)
            glu(3)
            dve.wait_ge(c_glu, 4)

            def between(u):
                if u < len(DVE_TAPS):
                    k = DVE_TAPS[u]
                    acc, src, w = cacc[:, 3, :], cin[:, 3, k:k + SEQ], tapw[:, 3, k:k + 1]
                    if u == 0:
                        ins = nc.vector.tensor_scalar(acc, src, w, None, ALU.mult)
                    else:
                        dve.wait_ge(tap_summed, u)
                        ins = nc.vector.scalar_tensor_tensor(out=acc, in0=src, scalar=w, in1=acc,
                                                             op0=ALU.mult, op1=ALU.add)
                    ins.then_inc(tap_summed, 1)
                if 0 <= u - AT_SUB < 4:
                    j = u - AT_SUB
                    dve.wait_ge(m_done, 1)
                    nc.vector.tensor_tensor(cd[:, j, :], cacc[:, j, :], PS[:, 7, :], ALU.subtract).then_inc(m_sub, 1)
                if u == AT_SCALE:
                    dve.wait_ge(v_root, 1)
                    nc.vector.reciprocal(sgc[:, 1, :], sgc[:, 0, :]).then_inc(v_inverse, 1)
            att[1].dve(dve, chain, y1, between)
            y_dve(dve, 1, (0, 2))

        def odd_pool(pool, chain):
            def add_taps(acc, n0, n1, start):
                for n in range(n0, n1):
                    pool.wait_ge(tap_scaled, n + 1)
                    if n == n0 and start:
                        ins = nc.gpsimd.tensor_copy(acc, tap_out[n % 2][:, :])
                    else:
                        pool.wait_ge(tap_added, n)
                        ins = nc.gpsimd.tensor_tensor(acc, acc, tap_out[n % 2][:, :], ALU.add)
                    ins.then_inc(tap_added, 1)

            add_taps(cacc[:, 2, :], 0, EARLY, True)
            pool.wait_ge(tap_added, EARLY)
            pool.wait_ge(s1_ready, 1)
            nc.gpsimd.memset(qT1[0][DH:P, :, :], 0.0).then_inc(q_padded, 1)
            pool.wait_ge(q_padded, 3)
            nc.gpsimd.memset(qT1[1][0:DH, :, :], 0.0).then_inc(q_padded, 1)
            pool.wait_ge(q_padded, 4)
            add_taps(cacc[:, 2, :], EARLY, TAPS, False)
            pool.wait_ge(c_conv, 2)
            add_taps(cacc2, TAPS, TAPS + len(POOL_TAPS), True)
            pool.wait_ge(tap_added, TAPS + len(POOL_TAPS))
            pool.wait_ge(tap_summed, len(DVE_TAPS))
            block3 = cacc[:, 3, :]
            nc.gpsimd.tensor_tensor(block3, block3, cacc2, ALU.add).then_inc(c_conv_pool, 1)
            pool.wait_ge(m_sub, 4)
            pool.wait_ge(m_sq, 4)
            pool.wait_ge(v_inverse, 1)
            for j in range(4):
                nc.gpsimd.tensor_tensor(cd[:, j, :], cd[:, j, :], sgc[:, 1, :], ALU.mult).then_inc(c_scaled, 1)

        logits_done = sem("logits_done")
        r_exp, r_exped = sem("r_exp"), sem("r_exped")
        chosen, ranked = sem("chosen"), sem("ranked")
        most_ready = sem("most_ready")
        pos_ready = sem("pos_ready")
        sel_ready, gathered, xT_ready = sem("sel_ready"), sem("gathered"), sem("xT_ready")
        gateup, silu_ready, hid_ready = sem("gateup"), sem("silu_ready"), sem("hid_ready")
        hid_turned, hidT_ready = sem("hid_turned"), sem("hidT_ready")
        down_lo, down_hi, y_lo, y_hi = sem("down_lo"), sem("down_hi"), sem("y_lo"), sem("y_hi")
        y_stored = [sem("y_stored0"), sem("y_stored1")]
        row_loaded = [sem(f"row_loaded{b}") for b in range(NT)]
        row_used = sem("row_used")

        o = 0
        def rt(n):
            nonlocal o
            o += n
            return rtmp[:, o - n:o]
        logit = rt(NT * 36).rearrange("p (t e) -> p t e", t=NT)
        cpad = rt(NT * 8).rearrange("p (t e) -> p t e", t=NT)
        top_c = rt(NT * 8).rearrange("p (t e) -> p t e", t=NT)
        idx_c = rt(NT * 8).rearrange("p (t e) -> p t e", t=NT).bitcast(U32)
        gid = rt(NT)
        goh = rt(NT * GROUPS).rearrange("p (t g) -> p t g", t=NT)
        fprod = rt(NT * 32).rearrange("p (t g e) -> p t g e", t=NT, g=GROUPS)
        fsel = rt(NT * 8).rearrange("p (t e) -> p t e", t=NT)
        top_f = rt(NT * 8).rearrange("p (t e) -> p t e", t=NT)
        idx_f = rt(NT * 8).rearrange("p (t e) -> p t e", t=NT).bitcast(U32)
        eid = rt(NT * 2).rearrange("p (t k) -> p t k", t=NT)
        cexp = rt(NT * GROUPS).rearrange("p (t g) -> p t g", t=NT)
        psum_ = rt(NT)
        e2 = rt(NT)
        one1 = rt(NT * 32).rearrange("p (t e) -> p t e", t=NT)
        one2 = rt(NT * 32).rearrange("p (t e) -> p t e", t=NT)
        both = rt(NT * 32).rearrange("p (t e) -> p t e", t=NT)
        both_b = rt(NT * 16).bitcast(BF16).rearrange("p (t e) -> p t e", t=NT)
        rank = rt(NT * 32).rearrange("p (t e) -> p t e", t=NT)
        prod = rt(NT * 32).rearrange("p (t e) -> p t e", t=NT)
        rk = rt(NT * 2).rearrange("p (t k) -> p t k", t=NT)
        over = rt(NT * 2 * (ROUNDS - 1)).rearrange("p (t j) -> p t j", j=ROUNDS - 1)
        mostf = rt(1)

        lT = hid_area
        lT_ready, logits_turned = sem("lT_ready"), sem("logits_turned")

        def router_pe(pe, l):
            u = 3 * l + 1
            wait_aT(pe, u)
            for c in range(KC // 2):
                for b in range(2):
                    last = pe.matmul(PS[CAP * b:CAP * b + 36, 0, :], wr[:, l, 4 * b + c, :], aT[:, 4 * b + c, :],
                                     start=(c == 0), stop=(c == KC // 2 - 1))
            last.then_inc(logits_done, 1)
            embed_pe(pe, l)
            pe.wait_ge(lT_ready, 2 * (l + 1))
            for b in range(2):
                for t in range(NT):
                    last = pe.transpose(PS[:, 4 + b, 36 * t:36 * (t + 1)],
                                        lT[CAP * b:CAP * b + 36, P * t:P * (t + 1)],
                                        ident[CAP * b:CAP * b + 36, CAP * b:CAP * b + 36])
            last.then_inc(logits_turned, 1)
            pe.wait_ge(chosen, l + 1)
            for t in range(NT + 1):
                for s in range(min(t + 1, NT)):
                    last = pe.matmul(PS[:, 1, 32 * t:32 * (t + 1)], (upper if s == t else ones_b)[:, :],
                                     both_b[:, s, :], start=(s == 0), stop=(s == min(t, NT - 1)))
            last.then_inc(ranked, 1)

        def router_dve(dve, chain, l):
            v = nc.vector
            chain.link(v.memset(cpad[:, :, :], NEG * 1e8))
            dve.wait_ge(logits_done, l + 1)
            for b in range(2):
                v.tensor_copy(lT[CAP * b:CAP * b + 36, :], PS[CAP * b:CAP * b + 36, 0, :]).then_inc(lT_ready, 1)
            dve.wait_ge(logits_turned, l + 1)
            lg = [PS[:, 4 + b, 0:36 * NT].rearrange("p (t e) -> p t e", t=NT) for b in range(2)]
            chain.link(v.tensor_tensor(logit, lg[0], rbias[:, l, :].unsqueeze(1).to_broadcast([P, NT, 36]), ALU.add))
            chain.link(v.tensor_tensor(logit, logit, lg[1], ALU.add))
            chain.link(v.tensor_copy(cpad[:, :, 0:GROUPS], logit[:, :, 0:GROUPS]))
            for t in range(NT):
                chain.step(v.max(top_c[:, t, :], cpad[:, t, :]))
            chain.wait()
            for t in range(NT):
                chain.step(v.max_index(idx_c[:, t, :], top_c[:, t, :], cpad[:, t, :]))
            chain.wait()
            chain.link(v.tensor_copy(gid, idx_c[:, :, 0]))
            chain.link(v.tensor_tensor(goh, iota[:, 0:GROUPS].unsqueeze(1).to_broadcast([P, NT, GROUPS]),
                                       gid.unsqueeze(2).to_broadcast([P, NT, GROUPS]), ALU.is_equal))
            chain.link(v.tensor_tensor(fprod, logit[:, :, GROUPS:36].rearrange("p t (g e) -> p t g e", g=GROUPS),
                                       goh.unsqueeze(3).to_broadcast([P, NT, GROUPS, PER_GROUP]), ALU.mult))
            chain.link(v.tensor_reduce(fsel, fprod.rearrange("p t g e -> p t e g"), AX.X, ALU.add))
            for t in range(NT):
                chain.step(v.max(top_f[:, t, :], fsel[:, t, :]))
            chain.wait()
            for t in range(NT):
                chain.step(v.max_index(idx_f[:, t, :], top_f[:, t, :], fsel[:, t, :]))
            chain.wait()
            chain.link(v.tensor_copy(eid, idx_f[:, :, 0:2]))
            chain.link(v.scalar_tensor_tensor(out=eid, in0=gid.unsqueeze(2).to_broadcast([P, NT, 2]),
                                              scalar=float(PER_GROUP), in1=eid, op0=ALU.mult, op1=ALU.add))
            ids = iota[:, 0:32].unsqueeze(1).to_broadcast([P, NT, 32])
            for k, one in enumerate((one1, one2)):
                chain.step(v.tensor_tensor(one, ids, eid[:, :, k:k + 1].to_broadcast([P, NT, 32]), ALU.is_equal))
            chain.wait()
            v.tensor_tensor(both_b, one1, one2, ALU.add).then_inc(chosen, 1)
            chain.step(v.tensor_tensor(both, one1, one2, ALU.add))
            copy_pT(dve, l)
            chain.step(v.tensor_tensor(cexp, logit[:, :, 0:GROUPS], top_c[:, :, 0:1].to_broadcast([P, NT, GROUPS]),
                                       ALU.subtract))
            chain.link(v.tensor_tensor(e2, top_f[:, :, 1], top_f[:, :, 0], ALU.subtract))
            dve.sem_inc(r_exp, 1)
            dve.wait_ge(ranked, l + 1)
            chain.link(v.tensor_copy(rank, PS[:, 1, 0:NT * 32].rearrange("p (t e) -> p t e", t=NT)))
            chain.link(v.scalar_tensor_tensor(out=prod, in0=rank, scalar=1.0, in1=both, op0=ALU.add, op1=ALU.mult))
            chain.link(v.tensor_scalar(rsel[:, :, :], prod, -1.0, None, ALU.add))

        def router_tail_dve(dve, chain, l):
            v = nc.vector
            chain.link(v.tensor_reduce(mostf, PS[:, 1, NT * 32:NT * 32 + 32], AX.X, ALU.max))
            v.tensor_copy(most[:, :], mostf).then_inc(most_ready, 1)
            dve.wait_ge(r_exped, l + 1)
            chain.link(v.tensor_reduce(psum_, cexp, AX.X, ALU.add))
            chain.link(v.tensor_scalar(prob[:, :, 1], e2, 1.0, None, ALU.add))
            chain.link(v.tensor_tensor(psum_, psum_, prob[:, :, 1], ALU.mult))
            chain.link(v.reciprocal(prob[:, :, 0], psum_))
            chain.link(v.tensor_tensor(prob[:, :, 1], prob[:, :, 0], e2, ALU.mult))
            for k, one in enumerate((one1, one2)):
                chain.link(v.tensor_tensor(prod, one, rank, ALU.mult))
                chain.link(v.tensor_reduce(rk[:, :, k], prod, AX.X, ALU.add))
            flat = rk.rearrange("p t k -> p (t k)")
            chain.link(v.tensor_tensor(over, flat.unsqueeze(2).to_broadcast([P, 2 * NT, ROUNDS - 1]),
                                       steps64[:, :].unsqueeze(1).to_broadcast([P, 2 * NT, ROUNDS - 1]), ALU.is_ge))
            chain.link(v.scalar_tensor_tensor(out=rk, in0=eid, scalar=float(CAP), in1=rk, op0=ALU.mult, op1=ALU.add))
            rnd = prod[:, 0, 0:2 * NT]
            chain.link(v.tensor_reduce(rnd, over, AX.X, ALU.add))
            chain.link(v.scalar_tensor_tensor(out=flat, in0=rnd, scalar=float(EXPERTS * CAP - CAP), in1=flat,
                                              op0=ALU.mult, op1=ALU.add))
            v.tensor_copy(posn[:, :, :], rk).then_inc(pos_ready, 1)

        def router_act(act, chain, l):
            act.wait_ge(r_exp, l + 1)
            chain.link(nc.scalar.activation(cexp, cexp, ACT.Exp))
            nc.scalar.activation(e2, e2, ACT.Exp).then_inc(r_exped, 1)

        def pair_items(l, q):
            return [first[f"moe{l}"] + 6 * q + x for x in range(6)]

        split_act, split_pool, split_dve = sem("split_act"), sem("split_pool"), sem("split_dve")
        SPLITS = 2 * NT - 1

        def last_part(dve, l):
            dve.wait_ge(split_act, 8 * (l + 1))
            nc.vector.tensor_tensor(split[2][NT - 1], rest[NT - 1], split[1][NT - 1],
                                    ALU.subtract).then_inc(split_dve, 1)

        def first_parts(l):
            act = nc.scalar
            for t in range(NT):
                if t == 3:
                    act.wait_ge(p_turned, l + 1)
                act.activation(split[0][t], xn[:, t, :], ACT.Copy).then_inc(split_act, 1)

        def second_parts(l):
            act = nc.scalar
            act.wait_ge(logits_done, l + 1)
            for t in range(NT):
                act.wait_ge(split_pool, SPLITS * l + t + 1)
                act.activation(split[1][t], rest[t], ACT.Copy).then_inc(split_act, 1)

        def split_rest(pool, l):
            for part in range(2):
                for t in range(NT - part):
                    pool.wait_ge(split_act, 8 * l + NT * part + t + 1)
                    x = rest[t] if part else xn[:, t, :]
                    nc.gpsimd.tensor_tensor(split[2][t] if part else rest[t], x, split[part][t],
                                            ALU.subtract).then_inc(split_pool, 1)

        def gather_pe(pe, l, it, q):
            g = PAIRS * l + 2 * it + q
            pe.wait_ge(sel_ready, NT * (g + 1))
            if not isinstance(it, int) or g >= 1:
                pe.wait_ge(xT_ready, g)
            gather_half(pe, q, 0)

        def gather_half(pe, q, b):
            for c in range(4 * b, 4 * b + 4):
                for n in range(3 * NT):
                    t, part = n // 3, n % 3
                    last = pe.matmul(PS[:, 2 + b, P * (c % 4):P * (c % 4 + 1)],
                                     split[part][t][:, P * c:P * (c + 1)], sel_b[:, q, t, :],
                                     start=(n == 0), stop=(n == 3 * NT - 1))
            last.then_inc((gather_lo, gathered)[b], 1)

        def pair_pe(pe, l, it, q, more):
            g = PAIRS * l + 2 * it + q
            ns = pair_items(l, q)
            pe.wait_ge(xT_ready, g + 1)
            if isinstance(it, int) and 2 * it + q == 0:
                pe.wait_ge(p_copied, 2 * (l + 1))
            if not isinstance(it, int) or g >= 1:
                pe.wait_ge(hid_ready, g)
            for part in range(2):
                for e in range(2):
                    n = ns[3 * e + part]
                    pe.wait_ge(slot_loaded[n % SLOTS], 16 * (n // SLOTS + 1) + 16 * it)
                for c in range(KC):
                    for e in range(2):
                        last = pe.matmul(PS[CAP * e:CAP * (e + 1), 4, FE * part:FE * (part + 1)],
                                         xT[:, q, c, CAP * e:CAP * (e + 1)],
                                         slot(ns[3 * e + part], KC)[:, c, :],
                                         start=(c == 0), stop=(c == KC - 1))
            last.then_inc(gateup, 1)
            if more:
                gather_pe(pe, l, it + q, 1 - q)
            pe.wait_ge(hid_ready, g + 1)
            if not isinstance(it, int) or g >= 1:
                pe.wait_ge(hidT_ready, g)
            for f in range(2):
                last = pe.transpose(PS[:, 5, P * f:P * (f + 1)], hid[:, q, P * f:P * (f + 1)], ident[:, :])
            last.then_inc(hid_turned, 1)
            if more:
                gather_half(pe, 1 - q, 1)
            pe.wait_ge(hidT_ready, g + 1)
            for e in range(2):
                n = ns[3 * e + 2]
                pe.wait_ge(slot_loaded[n % SLOTS], 16 * (n // SLOTS + 1) + 16 * it)
            for n in range(2):
                if not isinstance(it, int) or g >= 1:
                    pe.wait_ge((y_lo, y_hi)[n], g)
                for f in range(2):
                    for e in range(2):
                        last = pe.matmul(PS[CAP * e:CAP * (e + 1), 6 + n, :],
                                         hidT[:, q, f, CAP * e:CAP * (e + 1)],
                                         slot(ns[3 * e + 2], 2)[:, f, HALF * n:HALF * (n + 1)],
                                         start=(f == 0), stop=(f == 1))
                last.then_inc((down_lo, down_hi)[n], 1)

        def sel_dve(l, it, q, dve):
            g = PAIRS * l + 2 * it + q
            if not isinstance(it, int) or g >= 2:
                dve.wait_ge(gathered, g - 1)
            for t in range(NT):
                r = rsel[:, t, bass.ds(4 * it + 2 * q, 2)]
                ins = nc.vector.tensor_tensor(sel_b[:, q, t, :].rearrange("p (e s) -> p e s", e=2),
                                              iota[:, :].unsqueeze(1).to_broadcast([P, 2, CAP]),
                                              r.unsqueeze(2).to_broadcast([P, 2, CAP]), ALU.is_equal)
                ins.then_inc(sel_ready, 1)

        xT_lo, gather_lo = sem("xT_lo"), sem("gather_lo")

        def copy_xT(l, it, q, b, dve):
            g = PAIRS * l + 2 * it + q
            dve.wait_ge((gather_lo, gathered)[b], g + 1)
            base = FFN + KC * l
            nc.vector.tensor_tensor(
                xT[:, q, 4 * b:4 * (b + 1), :], PS[:, 2 + b, :].rearrange("p (c s) -> p c s", c=4),
                cols[:, base + 4 * b:base + 4 * (b + 1)].unsqueeze(2).to_broadcast([P, 4, P]),
                ALU.mult).then_inc((xT_lo, xT_ready)[b], 1)

        def pair_dve(dve, l, it, q, more, more_sel):
            g = PAIRS * l + 2 * it + q
            dve.wait_ge(silu_ready, g + 1)
            nc.vector.tensor_tensor(hid[:, q, :], sgate[:, q, :], PS[:, 4, FE:2 * FE],
                                    ALU.mult).then_inc(hid_ready, 1)
            if more:
                copy_xT(l, it + q, 1 - q, 0, dve)
            dve.wait_ge(hid_turned, g + 1)
            nc.vector.tensor_copy(hidT[:, q, :, :], PS[:, 5, 0:2 * P].rearrange("p (f s) -> p f s", f=2)).then_inc(hidT_ready, 1)
            if more:
                copy_xT(l, it + q, 1 - q, 1, dve)
            if more_sel:
                sel_dve(l, it + 1, q, dve)
            dve.wait_ge(down_hi, g + 1)
            if not isinstance(it, int) or g >= 2:
                dve.wait_ge(y_stored[q], 16 * (PAIRS // 2 * l + it))
            nc.vector.tensor_copy(ysb[:, q, HALF:D], PS[:, 7, :]).then_inc(y_hi, 1)

        def pair_act(act, l, it, q):
            g = PAIRS * l + 2 * it + q
            act.wait_ge(gateup, g + 1)
            if not isinstance(it, int) or g >= 2:
                act.wait_ge(hid_ready, g - 1)
            nc.scalar.activation(sgate[:, q, :], PS[:, 4, 0:FE], ACT.Silu).then_inc(silu_ready, 1)
            act.wait_ge(down_lo, g + 1)
            if not isinstance(it, int) or g >= 2:
                act.wait_ge(y_stored[q], 16 * (PAIRS // 2 * l + it))
            nc.scalar.activation(ysb[:, q, 0:HALF], PS[:, 6, :], ACT.Copy).then_inc(y_lo, 1)
            act.wait_ge(y_lo, g + 1)
            act.wait_ge(y_hi, g + 1)
            act.dma_start(table.rearrange("(r s) d -> r s d", s=P)[bass.ds(2 * it + q, 1)].rearrange("r s d -> (r s) d"),
                          ysb[:, q, :]).then_inc(y_stored[q], 16)

        STEPS = PAIRS // 2
        cold = [{n: sem(f"over{l}_{n}") for n in ("loaded", "used", "shifted", "pe", "dve", "act", "stored")}
                for l in range(DEPTH)]
        OVER_PE = ("gathered", "gateup", "turned", "down")
        OVER_DVE = ("sel0", "sel1", "sel2", "sel3", "xT", "hid", "hidT", "y_hi")
        OVER_ACT = ("silu", "y_lo")

        def over_wait(eng, l, u, what):
            for name, steps in (("pe", OVER_PE), ("dve", OVER_DVE), ("act", OVER_ACT)):
                if what in steps:
                    eng.wait_ge(cold[l][name], u * len(steps) + (steps.index(what) + 1))

        def overflow(eng, l, body, before_round=None):
            n = eng.value_load(most[0:1, 0:1], min_val=0, max_val=SEQ)
            with eng.If(n > CAP):
                for q in range(2):
                    eng.wait_ge(y_stored[q], 16 * STEPS * (l + 1))
                with eng.Fori(0, ROUNDS - 1) as r:
                    if before_round:
                        before_round(r)
                    with eng.Fori(0, EXPERTS) as e:
                        body(r * EXPERTS + e, r, e)
                overflow_end(eng, l)
            eng.end_ifs()

        UNITS_OVER = (ROUNDS - 1) * EXPERTS

        def overflow_end(eng, l):
            eng.wait_ge(cold[l]["stored"], 16 * UNITS_OVER)

        def over_sp(sp, l):
            s = cold[l]
            sp.wait_ge(most_ready, l + 1)

            def body(u, r, e):
                sp.wait_ge(s["used"], u + 1)
                sp.dma_start(cold_gate.rearrange("p (c f) -> p c f", c=KC),
                             a["moe_w_gate"][l, bass.ds(e, 1)].rearrange("e (c p) f -> p (e c) f", p=P)).then_inc(s["loaded"], 16)
                sp.dma_start(cold_up.rearrange("p (c f) -> p c f", c=KC),
                             a["moe_w_up"][l, bass.ds(e, 1)].rearrange("e (c p) f -> p (e c) f", p=P)).then_inc(s["loaded"], 16)
                for f in range(2):
                    sp.dma_start(cold_down[f], a["moe_w_down"][l, bass.ds(e, 1), P * f:P * (f + 1), :].rearrange(
                        "e p f -> (e p) f")).then_inc(s["loaded"], 16)
            overflow(sp, l, body)

        def over_dve(dve, l, chain):
            s = cold[l]

            def shift(r):
                nc.vector.tensor_scalar(rsel[:, :, :], rsel[:, :, :], -float(CAP), None, ALU.add).then_inc(s["shifted"], 1)

            def body(u, r, e):
                dve.wait_ge(s["shifted"], r + 1)
                for t in range(NT):
                    nc.vector.tensor_tensor(sel[:, 0, t, 0:CAP], iota[:, :],
                                            rsel[:, t, bass.ds(e, 1)].to_broadcast([P, CAP]),
                                            ALU.is_equal).then_inc(s["dve"], 1)
                over_wait(dve, l, u, "gathered")
                nc.vector.tensor_tensor(
                    xT[:, 0, :, 0:CAP], PS[:, 2, :].rearrange("p (c s) -> p c s", c=KC),
                    cols[:, FFN + KC * l:FFN + KC * (l + 1)].unsqueeze(2).to_broadcast([P, KC, CAP]),
                    ALU.mult).then_inc(s["dve"], 1)
                over_wait(dve, l, u, "silu")
                nc.vector.tensor_tensor(hid[0:CAP, 0, :], sgate[0:CAP, 0, :], PS[0:CAP, 4, FE:2 * FE],
                                        ALU.mult).then_inc(s["dve"], 1)
                over_wait(dve, l, u, "turned")
                nc.vector.tensor_copy(hidT[:, 0, :, :], PS[:, 5, 0:2 * P].rearrange("p (f s) -> p f s", f=2)).then_inc(s["dve"], 1)
                over_wait(dve, l, u, "down")
                nc.vector.tensor_copy(ysb[0:CAP, 0, HALF:D], PS[0:CAP, 7, :]).then_inc(s["dve"], 1)
                dve.wait_ge(s["stored"], 16 * u + 16)
                dve.sem_inc(s["used"], 1)
            dve.wait_ge(sel_ready, NT * PAIRS * (l + 1))
            dve.wait_ge(y_hi, PAIRS * (l + 1))
            dve.sem_inc(s["used"], 1)
            overflow(dve, l, body, shift)

        def over_act(act, l):
            s = cold[l]

            def body(u, r, e):
                over_wait(act, l, u, "gateup")
                nc.scalar.activation(sgate[0:CAP, 0, :], PS[0:CAP, 4, 0:FE], ACT.Silu).then_inc(s["act"], 1)
                over_wait(act, l, u, "down")
                nc.scalar.activation(ysb[0:CAP, 0, 0:HALF], PS[0:CAP, 6, :], ACT.Copy).then_inc(s["act"], 1)
                over_wait(act, l, u, "y_lo")
                over_wait(act, l, u, "y_hi")
                act.dma_start(table.rearrange("(n s) d -> n s d", s=CAP)[bass.ds(u + EXPERTS, 1)].rearrange("n s d -> (n s) d"),
                              ysb[0:CAP, 0, :]).then_inc(s["stored"], 16)
                act.wait_ge(s["stored"], 16 * u + 16)
            overflow(act, l, body)

        def over_pe(pe, l):
            s = cold[l]

            def body(u, r, e):
                over_wait(pe, l, u, "sel3")
                for c in range(KC):
                    for t in range(NT):
                        last = pe.matmul(PS[:, 2, CAP * c:CAP * (c + 1)], xn[:, t, P * c:P * (c + 1)],
                                         sel[:, 0, t, 0:CAP], start=(t == 0), stop=(t == NT - 1))
                last.then_inc(s["pe"], 1)
                over_wait(pe, l, u, "xT")
                pe.wait_ge(s["loaded"], 64 * u + 64)
                for part, w in enumerate((cold_gate, cold_up)):
                    for c in range(KC):
                        last = pe.matmul(PS[0:CAP, 4, FE * part:FE * (part + 1)], xT[:, 0, c, 0:CAP],
                                         w.rearrange("p (c f) -> p c f", c=KC)[:, c, :],
                                         start=(c == 0), stop=(c == KC - 1))
                last.then_inc(s["pe"], 1)
                over_wait(pe, l, u, "hid")
                for f in range(2):
                    last = pe.transpose(PS[:, 5, P * f:P * (f + 1)], hid[:, 0, P * f:P * (f + 1)], ident[:, :])
                last.then_inc(s["pe"], 1)
                over_wait(pe, l, u, "hidT")
                for n in range(2):
                    for f in range(2):
                        last = pe.matmul(PS[0:CAP, 6 + n, :], hidT[:, 0, f, 0:CAP],
                                         cold_down[f][:, HALF * n:HALF * (n + 1)],
                                         start=(f == 0), stop=(f == 1))
                last.then_inc(s["pe"], 1)
            overflow(pe, l, body)

        def combine_pool(pool, l):
            pool.wait_ge(most_ready, l + 1)
            pool.wait_ge(pos_ready, l + 1)
            for q in range(2):
                pool.wait_ge(y_stored[q], 16 * STEPS * (l + 1))
            n = pool.value_load(most[0:1, 0:1], min_val=0, max_val=SEQ)

            def gathers(rows_of):
                for m in range(2 * NT):
                    t, k = m // 2, m % 2
                    if m >= NT:
                        pool.wait_ge(*row_added(l, m - NT))
                    nc.gpsimd.indirect_dma_start(
                        out=gath[m % NT], out_offset=None, in_=rows_of,
                        in_offset=bass.IndirectOffsetOnAxis(ap=posn[:, t, k:k + 1], axis=0)
                    ).then_inc(row_loaded[m % NT], 16)

            with pool.If(n > CAP):
                overflow_end(pool, l)
                gathers(table)
            with pool.Else():
                gathers(table[0:EXPERTS * CAP])
            pool.end_ifs()

        def row_added(l, m):
            t, k = m // 2, m % 2
            return (h_ready, NT * (3 * l + 1) + t + 1) if k else (row_used, NT * l + t + 1)

        def combine_dve(dve, l, t):
            for m in (2 * t, 2 * t + 1):
                k = m % 2
                dve.wait_ge(row_loaded[m % NT], 16 * (2 * l + m // NT + 1))
                if k:
                    dve.wait_ge(*row_added(l, m - 1))
                nc.vector.scalar_tensor_tensor(out=h[:, t, :], in0=gath[m % NT], scalar=prob[:, t, k:k + 1],
                                               in1=h[:, t, :], op0=ALU.mult, op1=ALU.add
                                               ).then_inc(row_added(l, m)[0], 1)

        p_loaded, p_turned, p_copied = sem("p_loaded"), sem("p_turned"), sem("p_copied")
        gate_done, emb_done, emb_copied = sem("gate_done"), sem("emb_done"), sem("emb_copied")
        sig_ready, gated = sem("sig_ready"), sem("gated")

        def embed_pe(pe, l):
            pe.wait_ge(p_loaded, 16 * (l + 1))
            for k in range(2):
                for t in range(NT):
                    last = pe.transpose(PS[:, 6 + k, P * t:P * (t + 1)], psb[:, t, P * k:P * (k + 1)], ident[:, :])
            last.then_inc(p_turned, 1)

        def added(l, m):
            t, n = m // 2, m % 2
            return (h_ready, NT * (3 * l + 2) + t + 1) if n else (gated, NT * l + t + 1)

        def project_pe(pe, l):
            np_ = first[f"pproj{l}"]
            landed(pe, np_)
            for m in range(2 * NT):
                t, n = m // 2, m % 2
                if m >= 4:
                    pe.wait_ge(emb_copied, 8 * l + m - 3)
                for k in range(2):
                    last = pe.matmul(PS[:, m % 4, :], pT[:, k, P * t:P * (t + 1)],
                                     slot(np_, 2)[:, k, HALF * n:HALF * (n + 1)],
                                     start=(k == 0), stop=(k == 1))
                last.then_inc(emb_done, 1)

        def project_act(act, l, ms):
            for m in ms:
                act.wait_ge(emb_done, 8 * l + m + 1)
                nc.scalar.activation(emb[:, m, :], PS[:, m % 4, :], ACT.Copy).then_inc(emb_copied, 1)

        def ple_pe(pe, l):
            ng = first[f"pgate{l}"]
            turn_pe(pe, 3 * l + 2, 0)
            pe.wait_ge(emb_copied, 8 * (l + 1))
            for x in range(4):
                landed(pe, ng + x)
            for m in range(2 * NT):
                t, n = m // 2, m % 2
                if m >= 4:
                    pe.wait_ge(*added(l, m - 4))
                wait_aT(pe, 3 * l + 2, t)
                for c in range(KC):
                    last = pe.matmul(PS[:, m % 4, :], aT[:, c, P * t:P * (t + 1)],
                                     slot(ng + 2 * n + c // 4, 4)[:, c % 4, :],
                                     start=(c == 0), stop=(c == KC - 1))
                last.then_inc(gate_done, 1)
                if m < NT - 1:
                    turn_pe(pe, 3 * l + 2, m + 1)

        def ple_act(act, chain, l):
            for m in range(2 * NT):
                act.wait_ge(gate_done, 8 * l + m + 1)
                if m >= 2:
                    act.wait_ge(*added(l, m - 2))
                nc.scalar.activation(sgp[:, m % 2, :], PS[:, m % 4, :], ACT.Sigmoid).then_inc(sig_ready, 1)
                if l + 1 < DEPTH and m % 2 and m >= 3:
                    square_act(act, chain, 3 * (l + 1), m // 2 - 1)

        def copy_pT(dve, l):
            dve.wait_ge(p_turned, l + 1)
            for k in range(2):
                nc.vector.tensor_copy(pT[:, k, :], PS[:, 6 + k, :]).then_inc(p_copied, 1)

        def ple_dve(dve, l, t):
            for n in range(2):
                m = 2 * t + n
                part = h[:, t, HALF * n:HALF * (n + 1)]
                dve.wait_ge(sig_ready, 8 * l + m + 1)
                dve.wait_ge(emb_copied, 8 * l + m + 1)
                nc.vector.tensor_tensor(sgp[:, m % 2, :], sgp[:, m % 2, :], emb[:, m, :],
                                        ALU.mult).then_inc(gated_mul, 1)
                dve.wait_ge(gated_mul, 8 * l + m + 1)
                nc.vector.tensor_tensor(part, part, sgp[:, m % 2, :], ALU.add).then_inc(added(l, m)[0], 1)

        gated_mul = sem("gated_mul")

        def released(n):
            for l in range(DEPTH):
                k = n - first[f"out{l}"]
                if 0 <= k < 4:
                    return proj_done, 8 * (l + 1)
                k = n - first[f"pproj{l}"]
                if 0 <= k < 5:
                    return (gate_done if k else emb_done), 8 * (l + 1)
                k = n - first[f"moe{l}"]
                if 0 <= k < 3 * EXPERTS:
                    return expert_released(l, 0, k)
            k = n - first["even_in"]
            if 0 <= k < 10:
                return z_done, NT * (k // 2 + 1)
            k = n - first["odd_q"]
            return (z1_done, NT) if k < 2 else (c_done, 8) if k < 6 else (z1_done, 2 * NT)

        def expert_released(l, it, k):
            pair = PAIRS * l + 2 * it + k // 6
            return (down_hi if k % 3 == 2 else gateup), pair + 1

        def small_loads(eng):
            loads = [
                (tap_rows, a["conv_w"][0]),
                (bf8[:, :], a["fox_b_f"].rearrange("o h -> h o")),
                (wf[:, :, :], kblocks(even_w, 0, KC, 2560, 2568)),
                (lng[:, :], a["gmlp_ln_g"].to_broadcast([P, HALF])),
                (lnb[:, :], a["gmlp_ln_b"].to_broadcast([P, HALF])),
                (rope[:, :, :, :], a["rope"].rearrange("f (t q) d -> q f t d", q=P)),
                (gq1[:, 0, :], a["swa_q_norm"].to_broadcast([P, DH])),
                (gq1[:, 1, :], a["swa_k_norm"].to_broadcast([P, DH])),
                (sinks[:, :], a["swa_sinks"].to_broadcast([P, HEADS])),
            ]
            for l in range(DEPTH):
                loads += [(wr[:, l, :, 0:4], kblocks(a["moe_w_coarse"][l], 0, KC, 0, 4)),
                          (rbias[:, l, 0:4], a["moe_b_coarse"][l:l + 1].to_broadcast([P, 4])),
                          (rbias[:, l, 4:36], a["moe_b_fine"][l:l + 1].rearrange("l g e -> l (g e)").to_broadcast([P, 32]))]
                loads += [(wr[:, l, :, 4 + 8 * g:12 + 8 * g], kblocks(a["moe_w_fine"][l, g], 0, KC, 0, 8))
                          for g in range(GROUPS)]
            assert len(loads) == N_SMALL
            for dst, src in loads:
                eng.dma_start(dst, src).then_inc(small_loaded, 16)

        def row_loads(eng):
            loads = [
                (rows[MIX:MIX + 16, :], a["norm_mix"].rearrange("l (c p) -> (l c) p", p=P)),
                (rows[FFN:FFN + 16, :], a["norm_ffn"].rearrange("l (c p) -> (l c) p", p=P)),
                (rows[PNORM:PNORM + 16, :], a["ple_norm"].rearrange("l (c p) -> (l c) p", p=P)),
                (rows[BS:BS + 8, :], a["gmlp_b_s"][0]),
                (rows[CLG:CLG + 4, :], a["conv_ln_g"][0].rearrange("(c p) -> c p", p=P)),
                (rows[CLB:CLB + 4, :], a["conv_ln_b"][0].rearrange("(c p) -> c p", p=P)),
                (rows[FQ:FQ + 1, :].rearrange("o (f d) -> o f d", f=2), a["fox_q_norm"].unsqueeze(1).to_broadcast([1, 2, DH])),
                (rows[FK:FK + 1, :].rearrange("o (f d) -> o f d", f=2), a["fox_k_norm"].unsqueeze(1).to_broadcast([1, 2, DH])),
            ]
            assert len(loads) == N_ROWS
            for dst, src in loads:
                eng.dma_start(dst, src).then_inc(rows_loaded, 16)

        rows_loaded = sem("rows_loaded")
        N_ROWS, N_SMALL = 8, 9 + DEPTH * (3 + GROUPS)

        @block.sync
        def _(sp):
            for t in range(NT):
                sp.dma_start(h[:, t, :], a["x"][0, P * t:P * (t + 1), :]).then_inc(x_loaded[t], 16)
            row_loads(sp)

            def load(n):
                src, c = items[n]
                if n >= SLOTS:
                    sp.wait_ge(*released(n - SLOTS))
                sp.dma_start(slot(n, c), src).then_inc(slot_loaded[n % SLOTS], 16)

            n = 0
            for l in range(DEPTH):
                m0 = first[f"moe{l}"]
                while n < m0 + SLOTS:
                    load(n)
                    n += 1
                with sp.Fori(1, STEPS) as it:
                    for x in range(4):
                        e = bass.ds(4 * it + x, 1)
                        for y, (w, c) in enumerate((("moe_w_gate", KC), ("moe_w_up", KC), ("moe_w_down", 2))):
                            k = 3 * x + y
                            s_, v_ = expert_released(l, it - 1, k)
                            sp.wait_ge(s_, v_)
                            sp.dma_start(slot(m0 + k, c), a[w][l, e].rearrange("e (c p) f -> p (e c) f", p=P)
                                         ).then_inc(slot_loaded[(m0 + k) % SLOTS], 16)
                n = m0 + 3 * EXPERTS
                over_sp(sp, l)
                while n < first[f"pgate{l}"] + 4:
                    if n == first[f"pgate{l}"] + 2:
                        sp.wait_ge(row_loaded[NT - 1], 16 * (2 * l + 1))
                    load(n)
                    n += 1
                sp.wait_ge(row_loaded[NT - 1], 32 * (l + 1))
            for t in range(NT):
                sp.wait_ge(h_ready, NT * (3 * DEPTH - 1) + t + 1)
                sp.dma_start(out[0, P * t:P * (t + 1), :], h[:, t, :]).then_inc(out_stored, 16)
            sp.wait_ge(out_stored, 16 * NT)

        @block.scalar
        def _(act):
            chain = Chain(act, act_chain)
            act.wait_ge(const_ready, 1)
            norm_act(act, chain, 0)
            for l in range(DEPTH):
                (even_act, odd_act)[l](act, chain)
                act.wait_ge(h_ready, 3 * NT * l + 1)
                act.dma_start(psb[:, :, :], a["p"][l, 0].rearrange("(t q) d -> q t d", q=P)).then_inc(p_loaded, 16)
                norm_act(act, chain, 3 * l + 1)
                first_parts(l)
                second_parts(l)
                router_act(act, chain, l)
                for q in range(2):
                    pair_act(act, l, 0, q)
                with act.Fori(1, STEPS) as it:
                    for q in range(2):
                        pair_act(act, l, it, q)
                act.wait_ge(most_ready, l + 1)
                over_act(act, l)
                u = 3 * l + 2
                project_act(act, l, range(0, 4))
                square_act(act, chain, u, 0)
                project_act(act, l, range(4, 8))
                copy_aT_act(act, u, 0)
                for t in range(1, NT):
                    square_act(act, chain, u, t)
                    copy_aT_act(act, u, t)
                ple_act(act, chain, l)
                if l + 1 < DEPTH:
                    copy_aT_act(act, 3 * l + 3, 0)
                    square_act(act, chain, 3 * l + 3, NT - 1)
                    for t in range(1, NT):
                        copy_aT_act(act, 3 * l + 3, t)

        @block.vector
        def _(dve):
            chain = Chain(dve, dve_chain)
            dve.wait_ge(const_ready, 1)
            norm_dve(dve, chain, 0, lambda t: None)
            for l in range(DEPTH):
                (even_dve, odd_dve)[l](dve, chain)
                norm_dve(dve, chain, 3 * l + 1, lambda t: out_dve(dve, l, t))
                router_dve(dve, chain, l)
                sel_dve(l, 0, 0, dve)
                last_part(dve, l)
                sel_dve(l, 0, 1, dve)
                copy_xT(l, 0, 0, 0, dve)
                copy_xT(l, 0, 0, 1, dve)
                router_tail_dve(dve, chain, l)
                for q in range(2):
                    pair_dve(dve, l, 0, q, True, True)
                with dve.Fori(1, STEPS - 1) as it:
                    for q in range(2):
                        pair_dve(dve, l, it, q, True, True)
                pair_dve(dve, l, STEPS - 1, 0, True, False)
                pair_dve(dve, l, STEPS - 1, 1, False, False)
                over_dve(dve, l, chain)
                norm_dve(dve, chain, 3 * l + 2, lambda t: combine_dve(dve, l, t))
                if l + 1 < DEPTH:
                    norm_dve(dve, chain, 3 * l + 3, lambda t: ple_dve(dve, l, t))
                else:
                    for t in range(NT):
                        ple_dve(dve, l, t)

        @block.tensor
        def _(pe):
            pe.wait_ge(const_ready, 1)
            for l in range(DEPTH):
                (even_pe, odd_pe)[l](pe)
                for t in range(NT):
                    turn_pe(pe, 3 * l + 1, t)
                router_pe(pe, l)
                pe.wait_ge(split_pool, SPLITS * (l + 1))
                pe.wait_ge(split_dve, l + 1)
                gather_pe(pe, l, 0, 0)
                gather_half(pe, 0, 1)
                for q in range(2):
                    pair_pe(pe, l, 0, q, True)
                with pe.Fori(1, STEPS - 1) as it:
                    for q in range(2):
                        pair_pe(pe, l, it, q, True)
                pair_pe(pe, l, STEPS - 1, 0, True)
                pair_pe(pe, l, STEPS - 1, 1, False)
                pe.wait_ge(most_ready, l + 1)
                over_pe(pe, l)
                project_pe(pe, l)
                ple_pe(pe, l)

        @block.gpsimd
        def _(pool):
            g = nc.gpsimd
            chain = Chain(pool, pool_chain)
            chain.step(g.memset(eps[:, :], EPS))
            chain.link(g.memset(ident[:, :], 0.0))
            g.affine_select(out=ident[:, :], in_=ident[:, :], compare_op=ALU.not_equal, fill=1.0,
                            base=0, pattern=[[-1, P]], channel_multiplier=1).then_inc(const_ready, 1)
            chain.step(g.memset(ones[:, :], 1.0))
            chain.step(g.memset(ones_b[:, :], 1.0))
            chain.step(g.memset(mean_w[:, :], 1.0 / 512))
            chain.step(g.memset(mask[:, :], 0.0))
            chain.step(g.memset(pick[:, :, :], 0.0))
            chain.step(g.memset(decay[:, :], 0.0))
            chain.step(g.iota(iota[:, :], pattern=[[1, CAP]], base=0, channel_multiplier=0,
                              allow_small_or_imprecise_dtypes=True))
            chain.link(g.iota(steps64[:, :], pattern=[[CAP, ROUNDS - 1]], base=CAP, channel_multiplier=0,
                              allow_small_or_imprecise_dtypes=True))
            chain.step(g.affine_select(out=upper[:, :], in_=ones_b[:, :], compare_op=ALU.is_gt, fill=0.0,
                                       base=0, pattern=[[1, P]], channel_multiplier=-1))
            chain.step(g.affine_select(out=mask[:, 0:P], in_=mask[:, 0:P], compare_op=ALU.is_gt, fill=NEG,
                                       base=0, pattern=[[1, P]], channel_multiplier=-1))
            chain.step(g.affine_select(out=mask[:, P:2 * P], in_=mask[:, P:2 * P], compare_op=ALU.is_ge, fill=NEG,
                                       base=0, pattern=[[-1, P]], channel_multiplier=1))
            for part in range(3):
                v = pick[32 * part:32 * part + HEADS, :, :]
                chain.link(g.affine_select(out=v, in_=v, compare_op=ALU.not_equal, fill=1.0, base=0,
                                           pattern=[[-1, HEADS], [0, P]], channel_multiplier=1))
            pool.wait_ge(const_ready, 1)
            g.tensor_copy(ident_b[:, :], ident[:, :]).then_inc(const_ready, 1)
            small_loads(pool)
            for l in range(DEPTH):
                (even_pool, odd_pool)[l](pool, chain)
                split_rest(pool, l)
                combine_pool(pool, l)



_INS = ['x', 'p', 'norm_mix', 'even_w_in', 'fox_b_f', 'gmlp_ln_g', 'gmlp_ln_b', 'gmlp_w_s', 'gmlp_b_s',
        'fox_q_norm', 'fox_k_norm', 'even_w_out', 'odd_w_in', 'swa_q_norm', 'swa_k_norm', 'swa_sinks',
        'conv_w', 'conv_ln_g', 'conv_ln_b', 'odd_w_out', 'norm_ffn', 'moe_w_coarse', 'moe_b_coarse',
        'moe_w_fine', 'moe_b_fine', 'moe_w_gate', 'moe_w_up', 'moe_w_down', 'ple_w_proj', 'ple_norm',
        'ple_w_gate']


def rope_table():
    inv = np.float32(500000.0) ** (-np.arange(ROT // 2, dtype=np.float32) * np.float32(2.0) / np.float32(ROT))
    ang = np.arange(SEQ, dtype=np.float32)[:, None] * inv[None, :].astype(np.float32)
    return np.stack([np.cos(ang), np.sin(ang)]).astype(np.float32)


def kernel(**inputs):
    import numpy as _np
    import concourse.bacc as _bacc
    from concourse import mybir as _mybir
    from concourse.bass_utils import run_bass_kernel_spmd as _run

    nc = _bacc.Bacc("TRN2", target_bir_lowering=False, num_devices=1)
    arrays, args = {}, {}
    for name in _INS:
        arrays[f"in_{name}_dram"] = _np.ascontiguousarray(inputs[name])
    arrays["in_rope_dram"] = rope_table()
    for name in _INS + ["rope"]:
        v = arrays[f"in_{name}_dram"]
        args[name] = nc.dram_tensor(f"in_{name}_dram", v.shape, _mybir.dt.from_np(v.dtype), kind="ExternalInput").ap()
    out = nc.dram_tensor("out_0_dram", (1, SEQ, D), F32, kind="ExternalOutput").ap()
    build(nc, args, out)
    r = _run(nc, [arrays], core_ids=[0])
    return r.results[0]["out_0_dram"]
```
